# Optimizing a Trainium2 kernel written in Bass

```python
import math
import jax, jax.numpy as jnp
from jax import lax
import numpy as np

D_MODEL = 2048
BATCH = 1
SEQ = 256
DEPTH = 2

N_A_LAYERS = DEPTH // 2
N_B_LAYERS = DEPTH - N_A_LAYERS
CONV_WIDTH = 3
D_FF = ((8 * D_MODEL // 3 + 255) // 256) * 256
DIFF_HEADS = D_MODEL // 256
DIFF_HEAD_DIM = D_MODEL // DIFF_HEADS // 2
V_HEAD_DIM = 2 * DIFF_HEAD_DIM
QK_WIDTH = DIFF_HEADS * 2 * DIFF_HEAD_DIM
V_WIDTH = DIFF_HEADS * V_HEAD_DIM
ROT_DIM = DIFF_HEAD_DIM // 4
ROPE_THETA = 500000.0
Q_BLOCK = 128
DEEPNORM_ALPHA = (2.0 * DEPTH) ** 0.25
DEEPNORM_BETA = (8.0 * DEPTH) ** -0.25
LN_EPS = 1e-5
SUBLN_EPS = 1e-5


def causal_dwconv(x, w):
    s = x.shape[1]
    xp = jnp.pad(x, ((0, 0), (CONV_WIDTH - 1, 0), (0, 0)))
    y = xp[:, 0:s] * w[0]
    for j in range(1, CONV_WIDTH):
        y = y + xp[:, j:j + s] * w[j]
    return y

def layer_norm(x, g, b):
    xf = x.astype(jnp.float32)
    mu = jnp.mean(xf, axis=-1, keepdims=True)
    var = jnp.mean(jnp.square(xf - mu), axis=-1, keepdims=True)
    y = (xf - mu) * lax.rsqrt(var + LN_EPS)
    return (y * g.astype(jnp.float32) + b.astype(jnp.float32)).astype(x.dtype)

def rms_norm(x, g):
    xf = x.astype(jnp.float32)
    y = xf * lax.rsqrt(jnp.mean(jnp.square(xf), axis=-1, keepdims=True) + SUBLN_EPS)
    return (y * g.astype(jnp.float32)).astype(x.dtype)

def rope_tables(positions):
    inv_freq = ROPE_THETA ** (-jnp.arange(0, ROT_DIM, 2, dtype=jnp.float32) / ROT_DIM)
    ang = positions.astype(jnp.float32)[..., None] * inv_freq
    return jnp.cos(ang), jnp.sin(ang)

def partial_rope(t, cos, sin):
    half = ROT_DIM // 2
    rot = t[..., :ROT_DIM].astype(jnp.float32)
    x1, x2 = rot[..., :half], rot[..., half:]
    c = cos[:, :, None, None, :]
    s = sin[:, :, None, None, :]
    rotated = jnp.concatenate([x1 * c - x2 * s, x2 * c + x1 * s], axis=-1).astype(t.dtype)
    return jnp.concatenate([rotated, t[..., ROT_DIM:]], axis=-1)

def short_conv_mixer(x, w_in, conv_w, w_out):
    b_gate, c_gate, xv = jnp.split(x @ w_in, 3, axis=-1)
    y = b_gate * causal_dwconv(c_gate * xv, conv_w)
    return y @ w_out

def conv_ffn(x, w_up, conv_w, conv_b, w_down):
    h = causal_dwconv(x @ w_up, conv_w) + conv_b
    g, u = jnp.split(h, 2, axis=-1)
    return (jax.nn.silu(g) * u) @ w_down

def shared_kv(x, w_k, w_v, cos, sin):
    bsz, s, _ = x.shape
    k = partial_rope((x @ w_k).reshape(bsz, s, DIFF_HEADS, 2, DIFF_HEAD_DIM), cos, sin)
    v = (x @ w_v).reshape(bsz, s, DIFF_HEADS, V_HEAD_DIM)
    return k, v

def diff_attention(x, k, v, cos, sin, w_q, lam, subln_g, w_o, lambda_init):
    bsz, s, _ = x.shape
    q = (x @ w_q).reshape(bsz, s, DIFF_HEADS, 2, DIFF_HEAD_DIM)
    q = partial_rope(q, cos, sin) * (DIFF_HEAD_DIM ** -0.5)
    lamf = lam.astype(jnp.float32)
    lam_full = (jnp.exp(jnp.sum(lamf[0] * lamf[1])) - jnp.exp(jnp.sum(lamf[2] * lamf[3]))
                + lambda_init)
    kpos = jnp.arange(s)
    neg = jnp.finfo(jnp.float32).min

    def block(i):
        start = i * Q_BLOCK
        qb = lax.dynamic_slice_in_dim(q, start, Q_BLOCK, axis=1)
        sc = jnp.einsum('bqhcd,bkhcd->bhcqk', qb, k).astype(jnp.float32)
        qpos = start + jnp.arange(Q_BLOCK)
        mask = kpos[None, :] <= qpos[:, None]
        p = jax.nn.softmax(jnp.where(mask, sc, neg), axis=-1)
        a = p[:, :, 0] - lam_full * p[:, :, 1]
        return jnp.einsum('bhqk,bkhe->bqhe', a.astype(v.dtype), v)

    o = lax.map(block, jnp.arange(s // Q_BLOCK))
    o = jnp.moveaxis(o, 0, 1).reshape(bsz, s, DIFF_HEADS, V_HEAD_DIM)
    o = rms_norm(o, subln_g) * (1.0 - lambda_init)
    return o.reshape(bsz, s, V_WIDTH) @ w_o

def first_inputs(seed: int = 0) -> dict:
    key = jax.random.key(seed)
    ks = jax.random.split(key, 16)
    f32 = jnp.float32
    nrm = lambda k, shape: jax.random.normal(k, shape, dtype=f32)
    x = nrm(ks[0], (BATCH, SEQ, D_MODEL))
    positions = jnp.broadcast_to(jnp.arange(SEQ, dtype=jnp.int32), (BATCH, SEQ))
    ln_g = 1.0 + 0.02 * nrm(ks[1], (DEPTH, 2, D_MODEL))
    ln_b = 0.02 * nrm(ks[2], (DEPTH, 2, D_MODEL))
    a_w_in = nrm(ks[3], (N_A_LAYERS, D_MODEL, 3 * D_MODEL)) * D_MODEL ** -0.5
    a_conv_w = nrm(ks[4], (N_A_LAYERS, CONV_WIDTH, D_MODEL)) * CONV_WIDTH ** -0.5
    a_w_out = nrm(ks[5], (N_A_LAYERS, D_MODEL, D_MODEL)) * (D_MODEL ** -0.5 * DEEPNORM_BETA)
    kv_w_k = nrm(ks[6], (D_MODEL, QK_WIDTH)) * D_MODEL ** -0.5
    kv_w_v = nrm(ks[7], (D_MODEL, V_WIDTH)) * (D_MODEL ** -0.5 * DEEPNORM_BETA)
    b_w_q = nrm(ks[8], (N_B_LAYERS, D_MODEL, QK_WIDTH)) * D_MODEL ** -0.5
    b_lambda = 0.1 * nrm(ks[9], (N_B_LAYERS, 4, DIFF_HEAD_DIM))
    b_subln_g = 1.0 + 0.02 * nrm(ks[10], (N_B_LAYERS, V_HEAD_DIM))
    b_w_o = nrm(ks[11], (N_B_LAYERS, V_WIDTH, D_MODEL)) * (V_WIDTH ** -0.5 * DEEPNORM_BETA)
    ffn_w_up = nrm(ks[12], (DEPTH, D_MODEL, 2 * D_FF)) * D_MODEL ** -0.5
    ffn_conv_w = nrm(ks[13], (DEPTH, CONV_WIDTH, 2 * D_FF)) * CONV_WIDTH ** -0.5
    ffn_conv_b = 0.02 * nrm(ks[14], (DEPTH, 2 * D_FF))
    ffn_w_down = nrm(ks[15], (DEPTH, D_FF, D_MODEL)) * (D_FF ** -0.5 * DEEPNORM_BETA)
    return {'x': x, 'positions': positions, 'ln_g': ln_g, 'ln_b': ln_b,
            'a_w_in': a_w_in, 'a_conv_w': a_conv_w, 'a_w_out': a_w_out,
            'kv_w_k': kv_w_k, 'kv_w_v': kv_w_v,
            'b_w_q': b_w_q, 'b_lambda': b_lambda, 'b_subln_g': b_subln_g, 'b_w_o': b_w_o,
            'ffn_w_up': ffn_w_up, 'ffn_conv_w': ffn_conv_w, 'ffn_conv_b': ffn_conv_b,
            'ffn_w_down': ffn_w_down}

def first_block(x, positions, ln_g, ln_b, a_w_in, a_conv_w, a_w_out, kv_w_k, kv_w_v,
              b_w_q, b_lambda, b_subln_g, b_w_o, ffn_w_up, ffn_conv_w, ffn_conv_b,
              ffn_w_down):
    cos, sin = rope_tables(positions)
    k_sh, v_sh = None, None
    for layer in range(DEPTH):
        if layer < N_A_LAYERS:
            mix = short_conv_mixer(x, a_w_in[layer], a_conv_w[layer], a_w_out[layer])
        else:
            j = layer - N_A_LAYERS
            if j == 0:
                k_sh, v_sh = shared_kv(x, kv_w_k, kv_w_v, cos, sin)
            lambda_init = 0.8 - 0.6 * math.exp(-0.3 * layer)
            mix = diff_attention(x, k_sh, v_sh, cos, sin, b_w_q[j], b_lambda[j],
                                 b_subln_g[j], b_w_o[j], lambda_init)
        x = layer_norm(DEEPNORM_ALPHA * x + mix, ln_g[layer, 0], ln_b[layer, 0])
        ffn = conv_ffn(x, ffn_w_up[layer], ffn_conv_w[layer], ffn_conv_b[layer], ffn_w_down[layer])
        x = layer_norm(DEEPNORM_ALPHA * x + ffn, ln_g[layer, 1], ln_b[layer, 1])
    return x


EPS = 1e-6
DSW_HEADS = 8
DSW_HEAD_DIM = D_MODEL // 16
DSW_WIDTH = DSW_HEADS * DSW_HEAD_DIM
DSW_PATTERNS = ((128, 1), (512, 4), (2048, 16))
DSW_BLOCK = 128
GLA_HEADS = 4
GLA_DK = D_MODEL // 16
GLA_DV = D_MODEL // 8
GLA_QK_WIDTH = GLA_HEADS * GLA_DK
GLA_WIDTH = GLA_HEADS * GLA_DV
GLA_RANK = 16
GLA_TAU = 16.0
S5_WIDTH = D_MODEL // 2
S5_GROUP = 16
S5_GROUPS = S5_WIDTH // S5_GROUP
S5_STATE = 64
S5_DT_MIN = 1e-3
S5_DT_MAX = 1e-1
HGRN_HEADS = 8
HGRN_DIM = D_MODEL // 16
HGRN_WIDTH = HGRN_HEADS * HGRN_DIM
CHUNK = 64
AB_WIDTH = DSW_WIDTH + GLA_WIDTH
CD_WIDTH = S5_WIDTH + HGRN_WIDTH
AB_SIZES = (DSW_WIDTH, DSW_WIDTH, DSW_WIDTH, GLA_QK_WIDTH, GLA_QK_WIDTH, GLA_WIDTH, GLA_RANK, AB_WIDTH)
CD_SIZES = (S5_WIDTH, HGRN_WIDTH, HGRN_WIDTH, HGRN_WIDTH, CD_WIDTH)
AB_IN = sum(AB_SIZES)
CD_IN = sum(CD_SIZES)
AB_SPLIT = tuple(int(v) for v in np.cumsum(AB_SIZES)[:-1])
CD_SPLIT = tuple(int(v) for v in np.cumsum(CD_SIZES)[:-1])
N_EVEN = (DEPTH + 1) // 2
N_ODD = DEPTH // 2


def rmsnorm(x, g):
    xf = x.astype(jnp.float32)
    return xf * lax.rsqrt(jnp.mean(xf * xf, axis=-1, keepdims=True) + EPS) * g

def head_rmsnorm(o, g):
    o = o * lax.rsqrt(jnp.mean(o * o, axis=-1, keepdims=True) + EPS)
    return o.reshape(o.shape[0], o.shape[1], -1) * g

def dilated_pattern(q, k, v, window, dilation):
    B, S, H, E = q.shape
    d = dilation
    M = S // d
    wc = window // d
    blk = DSW_BLOCK
    nb = -(-M // blk)
    Mp = nb * blk

    def strided(t):
        return jnp.pad(t.reshape(B, M, d, H, E), ((0, 0), (0, Mp - M), (0, 0), (0, 0), (0, 0)))

    def band(t):
        tp = jnp.pad(t, ((0, 0), (blk, 0), (0, 0), (0, 0), (0, 0)))
        prev = tp[:, :Mp].reshape(B, nb, blk, d, H, E)
        cur = t.reshape(B, nb, blk, d, H, E)
        return jnp.concatenate([prev, cur], axis=2)

    qb = strided(q).reshape(B, nb, blk, d, H, E)
    kb = band(strided(k))
    vb = band(strided(v))
    s = jnp.einsum('bnidhe,bnjdhe->bndhij', qb, kb) * (E ** -0.5)
    i_idx = np.arange(blk)[:, None]
    j_idx = np.arange(2 * blk)[None, :]
    n_idx = np.arange(nb)[:, None, None]
    offset = blk + i_idx - j_idx
    key_pos = (n_idx - 1) * blk + j_idx
    mask = (offset >= 0) & (offset <= wc) & (key_pos >= 0)
    s = jnp.where(mask[None, :, None, None], s, -jnp.inf)
    m = jnp.max(s, axis=-1, keepdims=True)
    p = jnp.exp(s - m)
    den = jnp.sum(p, axis=-1)
    o = jnp.einsum('bndhij,bnjdhe->bnidhe', p, vb) / jnp.transpose(den, (0, 1, 4, 2, 3))[..., None]
    lse = jnp.transpose(m[..., 0] + jnp.log(den), (0, 1, 4, 2, 3))
    o = o.reshape(B, Mp, d, H, E)[:, :M].reshape(B, S, H, E)
    lse = lse.reshape(B, Mp, d, H)[:, :M].reshape(B, S, H)
    return o, lse

def dilated_attention(q, k, v):
    outs, lses = [], []
    for window, dilation in DSW_PATTERNS:
        o, lse = dilated_pattern(q, k, v, window, dilation)
        outs.append(o)
        lses.append(lse)
    w = jax.nn.softmax(jnp.stack(lses, axis=0), axis=0)
    return jnp.einsum('pbsh,pbshe->bshe', w, jnp.stack(outs, axis=0))

def chunked_gated_linear_attention(q, k, v, log_g):
    B, S, H, K = q.shape
    V = v.shape[-1]
    n = S // CHUNK

    def blocks(t):
        return jnp.moveaxis(t.reshape(B, n, CHUNK, H, t.shape[-1]), 1, 0)

    qc, kc, vc = blocks(q), blocks(k), blocks(v)
    bc = jnp.cumsum(blocks(log_g), axis=2)
    causal = np.tril(np.ones((CHUNK, CHUNK), dtype=bool))[None, :, :, None, None]

    def step(state, inp):
        qi, ki, vi, bi = inp
        inter = jnp.einsum('bihk,bhkv->bihv', qi * jnp.exp(bi), state)
        diff = bi[:, :, None] - bi[:, None, :]
        decay = jnp.exp(jnp.where(causal, diff, -jnp.inf))
        scores = jnp.einsum('bihk,bjhk,bijhk->bhij', qi, ki, decay)
        intra = jnp.einsum('bhij,bjhv->bihv', scores, vi)
        b_last = bi[:, -1]
        k_dec = ki * jnp.exp(b_last[:, None] - bi)
        state = state * jnp.exp(b_last)[..., None] + jnp.einsum('bjhk,bjhv->bhkv', k_dec, vi)
        return state, inter + intra

    state0 = jnp.zeros((B, H, K, V), jnp.float32)
    _, out = lax.scan(step, state0, (qc, kc, vc, bc))
    return jnp.moveaxis(out, 0, 1).reshape(B, S, H, V)

def _cmul(ar, ai, br, bi):
    return ar * br - ai * bi, ar * bi + ai * br

def _s5_combine(e1, e2):
    a1r, a1i, b1r, b1i = e1
    a2r, a2i, b2r, b2i = e2
    ar, ai = _cmul(a2r, a2i, a1r, a1i)
    br, bi = _cmul(a2r, a2i, b1r, b1i)
    return ar, ai, br + b2r, bi + b2i

def s5_mixer(u, lam_re, lam_im, log_dt, b_re, b_im, c_re, c_im, d_skip, w_glu, b_glu):
    B, S, _ = u.shape
    f32 = jnp.float32
    lam_re, lam_im = lam_re.astype(f32), lam_im.astype(f32)
    b_re, b_im, c_re, c_im = b_re.astype(f32), b_im.astype(f32), c_re.astype(f32), c_im.astype(f32)
    ug = u.reshape(B, S, S5_GROUPS, S5_GROUP)
    dt = jnp.exp(log_dt.astype(f32))[:, None]
    mag = jnp.exp(lam_re * dt)
    ang = lam_im * dt
    ab_re, ab_im = mag * jnp.cos(ang), mag * jnp.sin(ang)
    inv = 1.0 / (lam_re * lam_re + lam_im * lam_im)
    nr, ni = ab_re - 1.0, ab_im
    co_re = (nr * lam_re + ni * lam_im) * inv
    co_im = (ni * lam_re - nr * lam_im) * inv
    bb_re, bb_im = _cmul(co_re[..., None], co_im[..., None], b_re, b_im)
    ut = jnp.swapaxes(ug, 0, 1)
    bu_re = jnp.einsum('gph,sbgh->sbgp', bb_re, ut)
    bu_im = jnp.einsum('gph,sbgh->sbgp', bb_im, ut)
    a_re = jnp.broadcast_to(ab_re, (S, 1, S5_GROUPS, S5_STATE))
    a_im = jnp.broadcast_to(ab_im, (S, 1, S5_GROUPS, S5_STATE))
    _, _, x_re, x_im = lax.associative_scan(_s5_combine, (a_re, a_im, bu_re, bu_im), axis=0)
    y = (jnp.einsum('ghp,sbgp->bsgh', c_re, x_re) - jnp.einsum('ghp,sbgp->bsgh', c_im, x_im)
         + d_skip * ug)
    y = jax.nn.gelu(y.reshape(B, S, S5_WIDTH))
    return y * jax.nn.sigmoid(y @ w_glu + b_glu)

def ab_layer(h, w_in, gla_w_gate, gla_b_gate, gla_norm_g, w_out):
    B, S, _ = h.shape
    z = h @ w_in
    qa, ka, va, qb, kb, vb, g_low, gate = jnp.split(z, AB_SPLIT, axis=-1)
    sh_a = (B, S, DSW_HEADS, DSW_HEAD_DIM)
    ya = dilated_attention(qa.reshape(sh_a), ka.reshape(sh_a), va.reshape(sh_a)).reshape(B, S, DSW_WIDTH)
    log_a = jax.nn.log_sigmoid(g_low @ gla_w_gate + gla_b_gate) / GLA_TAU
    sh_k = (B, S, GLA_HEADS, GLA_DK)
    ob = chunked_gated_linear_attention((qb * GLA_DK ** -0.5).reshape(sh_k), kb.reshape(sh_k),
                                        vb.reshape(B, S, GLA_HEADS, GLA_DV), log_a.reshape(sh_k))
    yb = head_rmsnorm(ob, gla_norm_g)
    y = jnp.concatenate([ya, yb], axis=-1) * jax.nn.silu(gate)
    return y @ w_out

def cd_layer(h, w_in, lam_re, lam_im, log_dt, b_re, b_im, c_re, c_im, d_skip, w_glu, b_glu,
             lower_bound, hgrn_norm_g, w_out):
    B, S, _ = h.shape
    z = h @ w_in
    u, qd, fd, idd, gate = jnp.split(z, CD_SPLIT, axis=-1)
    yc = s5_mixer(u, lam_re, lam_im, log_dt, b_re, b_im, c_re, c_im, d_skip, w_glu, b_glu)
    f = lower_bound + (1.0 - lower_bound) * jax.nn.sigmoid(fd)
    sh = (B, S, HGRN_HEADS, HGRN_DIM)
    od = chunked_gated_linear_attention(jax.nn.silu(qd).reshape(sh), (1.0 - f).reshape(sh),
                                        idd.reshape(sh), jnp.log(f).reshape(sh))
    yd = head_rmsnorm(od, hgrn_norm_g)
    y = jnp.concatenate([yc, yd], axis=-1) * jax.nn.silu(gate)
    return y @ w_out

def second_inputs(seed: int = 0) -> dict:
    key = jax.random.key(seed)
    ks = jax.random.split(key, 24)
    f32 = jnp.float32

    def nrm(k, shape, s):
        return s * jax.random.normal(k, shape, f32)

    G, P, Hc = S5_GROUPS, S5_STATE, S5_GROUP
    return {
        'x': nrm(ks[0], (BATCH, SEQ, D_MODEL), 1.0),
        'norm_g': 1.0 + nrm(ks[1], (DEPTH, D_MODEL), 0.02),
        'final_g': 1.0 + nrm(ks[2], (D_MODEL,), 0.02),
        'ab_w_in': nrm(ks[3], (N_EVEN, D_MODEL, AB_IN), D_MODEL ** -0.5),
        'gla_w_gate': nrm(ks[4], (N_EVEN, GLA_RANK, GLA_QK_WIDTH), GLA_RANK ** -0.5),
        'gla_b_gate': nrm(ks[5], (N_EVEN, GLA_QK_WIDTH), 0.1),
        'gla_norm_g': 1.0 + nrm(ks[6], (N_EVEN, GLA_WIDTH), 0.02),
        'ab_w_out': nrm(ks[7], (N_EVEN, AB_WIDTH, D_MODEL), AB_WIDTH ** -0.5),
        'cd_w_in': nrm(ks[8], (N_ODD, D_MODEL, CD_IN), D_MODEL ** -0.5),
        's5_lam_re': -0.5 + nrm(ks[9], (N_ODD, G, P), 0.01),
        's5_lam_im': math.pi * jnp.arange(P, dtype=f32) + nrm(ks[10], (N_ODD, G, P), 0.01),
        's5_log_dt': jax.random.uniform(ks[11], (N_ODD, G), f32, math.log(S5_DT_MIN), math.log(S5_DT_MAX)),
        's5_b_re': nrm(ks[12], (N_ODD, G, P, Hc), (2 * Hc) ** -0.5),
        's5_b_im': nrm(ks[13], (N_ODD, G, P, Hc), (2 * Hc) ** -0.5),
        's5_c_re': nrm(ks[14], (N_ODD, G, Hc, P), 0.5),
        's5_c_im': nrm(ks[15], (N_ODD, G, Hc, P), 0.5),
        's5_d': nrm(ks[16], (N_ODD, G, Hc), 1.0),
        's5_w_glu': nrm(ks[17], (N_ODD, S5_WIDTH, S5_WIDTH), S5_WIDTH ** -0.5),
        's5_b_glu': nrm(ks[18], (N_ODD, S5_WIDTH), 0.1),
        'hgrn_gamma': nrm(ks[19], (DEPTH, HGRN_WIDTH), 1.0),
        'hgrn_norm_g': 1.0 + nrm(ks[20], (N_ODD, HGRN_WIDTH), 0.02),
        'cd_w_out': nrm(ks[21], (N_ODD, CD_WIDTH, D_MODEL), CD_WIDTH ** -0.5),
    }

def second_block(x, norm_g, final_g, ab_w_in, gla_w_gate, gla_b_gate, gla_norm_g, ab_w_out,
              cd_w_in, s5_lam_re, s5_lam_im, s5_log_dt, s5_b_re, s5_b_im, s5_c_re, s5_c_im,
              s5_d, s5_w_glu, s5_b_glu, hgrn_gamma, hgrn_norm_g, cd_w_out):
    h = x.astype(jnp.float32)
    sm = jax.nn.softmax(hgrn_gamma.astype(jnp.float32), axis=0)
    lower_bounds = jnp.cumsum(sm, axis=0) - sm[0]
    for l in range(DEPTH):
        hn = rmsnorm(h, norm_g[l])
        j = l // 2
        if l % 2 == 0:
            h = h + ab_layer(hn, ab_w_in[j], gla_w_gate[j], gla_b_gate[j], gla_norm_g[j], ab_w_out[j])
        else:
            h = h + cd_layer(hn, cd_w_in[j], s5_lam_re[j], s5_lam_im[j], s5_log_dt[j], s5_b_re[j],
                             s5_b_im[j], s5_c_re[j], s5_c_im[j], s5_d[j], s5_w_glu[j], s5_b_glu[j],
                             lower_bounds[l], hgrn_norm_g[j], cd_w_out[j])
    return rmsnorm(h, final_g).astype(x.dtype)


_first_inputs = second_inputs


def second_inputs(seed=0):
    import zlib

    import numpy as np

    out = dict(_first_inputs(seed))
    spreads = {}
    factors = {'final_g': 20.998,
     'gla_b_gate': 3.151,
     'gla_norm_g': 6.458,
     's5_lam_re': 200.0,
     's5_b_glu': 200.0,
     'hgrn_norm_g': 99.613,
     's5_lam_im': 64.0,
     's5_log_dt': 64.0,
     's5_b_re': 64.0,
     's5_b_im': 64.0,
     's5_c_re': 64.0,
     's5_c_im': 64.0,
     's5_w_glu': 51.144,
     's5_d': 4.621}
    for name, (base, spread) in spreads.items():
        noise = np.random.default_rng([zlib.crc32(name.encode()), seed]).standard_normal(out[name].shape)
        drawn = base * np.exp(spread * noise) if base else spread * noise
        out[name] = __import__('jax').numpy.asarray(drawn.astype(out[name].dtype))
    for name, factor in factors.items():
        out[name] = (out[name] * factor).astype(out[name].dtype)
    return out


_narrow_inputs = second_inputs


def second_inputs(seed=0):
    out = dict(_narrow_inputs(seed))
    wider = {'final_g': 3.1, 's5_d': 3.12, 's5_w_glu': 3.92, 's5_b_glu': 12.0, 'hgrn_norm_g': 3.42}
    for name, times in wider.items():
        mean = out[name].mean()
        out[name] = (mean + times * (out[name] - mean)).astype(out[name].dtype)
    return out


def setup_inputs(seed=0):
    out = dict(first_inputs(seed))
    for name, value in second_inputs(seed + 1).items():
        if name != "x":
            out[name + "_2"] = value
    return out


def reference(
    x, positions, ln_g, ln_b, a_w_in, a_conv_w, a_w_out, kv_w_k, kv_w_v, b_w_q, b_lambda,
    b_subln_g, b_w_o, ffn_w_up, ffn_conv_w, ffn_conv_b, ffn_w_down, norm_g_2, final_g_2,
    ab_w_in_2, gla_w_gate_2, gla_b_gate_2, gla_norm_g_2, ab_w_out_2, cd_w_in_2, s5_lam_re_2,
    s5_lam_im_2, s5_log_dt_2, s5_b_re_2, s5_b_im_2, s5_c_re_2, s5_c_im_2, s5_d_2, s5_w_glu_2,
    s5_b_glu_2, hgrn_gamma_2, hgrn_norm_g_2, cd_w_out_2,
):
    x = first_block(
        x, positions, ln_g, ln_b, a_w_in, a_conv_w, a_w_out, kv_w_k, kv_w_v, b_w_q, b_lambda,
        b_subln_g, b_w_o, ffn_w_up, ffn_conv_w, ffn_conv_b, ffn_w_down,
    )
    return second_block(
        x, norm_g_2, final_g_2, ab_w_in_2, gla_w_gate_2, gla_b_gate_2, gla_norm_g_2, ab_w_out_2,
        cd_w_in_2, s5_lam_re_2, s5_lam_im_2, s5_log_dt_2, s5_b_re_2, s5_b_im_2, s5_c_re_2,
        s5_c_im_2, s5_d_2, s5_w_glu_2, s5_b_glu_2, hgrn_gamma_2, hgrn_norm_g_2, cd_w_out_2,
    )


_drawn_inputs = setup_inputs


def setup_inputs(seed=0):
    import zlib

    import numpy as np

    out = dict(_drawn_inputs(seed))
    spreads = {}
    factors = {'b_subln_g': 3.703, 's5_b_glu_2': 3.266}
    for name, (base, spread) in spreads.items():
        noise = np.random.default_rng([zlib.crc32(name.encode()), seed]).standard_normal(out[name].shape)
        drawn = base * np.exp(spread * noise) if base else spread * noise
        out[name] = __import__('jax').numpy.asarray(drawn.astype(out[name].dtype))
    for name, factor in factors.items():
        out[name] = (out[name] * factor).astype(out[name].dtype)
    return out
```

```python
import math
from collections import deque
from contextlib import ExitStack

import numpy as np

import concourse.bass as bass
from concourse import mybir

F32 = mybir.dt.float32
BF16 = mybir.dt.bfloat16
I32 = mybir.dt.int32
ALU = mybir.AluOpType
ACT = mybir.ActivationFunctionType
AX = mybir.AxisListType

D = 2048
T = 256
NT = D // 128
DFF = 5632
NF = DFF // 128
ALPHA = 4.0 ** 0.25
LAM_INIT = 0.8 - 0.6 * math.exp(-0.3)
NEG = -1e30
RF = 4
RB = 4
LA = 3

MAGIC = 12582912.0
TWO_PI = 2.0 * math.pi
C1 = 6.28125
C2 = float(np.float32(np.round((TWO_PI - C1) * 2.0 ** 21) / 2.0 ** 21))
C3 = float(np.float32(TWO_PI - C1 - C2))
PI_CLAMP = 3.1415925


def columns(spec):
    at, out = 0, {}
    for name, n in spec:
        out[name] = (at, at + n)
        at += n
    return out, at


CONST, NCONST = columns([("ident", 128), ("rope", 32), ("freq", 1), ("eps5", 1), ("eps6", 1), ("one", 1),
                         ("halfpi", 1), ("zero", 1), ("mask", 384), ("dmask", 384), ("dcount", 384),
                         ("lmask", 1024), ("time", 256)])
PARAM, NPARAM = columns([("ln_g", 64), ("ln_b", 64), ("a_conv", 48), ("f_conv", 528), ("f_bias", 176),
                         ("subln", 2), ("norm", 32), ("final", 16), ("gla_b", 4), ("gla_norm", 8),
                         ("lam_re", 32), ("lam_im", 32), ("log_dt", 32), ("s5_d", 8), ("b_glu", 8),
                         ("gamma", 16), ("hgrn_norm", 8), ("b_lambda", 4)])


def constants():
    c = np.zeros((128, NCONST), np.float32)

    def put(name, v):
        a, b = CONST[name]
        c[:, a:b] = v

    put("ident", np.eye(128))
    rope = np.zeros((128, 32))
    for i in range(16):
        rope[i + 16, i] = -1.0
        rope[i, i + 16] = 1.0
    put("rope", rope)
    freq = np.float32(500000.0) ** (-np.arange(0, 32, 2, dtype=np.float32) / np.float32(32))
    col = np.zeros((128, 1))
    col[0:16, 0] = freq
    col[16:32, 0] = freq
    put("freq", col)
    put("eps5", 1e-5)
    put("eps6", 1e-6)
    put("one", 1.0)
    put("halfpi", math.pi / 2)
    i = np.arange(128)[:, None]
    j = np.arange(128)[None, :]
    tri = np.where(j <= i, 0.0, NEG)
    put("mask", np.concatenate([np.zeros((128, 128)), tri, tri], 1))
    d = np.concatenate([128 + i - j, i - j, i - j], 1)
    count = (d >= 0) * ((d <= 128).astype(int) + (d % 4 == 0) + (d % 16 == 0))
    put("dmask", np.where(count > 0, 0.0, NEG))
    put("dcount", count)
    lm = np.zeros((128, 8, 128))
    lm[:, 0, :] = i == j
    for l in range(1, 8):
        h = 2 ** (l - 1)
        lm[:, l, :] = (i // (2 * h) == j // (2 * h)) & (i % (2 * h) < h) & (j % (2 * h) >= h)
    put("lmask", lm.reshape(128, 1024))
    put("time", np.arange(256)[None, :])
    return c


class Queue:

    def __init__(self, eng, sem):
        self.eng, self.sem, self.n, self.seen = eng, sem, 0, {}

    def w(self, *marks):
        for m in marks:
            if m is None:
                continue
            q, v = m
            if self.seen.get(id(q), 0) < v:
                self.eng.wait_ge(q.sem, v)
                self.seen[id(q)] = v
        return self.eng

    def do(self, ins, by=1):
        ins.then_inc(self.sem, by)
        self.n += by
        return self, self.n

    def now(self):
        return (self, self.n) if self.n else None


def two_block_model(nc, A, out):
    ctx = ExitStack()
    with ctx:
        def sb(name, shape, dt=F32):
            return ctx.enter_context(nc.sbuf_tensor(name, shape, dt))

        def sem(name):
            return ctx.enter_context(nc.semaphore(name))

        XA = sb("XA", [128, NT, T])
        XH = sb("XH", [128, NT, T], BF16)
        XL = sb("XL", [128, NT, T], BF16)
        WF = sb("WF", [128, RF, 4, 512])
        WH = sb("WH", [128, RB, 4, 512], BF16)
        WL = sb("WL", [128, RB, 4, 512], BF16)
        CN = sb("CN", [128, NCONST])
        PR = sb("PR", [128, NPARAM])
        ONE_D = sb("ONE_D", [128, 128])
        ONE_256 = sb("ONE_256", [128, 128])
        ONE_128 = sb("ONE_128", [128, 128])
        SCR = sb("SCR", [128, 23040])
        STAT = sb("STAT", [128, 4, T])
        PSG = [ctx.enter_context(nc.psum_tensor(f"PSG{i}", [128, 4, T], F32)) for i in range(2)]
        PB = ctx.enter_context(nc.psum_tensor("PB", [128, 4, 512], F32))

        PE = Queue(nc.tensor, sem("s_pe"))
        V = Queue(nc.vector, sem("s_v"))
        S = Queue(nc.scalar, sem("s_s"))
        G = Queue(nc.gpsimd, sem("s_g"))
        SP = Queue(nc.sync, sem("s_sp"))
        d_in = Queue(None, sem("d_in"))
        d_w = [Queue(None, sem(f"d_w{i}")) for i in range(RF)]
        d_out = Queue(None, sem("d_out"))

        def dma(q, dst, src, *marks):
            return q.do(SP.w(*marks).dma_start(dst, src), 16)

        def cn(name, a=0, n=None):
            lo, hi = CONST[name]
            return CN[:, lo + a:hi if n is None else lo + a + n]

        def pr(name, a=0, n=1):
            lo = PARAM[name][0]
            return PR[:, lo + a:lo + a + n]

        def bc(ap, n):
            return ap.unsqueeze(1).broadcast_to([128, n, ap.shape[-1]])

        def bcl(ap, n):
            return ap.unsqueeze(2).broadcast_to([ap.shape[0], ap.shape[1], n])

        def scr(at, *shape, dt=F32):
            n = int(np.prod(shape))
            words = n if dt == F32 else n // 2
            v = SCR[:, at:at + words]
            if dt != F32:
                v = v.bitcast(dt)
            if len(shape) == 2:
                v = v.rearrange("p (a b) -> p a b", b=shape[1])
            if len(shape) == 3:
                v = v.rearrange("p (a b c) -> p a b c", b=shape[1], c=shape[2])
            return v

        def barrier():
            marks = [q.now() for q in (PE, V, S, G)]
            for q in (PE, V, S, G, SP):
                q.w(*[m for m in marks if m and m[0] is not q])
                if q.now() and q in (V, S, G):
                    q.w(q.now())

        background = deque()

        def step():
            while background:
                try:
                    next(background[0])
                    return
                except StopIteration:
                    background.popleft()

        def drain():
            while background:
                step()

        t_cn = dma(d_in, CN[:, :], A["consts"])
        t_cn = dma(d_in, PR[:, :], A["params"])
        t_in = dma(d_in, XA[:, :, :], A["xT"].rearrange("(t p) n -> p t n", p=128))
        G.do(G.w().memset(ONE_D[:, :], 1.0 / D))
        G.do(G.w().memset(ONE_256[:, :], 1.0 / 256))
        t_one = G.do(G.w().memset(ONE_128[:, :], 1.0 / 128))
        for q in (PE, V, S, G):
            q.w(t_in, t_one)

        groups = []

        def add(w, col, width, K, tag):
            groups.append(dict(w=w, col=col, width=width, K=K, tag=tag))

        for j in range(4):
            for part in (1, 2, 0):
                add(A["a_w_in"], part * D + j * 512, 512, D, "abc"[part])
        for j in range(4):
            add(A["a_w_out"], j * 512, 512, D, "o")

        def add_ffn(l):
            for j in range(11):
                add(A["ffn_w_up"][l], j * 512, 512, D, "g")
                add(A["ffn_w_up"][l], DFF + j * 512, 512, D, "u")
            for j in range(4):
                add(A["ffn_w_down"][l], j * 512, 512, DFF, "down")

        add_ffn(0)
        for w in ("kv_w_v", "kv_w_k", "b_w_q", "b_w_o"):
            for j in range(4):
                add(A[w], j * 512, 512, D, w)
        add_ffn(1)
        AB = [("va", 2048, 2), ("ka", 1024, 2), ("qa", 0, 2), ("kb", 3584, 1), ("qb", 3072, 1), ("vb", 4096, 2)]
        for tag, col, n in AB:
            for j in range(n):
                add(A["ab_w_in"], col + 512 * j, 512, D, tag)
        add(A["ab_w_in"], 5120, 16, D, "glow")
        for j in range(4):
            add(A["ab_w_in"], 5136 + 512 * j, 512, D, "gate")
        for j in range(4):
            add(A["ab_w_out"], j * 512, 512, D, "o")
        for tag, col, n in [("u", 0, 2), ("gate", 4096, 4), ("idd", 3072, 2), ("fd", 2048, 2), ("qd", 1024, 2)]:
            for j in range(n):
                add(A["cd_w_in"], col + 512 * j, 512, D, tag)
        for j in range(2):
            add(A["s5_w_glu"], j * 512, 512, 1024, "glu")
        for j in range(4):
            add(A["cd_w_out"], j * 512, 512, D, "o")

        chunks = []
        for g in groups:
            g["first"] = len(chunks)
            rows = 512 if g["width"] == 512 else g["K"]
            for k0 in range(0, g["K"], rows):
                chunks.append((g, k0, rows))

        def shaped(ring, i, rows, width):
            if width == 512:
                return ring[:, i, :, :]
            n = rows // 128 * width
            return ring[:, i, 0, 0:n].rearrange("p (t n) -> p t n", n=width)

        t_load, t_split, t_used = {}, {}, {}

        def load(i):
            if i >= len(chunks) or i in t_load:
                return
            g, k0, rows = chunks[i]
            src = g["w"][k0:k0 + rows, g["col"]:g["col"] + g["width"]].rearrange("(t p) n -> p t n", p=128)
            before = t_split.get(i - RF, (None, None))
            t_load[i] = dma(d_w[i % RF], shaped(WF, i % RF, rows, g["width"]), src, *before)

        def split(i):
            if i >= len(chunks) or i in t_split:
                return
            load(i)
            g, k0, rows = chunks[i]
            w, h, l = (shaped(r, i % n, rows, g["width"]) for r, n in ((WF, RF), (WH, RB), (WL, RB)))
            free = t_used.get(i - RB)
            t_h = S.do(S.w(t_load[i], free).activation(h, w, ACT.Copy))
            t_l = V.do(V.w(t_load[i], t_h, free).tensor_tensor(l, w, h, ALU.subtract))
            t_split[i] = (t_h, t_l)
            load(i + RF)

        for i in range(RF):
            load(i)

        state = dict(g=0, free=[None, None])

        def gemm(tags, x, evac, row_major=False):
            xh, xl, xt = x
            for tag in tags:
                gi = state["g"]
                g = groups[gi]
                assert g["tag"] == tag, (g["tag"], tag)
                state["g"] += 1
                ps = PSG[gi % 2]
                psr = ps[:, :, :].rearrange("p a b -> p (a b)").rearrange("p (t n) -> p t n", n=512)
                PE.w(state["free"][gi % 2])
                nk = g["K"] // 128
                k = 0
                i = g["first"]
                while k < nk:
                    for ahead in range(LA + 1):
                        split(i + ahead) if ahead == 0 or i + ahead - RB in t_used or i + ahead < RB else None
                    _, k0, rows = chunks[i]
                    h, l = (shaped(r, i % RB, rows, g["width"]) for r in (WH, WL))
                    PE.w(*t_split[i])
                    for kk in range(rows // 128):
                        PE.w(xt[k])
                        st, sp = k == 0, k == nk - 1
                        if g["width"] == 16:
                            for n, (a, b) in enumerate(((h, xh), (h, xl), (l, xh))):
                                last = nc.tensor.matmul(ps[0:16, 0, :], a[:, kk, :], b[:, k, :],
                                                        start=st and n == 0, stop=sp and n == 2,
                                                        skip_group_check=True)
                        elif row_major:
                            for m in range(2):
                                c = slice(m * 128, m * 128 + 128)
                                for n, (a, b) in enumerate(((xh, h), (xh, l), (xl, h))):
                                    last = nc.tensor.matmul(psr[:, m, :], a[:, k, c], b[:, kk, :],
                                                            start=st and n == 0, stop=sp and n == 2,
                                                            skip_group_check=True)
                        else:
                            for m in range(4):
                                c = slice(m * 128, m * 128 + 128)
                                for n, (a, b) in enumerate(((h, xh), (h, xl), (l, xh))):
                                    last = nc.tensor.matmul(ps[:, m, :], a[:, kk, c], b[:, k, :],
                                                            start=st and n == 0 and m % 2 == 0,
                                                            stop=sp and n == 2, skip_group_check=True)
                        k += 1
                    t_used[i] = PE.do(last)
                    i += 1
                    step()
                done = PE.now()
                state["free"][gi % 2] = evac(gi - 0, psr if row_major else ps, done)

        def split_x(hi, lo, src, *marks):
            t_h = S.do(S.w(*marks).activation(hi, src, ACT.Copy))
            return V.do(V.w(t_h, *marks).tensor_tensor(lo, src, hi, ALU.subtract))

        def mm(o, lhsT, rhs, start, stop):
            return nc.tensor.matmul(o, lhsT, rhs, start=start, stop=stop, skip_group_check=True)

        SQ = None

        def sums(marks, src, bank, of):
            for g in range(4):
                PE.w(marks[g])
                for n in range(4):
                    k = 4 * g + n
                    last = mm(PB[:, bank, 0:T], of[:, :], src(k), k == 0, k == NT - 1)
                if g == 3:
                    state["sum"] = PE.do(last)
                else:
                    state["sum"] = PE.do(last)
                yield

        def rstd(bank, mark, eps, dst):
            t = S.do(S.w(mark).activation(dst, PB[:, bank, 0:T], ACT.Sqrt, bias=cn(eps)))
            return V.do(V.w(t).reciprocal(dst, dst))

        def layer_norm(which, SQ):
            drain()
            t_m = S.do(S.w(state["sum"]).activation(STAT[:, 0, :], PB[:, 0, 0:T], ACT.Copy))
            t_c, t_s = [], []
            for g in range(4):
                x = XA[:, 4 * g:4 * g + 4, :]
                t_c.append(V.do(V.w(t_m).tensor_tensor(x, x, bc(STAT[:, 0, :], 4), ALU.subtract)))
            t_q = [None, None]
            for g in range(4):
                t_s.append(S.do(S.w(t_c[g], t_q[g % 2]).activation(SQ[g % 2], XA[:, 4 * g:4 * g + 4, :], ACT.Square)))
                PE.w(t_s[g])
                for n in range(4):
                    k = 4 * g + n
                    last = mm(PB[:, 1, 0:T], ONE_D[:, :], SQ[g % 2][:, n, :], k == 0, k == NT - 1)
                t_q[g % 2] = PE.do(last)
            t_r = rstd(1, t_q[1], "eps5", STAT[:, 1, :])
            marks = []
            for g in range(4):
                x = XA[:, 4 * g:4 * g + 4, :]
                t_n = V.do(V.w(t_r).tensor_tensor(x, x, bc(STAT[:, 1, :], 4), ALU.mult))
                for n in range(4):
                    k = 4 * g + n
                    V.w(t_n)
                    t = V.do(nc.vector.tensor_scalar(XA[:, k, :], XA[:, k, :], pr("ln_g", 16 * which + k),
                                                     pr("ln_b", 16 * which + k), ALU.mult, ALU.add))
                t = split_x(XH[:, 4 * g:4 * g + 4, :], XL[:, 4 * g:4 * g + 4, :], x, t)
                marks += [t] * 4
            return XH, XL, marks

        def rms_norm(weight, SQ, done=None):
            t_q = [None, None]
            for g in range(4):
                t_s = S.do(S.w(V.now(), t_q[g % 2]).activation(SQ[g % 2], XA[:, 4 * g:4 * g + 4, :], ACT.Square))
                PE.w(t_s)
                for n in range(4):
                    k = 4 * g + n
                    last = mm(PB[:, 1, 0:T], ONE_D[:, :], SQ[g % 2][:, n, :], k == 0, k == NT - 1)
                t_q[g % 2] = PE.do(last)
            t_r = rstd(1, t_q[1], "eps6", STAT[:, 1, :])
            marks = []
            for g in range(4):
                for n in range(4):
                    k = 4 * g + n
                    V.w(t_r, t_q[1], t_q[0])
                    dst = XA[:, k, :] if done else SQ[g % 2][:, n, :]
                    t = V.do(nc.vector.scalar_tensor_tensor(dst, XA[:, k, :], weight(k), STAT[:, 1, :],
                                                            ALU.mult, ALU.mult))
                if done:
                    done(g, t)
                else:
                    t = split_x(XH[:, 4 * g:4 * g + 4, :], XL[:, 4 * g:4 * g + 4, :], SQ[g % 2], t)
                    V.w(t)
                    marks += [t] * 4
            return XH, XL, marks

        def residual(scale):
            at = [0]
            marks = []

            def evac(gi, ps, done):
                g = at[0]
                at[0] += 1
                x = XA[:, 4 * g:4 * g + 4, :]
                if scale is None:
                    t = V.do(V.w(done).tensor_tensor(x, ps[:, :, :], x, ALU.add))
                else:
                    t = V.do(V.w(done).scalar_tensor_tensor(x, x, scale, ps[:, :, :], ALU.mult, ALU.add))
                marks.append(t)
                if scale is not None:
                    background.append(one_sum(g, t))
                return t

            def one_sum(g, t):
                PE.w(t)
                for n in range(4):
                    k = 4 * g + n
                    last = mm(PB[:, 0, 0:T], ONE_D[:, :], XA[:, k, :], k == 0, k == NT - 1)
                state["sum"] = PE.do(last)
                yield

            return evac

        marks = []
        for g in range(4):
            t = split_x(XH[:, 4 * g:4 * g + 4, :], XL[:, 4 * g:4 * g + 4, :], XA[:, 4 * g:4 * g + 4, :])
            marks += [t] * 4
        x = (XH, XL, marks)

        YH = scr(0, NT, T, dt=BF16)
        YL = scr(2048, NT, T, dt=BF16)
        CB = scr(4096, 4, T)
        CX = scr(5120, 4, T + 2)
        CA = scr(6160, 4, T)
        YF = scr(7184, 4, T)
        y_marks = []
        st = {}
        t_pad = G.do(G.w().memset(CX[:, :, 0:2], 0.0))

        def mixer(gi, ps, done):
            tag = groups[gi]["tag"]
            j = gi // 3
            if tag == "b":
                st["c"] = S.do(S.w(done, st.get("cx")).activation(CB, ps[:, :, :], ACT.Copy))
                return st["c"]
            if tag == "c":
                st["cx"] = V.do(V.w(done, st["c"], st.get("conv"), t_pad).tensor_tensor(
                    CX[:, :, 2:T + 2], ps[:, :, :], CB, ALU.mult))
                return st["cx"]
            ts = []
            for n in range(4):
                V.w(st["cx"], st.get("yf"))
                ts.append(V.do(nc.vector.tensor_scalar(CA[:, n, :], CX[:, n, 0:T], pr("a_conv", 4 * j + n), None,
                                                       ALU.mult)))
            for tap in (1, 2):
                for n in range(4):
                    V.w(ts[n])
                    ts[n] = V.do(nc.vector.scalar_tensor_tensor(
                        CA[:, n, :], CX[:, n, tap:tap + T], pr("a_conv", 16 * tap + 4 * j + n), CA[:, n, :],
                        ALU.mult, ALU.add))
            st["conv"] = ts[3]
            t = V.do(V.w(done, ts[3], st.get("y")).tensor_tensor(YF, ps[:, :, :], CA, ALU.mult))
            st["yf"] = t
            st["y"] = split_x(YH[:, 4 * j:4 * j + 4, :], YL[:, 4 * j:4 * j + 4, :], YF, t)
            y_marks.extend([st["y"]] * 4)
            return t

        gemm(["b", "c", "a"] * 4, x, mixer)
        SQA = [scr(8208, 4, T), scr(9232, 4, T)]
        gemm(["o"] * 4, (YH, YL, y_marks), residual(ALPHA))
        x = layer_norm(0, SQA)

        def ffn(l, x):
            barrier()
            HH = scr(0, NF, T, dt=BF16)
            HL = scr(NF * 128, NF, T, dt=BF16)
            B0 = NF * 256
            GA = scr(B0, 4, T)
            GS = scr(B0 + 1024, 4, T)
            UA = scr(B0 + 2048, 4, T)
            HF = scr(B0 + 3072, 4, T)
            SQF = [scr(B0 + 4096, 4, T), scr(B0 + 5120, 4, T)]
            h_marks = []
            st = {}

            def evac(gi, ps, done):
                tag = groups[gi]["tag"]
                j = st.get("j", 0)
                dst, base, free = (GA, 0, st.get("gs")) if tag == "g" else (UA, NF, st.get("hf"))
                ts = []
                for n in range(4):
                    f = base + 4 * j + n
                    S.w(done, free)
                    ts.append(S.do(nc.scalar.activation(dst[:, n, :], ps[:, n, :], ACT.Identity,
                                                        bias=pr("f_bias", 88 * l + f),
                                                        scale=pr("f_conv", 264 * l + 176 + f))))
                for tap, sh in ((1, 1), (0, 2)):
                    for n in range(4):
                        f = base + 4 * j + n
                        V.w(ts[n], ts[n | 1])
                        ts[n] = V.do(nc.vector.scalar_tensor_tensor(
                            dst[:, n, sh:T], ps[:, n, 0:T - sh], pr("f_conv", 264 * l + 88 * tap + f),
                            dst[:, n, sh:T], ALU.mult, ALU.add))
                if tag == "g":
                    st["gs"] = S.do(S.w(ts[3], st.get("hf")).activation(GS, GA, ACT.Silu))
                else:
                    st["hf"] = V.do(V.w(ts[3], st["gs"], st.get("h")).tensor_tensor(HF, UA, GS, ALU.mult))
                    st["h"] = split_x(HH[:, 4 * j:4 * j + 4, :], HL[:, 4 * j:4 * j + 4, :], HF, st["hf"])
                    h_marks.extend([st["h"]] * 4)
                    st["j"] = j + 1
                return ts[3]

            gemm(["g", "u"] * 11, x, evac)
            gemm(["down"] * 4, (HH, HL, h_marks), residual(ALPHA))
            return layer_norm(2 * l + 1, SQF)

        x = ffn(0, x)

        barrier()
        KA = scr(0, NT, T)
        VT = scr(4096, 2, D)
        YH = scr(8192, NT, T, dt=BF16)
        YL = scr(10240, NT, T, dt=BF16)
        QA = [scr(12288, 4, T), scr(13312, 4, T)]
        COS = scr(14336, T)
        SIN = scr(14592, T)
        W0 = 14848
        RT = scr(W0, 4, T)
        SS = scr(W0 + 1024, 2, 384)
        PP = scr(W0 + 1792, 2, 384)
        AA = scr(W0 + 2560, 2, 384)
        AT = scr(W0 + 3328, 384)
        OF = scr(W0 + 3712, 2, T)
        OQ = scr(W0 + 4224, 2, T)
        SM = scr(W0 + 4736, 64)
        POSI = scr(W0 + 4800, T).bitcast(I32)
        SQB = [scr(W0 + 5056, 4, T), scr(W0 + 6080, 4, T)]
        GN = SM[:, 32:34]
        LAM = SM[:, 34:35]

        def reduce_angle(dst, src, tmp, *marks):
            t = V.do(V.w(*marks).tensor_scalar(tmp, src, 1.0 / TWO_PI, MAGIC, ALU.mult, ALU.add))
            t = V.do(V.w(t).tensor_scalar(tmp, tmp, MAGIC, None, ALU.subtract))
            t = V.do(V.w(t).scalar_tensor_tensor(dst, tmp, -C1, src, ALU.mult, ALU.add))
            t = V.do(V.w(t).scalar_tensor_tensor(dst, tmp, -C2, dst, ALU.mult, ALU.add))
            t = V.do(V.w(t).scalar_tensor_tensor(dst, tmp, -C3, dst, ALU.mult, ALU.add))
            return V.do(V.w(t).tensor_scalar(dst, dst, PI_CLAMP, -PI_CLAMP, ALU.min, ALU.max))

        def cos_sin(cos, sin, ang, tmp, mark, *free):
            t_s = S.do(S.w(mark, *free).activation(sin, ang, ACT.Sin))
            t_a = S.do(S.w(mark).activation(tmp, ang, ACT.Abs))
            return t_s, S.do(S.w(t_a).activation(cos, tmp, ACT.Sin, bias=cn("halfpi"), scale=-1.0))

        d_pos = Queue(None, sem("d_pos"))
        t_p = dma(d_pos, POSI, A["positions"].partition_broadcast(128))
        t = V.do(V.w(t_p).tensor_scalar(RT[:, 0, :], POSI, 1.0, None, ALU.mult))
        t = V.do(V.w(t).tensor_scalar(RT[:, 0, :], RT[:, 0, :], cn("freq"), None, ALU.mult))
        t = reduce_angle(RT[:, 1, :], RT[:, 0, :], RT[:, 2, :], t)
        t_sin, t_cos = cos_sin(COS, SIN, RT[:, 1, :], RT[:, 2, :], t)

        lb = pr("b_lambda", 0, 4)
        t = V.do(V.w().tensor_tensor(SM[:, 36:37], lb[:, 0:1], lb[:, 1:2], ALU.mult))
        t = V.do(V.w().tensor_tensor(SM[:, 37:38], lb[:, 2:3], lb[:, 3:4], ALU.mult))
        t = PE.do(mm(PE.w(t) and PB[:, 3, 0:2], ONE_128[:, :], SM[:, 36:38], True, True))
        t = S.do(S.w(t).activation(SM[:, 38:40], PB[:, 3, 0:2], ACT.Exp, scale=128.0))
        t = V.do(V.w(t).tensor_tensor(SM[:, 40:41], SM[:, 38:39], SM[:, 39:40], ALU.subtract))
        t_lam = V.do(V.w(t).tensor_scalar(LAM, SM[:, 40:41], LAM_INIT, None, ALU.add))
        t_gn = V.do(V.w().tensor_scalar(GN, pr("subln", 0, 2), 1.0 - LAM_INIT, None, ALU.mult))

        v_marks = []

        def v_evac(dst, marks):
            def evac(gi, ps, done):
                j = len(marks)
                t = S.do(S.w(done).activation(dst[:, :, 512 * j:512 * j + 512], ps, ACT.Copy))
                marks.append(t)
                return t
            return evac

        gemm(["kv_w_v"] * 4, x, v_evac(VT, v_marks), row_major=True)

        def rotate(dst, ps, done, *free):
            t = S.do(S.w(done, *free).activation(dst, ps[:, :, :], ACT.Copy))
            yield t
            PE.w(t, st.get("rope"))
            for m in range(2):
                t_r = PE.do(mm(PB[0:32, m, :], CN[0:32, CONST["rope"][0]:CONST["rope"][1]],
                               dst[0:32, 2 * m:2 * m + 2, :], True, True))
            sw = PB[0:32, 0:2, :].rearrange("p a (b t) -> p (a b) t", t=T)

            def b32(ap):
                return ap[0:32, :].unsqueeze(1).broadcast_to([32, 4, T])

            t1 = V.do(V.w(t_r, t_sin, st.get("rope")).tensor_tensor(RT[0:32, :, :], sw, b32(SIN), ALU.mult))
            t2 = V.do(V.w(t_cos).tensor_tensor(dst[0:32, :, :], dst[0:32, :, :], b32(COS), ALU.mult))
            st["rope"] = V.do(V.w(t1, t2).tensor_tensor(dst[0:32, :, :], dst[0:32, :, :], RT[0:32, :, :], ALU.add))
            yield

        st = {}
        k_marks = {}

        def k_evac(gi, ps, done):
            j = st.setdefault("k", 0)
            st["k"] += 1
            gen = rotate(KA[:, 4 * j:4 * j + 4, :], ps, done)
            t = next(gen)
            background.append(gen)
            return t

        gemm(["kv_w_k"] * 4, x, k_evac)

        def scores(q, k, pair, scale, mask):
            (q0, k0), (q1, k1) = pair
            PE.w(st.get("ss"))
            for c, (a, b) in enumerate(pair):
                mm(PB[:, c, 0:256], q[:, a, 128:256], k[:, b, :], True, True)
                t = PE.do(mm(PB[:, c, 256:384], q[:, a, 0:128], k[:, b, 0:128], False, True))
            V.w(t, st.get("exp"))
            for c in range(2):
                t = V.do(nc.vector.scalar_tensor_tensor(SS[:, c, :], PB[:, c, 0:384], scale, mask, ALU.mult, ALU.add))
            st["ss"] = t
            V.w(t)
            V.do(nc.vector.tensor_reduce(SM[:, 0:2], SS[:, :, 0:256], AX.X, ALU.max, negate=True))
            t = V.do(nc.vector.tensor_reduce(SM[:, 2:4], SS[:, :, 256:384], AX.X, ALU.max, negate=True))
            return t

        def exps(mark, *free):
            S.w(mark, *free)
            for c in range(2):
                S.do(nc.scalar.activation(PP[:, c, 0:256], SS[:, c, 0:256], ACT.Exp, bias=SM[:, c:c + 1],
                                          accum_out=SM[:, 4 + c:5 + c]))
                t = S.do(nc.scalar.activation(PP[:, c, 256:384], SS[:, c, 256:384], ACT.Exp,
                                              bias=SM[:, 2 + c:3 + c], accum_out=SM[:, 6 + c:7 + c]))
            st["exp"] = t
            return t

        def turn(a, mark, *free):
            PE.w(mark, st.get("at"))
            PE.do(nc.tensor.transpose(PB[:, 2, 0:128], a[:, 256:384], cn("ident")))
            PE.do(nc.tensor.transpose(PB[:, 2, 128:256], a[:, 0:128], cn("ident")))
            t = PE.do(nc.tensor.transpose(PB[:, 2, 256:384], a[:, 128:256], cn("ident")))
            st["at"] = S.do(S.w(t, st.get("pv")).activation(AT, PB[:, 2, 0:384], ACT.Copy))
            return st["at"]

        def weighted(v, col, nv, at, mark):
            PE.w(mark, st.get("of"))
            for e in range(nv):
                c = slice(col + 128 * e, col + 128 * e + 128)
                mm(PB[:, 3, T * e:T * e + T], v[:, 0, c], at[:, 0:256], e == 0, False)
                t = PE.do(mm(PB[:, 3, T * e + 128:T * e + T], v[:, 1, c], at[:, 256:384], False, True))
            st["pv"] = t
            return t

        def head_norm(nv, mark, ones, eps, bank):
            o = PB[:, 3, 0:nv * T].rearrange("p (a b) -> p a b", b=T)
            t_o = S.do(S.w(mark, st.get("ofu")).activation(OF[:, 0:nv, :], o, ACT.Copy))
            t_q = S.do(S.w(st.get("ms")).activation(OQ[:, 0:nv, :], o, ACT.Square))
            st["of"] = t_q
            yield
            PE.w(t_q, st.get("ln"))
            for e in range(nv):
                t = PE.do(mm(PB[:, bank, 0:T], ones[:, :], OQ[:, e, :], e == 0, e == nv - 1))
            st["ms"] = t
            t = S.do(S.w(t, st.get("ofu")).activation(STAT[:, 2, :], PB[:, bank, 0:T], ACT.Ln, bias=cn(eps)))
            st["ln"] = t
            t = S.do(S.w(t).activation(STAT[:, 2, :], STAT[:, 2, :], ACT.Exp, scale=-0.5))
            st["rms"] = (t, t_o)
            yield

        y_marks = [None] * NT

        def diff_head(h, Q, first):
            t = scores(Q, KA, ((first, 2 * h), (first + 1, 2 * h + 1)), 128.0 ** -0.5, cn("mask"))
            st["q"] = PE.now()
            yield
            t = exps(t, st.get("aa"))
            t = V.do(V.w(t).reciprocal(SM[:, 8:12], SM[:, 4:8]))
            t = V.do(V.w(t, t_lam).tensor_scalar(SM[:, 12:16], SM[:, 8:12], LAM, -1.0, ALU.mult, ALU.mult))
            V.w(t, st.get("tr"))
            for sl, b in ((slice(0, 256), 0), (slice(256, 384), 2)):
                t = V.do(nc.vector.tensor_scalar(AA[:, 0, sl], PP[:, 0, sl], SM[:, 8 + b:9 + b], None, ALU.mult))
            V.w(t)
            for sl, b in ((slice(0, 256), 0), (slice(256, 384), 2)):
                t = V.do(nc.vector.scalar_tensor_tensor(AA[:, 0, sl], PP[:, 1, sl], SM[:, 13 + b:14 + b],
                                                        AA[:, 0, sl], ALU.mult, ALU.add))
            st["aa"] = t
            yield
            t = turn(AA[:, 0, :], t)
            st["tr"] = PE.now()
            yield
            t = weighted(VT, 256 * h, 2, AT, t)
            yield from head_norm(2, t, ONE_256, "eps5", 2)
            V.w(*st["rms"])
            V.w(st["rms"][1], t_gn)
            for e in range(2):
                t = V.do(nc.vector.scalar_tensor_tensor(OF[:, e, :], OF[:, e, :], GN[:, e:e + 1], STAT[:, 2, :],
                                                        ALU.mult, ALU.mult))
            st["at"] = st["ln"]
            st["ofu"] = split_x(YH[:, 2 * h:2 * h + 2, :], YL[:, 2 * h:2 * h + 2, :], OF, t)
            y_marks[2 * h] = y_marks[2 * h + 1] = st["ofu"]
            yield

        def q_evac(gi, ps, done):
            j = st.setdefault("qn", 0)
            st["qn"] += 1
            while j >= 2 and ("q", j - 2) not in st:
                step()
            gen = rotate(QA[j % 2], ps, done, st.get(("q", j - 2)))
            t = next(gen)

            def heads():
                yield from gen
                PE.w(st["rope"], *v_marks)
                yield from diff_head(2 * j, QA[j % 2], 0)
                yield from diff_head(2 * j + 1, QA[j % 2], 2)
                st[("q", j)] = st["q"]

            background.append(heads())
            return t

        gemm(["b_w_q"] * 4, x, q_evac)
        drain()
        gemm(["b_w_o"] * 4, (YH, YL, y_marks), residual(ALPHA))
        x = layer_norm(2, SQB)
        x = ffn(1, x)

        def gla_heads(H, nv, q, k, b, v, ones, weight, dst, E, KT, MS, RED):
            for h in range(H):
                bb = b[:, h, :]
                V.w(st.get("e_used"), st.get("k_used"))
                for l in range(1, 8):
                    w = 2 ** l
                    src = bb.rearrange("p (n w) -> p n w", w=w)
                    mid = src[:, :, w // 2 - 1:w // 2].broadcast_to([128, T // w, w])
                    t = V.do(nc.vector.tensor_tensor(E[:, l - 1, :].rearrange("p (n w) -> p n w", w=w), src, mid,
                                                     ALU.subtract))
                V.do(nc.vector.tensor_scalar(E[:, 7, 0:128], bb[:, 0:128], bb[:, 127:128], None, ALU.subtract))
                t = V.do(nc.vector.tensor_copy(E[:, 7, 128:256], bb[:, 128:256]))
                t = S.do(S.w(t, V.now()).activation(E, E, ACT.Abs))
                t = S.do(S.w(t).activation(E, E, ACT.Exp, scale=-1.0))
                t_k = G.do(G.w(t, st.get("k_used")).tensor_tensor(KT, E, bc(k[:, h, :], 8), ALU.mult))
                t_q = V.do(V.w(t, t_k).tensor_tensor(E, E, bc(q[:, h, :], 8), ALU.mult))
                yield
                for m in range(2):
                    c = slice(128 * m, 128 * m + 128)
                    PE.w(t_q, t_k, st.get("ms_read"))
                    for l in range(8):
                        lhs, rhs = (k[:, h, c], q[:, h, c]) if l == 0 else (KT[:, l - 1, c], E[:, l - 1, c])
                        last = mm(PB[:, l // 4, 128 * (l % 4):128 * (l % 4) + 128], lhs, rhs, l % 4 == 0, True)
                    t = PE.do(last)
                    t = V.do(V.w(t, st.get("red")).tensor_tensor(
                        MS, PB[:, 0:2, :].rearrange("p a b -> p (a b)"), cn("lmask"), ALU.mult))
                    st["ms_read"] = t
                    V.w(t, st.get("pv"))
                    t = V.do(nc.vector.tensor_reduce(RED[:, 256 * m:256 * m + 128],
                                                     MS.rearrange("p (l t) -> p t l", l=8), AX.X, ALU.add))
                    st["red"] = t
                    yield
                PE.w(st.get("cross"), st.get("ln"))
                last = PE.do(mm(PB[:, 2, 0:128], KT[:, 7, 0:128], E[:, 7, 128:256], True, True))
                st["e_used"] = st["k_used"] = last
                t_x = S.do(S.w(last, st.get("pv")).activation(RED[:, 128:256], PB[:, 2, 0:128], ACT.Copy))
                st["cross"] = t_x
                PE.w(t_x)
                t = weighted(v, 128 * nv * h, nv, RED, t)
                yield
                st["ln"] = t_x
                yield from head_norm(nv, t, ones, "eps6", 2)
                V.w(*st["rms"])
                for e in range(nv):
                    t = V.do(nc.vector.scalar_tensor_tensor(dst[:, nv * h + e, :], OF[:, e, :], weight(nv * h + e),
                                                            STAT[:, 2, :], ALU.mult, ALU.mult))
                st["ofu"] = t
                st["y"] = t
                yield

        barrier()
        st = {}
        VA = scr(0, 2, 1024)
        KA = scr(2048, 8, T)
        QD = scr(4096, 8, T)
        E1 = scr(0, 8, T)
        KT1 = scr(2048, 8, T)
        MS = scr(4096, 1024)
        RED = scr(5120, 384)
        LG = scr(6144, 4, T)
        KB = scr(7168, 4, T)
        QB = scr(8192, 4, T)
        BB = scr(9216, 4, T)
        VB = scr(10240, 2, 1024)
        YR = scr(12288, 16, T)
        GT = scr(16384, 16, T)
        W0 = 20480
        SS = scr(W0, 2, 384)
        PP = scr(W0 + 768, 2, 384)
        AT = scr(W0 + 1536, 384)
        OF = scr(W0 + 1920, 2, T)
        OQ = scr(W0, 2, T)
        SM = scr(W0 + 2432, 64)
        AA = PP
        SQC = [scr(6144, 4, T), scr(7168, 4, T)]
        x = rms_norm(lambda k: pr("norm", k), SQC)
        barrier()

        def keep(dst, per, scale=1.0, marks=None):
            at = [0]

            def evac(gi, ps, done):
                j = at[0]
                at[0] += 1
                t = S.do(S.w(done).activation(dst[:, 4 * j:4 * j + 4, :], ps[:, :, :], ACT.Copy, scale=scale))
                if marks is not None:
                    marks.append(t)
                return t
            return evac

        va_marks, a_marks = [], []
        gemm(["va"] * 2, x, v_evac(VA, va_marks), row_major=True)
        gemm(["ka"] * 2, x, keep(KA, 4, marks=a_marks))
        gemm(["qa"] * 2, x, keep(QD, 4, marks=a_marks))

        def dilated():
            PE.w(*va_marks, *a_marks)
            for h in range(0, 8, 2):
                t = scores(QD, KA, ((h, h), (h + 1, h + 1)), 128.0 ** -0.5, cn("dmask"))
                yield
                t = exps(t, st.get("tr"))
                t = V.do(V.w(t).tensor_tensor(PP, PP, bc(cn("dcount"), 2), ALU.mult))
                V.w(t)
                V.do(nc.vector.tensor_reduce(SM[:, 8:10], PP[:, :, 0:256], AX.X, ALU.add))
                t = V.do(nc.vector.tensor_reduce(SM[:, 10:12], PP[:, :, 256:384], AX.X, ALU.add))
                t = V.do(V.w(t).reciprocal(SM[:, 12:16], SM[:, 8:12]))
                V.w(t)
                for c in range(2):
                    V.do(nc.vector.tensor_scalar(PP[:, c, 0:256], PP[:, c, 0:256], SM[:, 12 + c:13 + c], None,
                                                 ALU.mult))
                    t = V.do(nc.vector.tensor_scalar(PP[:, c, 256:384], PP[:, c, 256:384], SM[:, 14 + c:15 + c],
                                                     None, ALU.mult))
                yield
                t_w = t
                for c in range(2):
                    t = turn(PP[:, c, :], t_w)
                    st["tr"] = PE.now()
                    yield
                    t = weighted(VA, 128 * (h + c), 1, AT, t)
                    st["of"] = S.do(S.w(t).activation(YR[:, h + c, :], PB[:, 3, 0:T], ACT.Copy))
                    yield

        background.append(dilated())
        b_marks = []
        gemm(["kb"], x, keep(KB, 4, marks=b_marks))
        gemm(["qb"], x, keep(QB, 4, 128.0 ** -0.5, marks=b_marks))
        vb_marks = []
        gemm(["vb"] * 2, x, v_evac(VB, vb_marks), row_major=True)
        drain()
        barrier()
        GW = scr(5504, 512)
        GL = scr(W0 + 768, T)
        d_gw = Queue(None, sem("d_gw"))
        t_gw = dma(d_gw, GW[0:16, :], A["gla_w_gate"])

        def low(gi, ps, done):
            st["gl"] = S.do(S.w(done).activation(GL[0:16, :], ps[0:16, 0, :], ACT.Copy))
            return st["gl"]

        gemm(["glow"], x, low)

        def gla():
            PE.w(t_gw, st["gl"])
            for n in range(4):
                t = PE.do(mm(PB[:, n // 2, T * (n % 2):T * (n % 2) + T], GW[0:16, 128 * n:128 * n + 128], GL[0:16, :],
                             n % 2 == 0, True))
            V.w(t)
            for n in range(4):
                t = V.do(nc.vector.tensor_scalar(LG[:, n, :], PB[:, n // 2, T * (n % 2):T * (n % 2) + T],
                                                 pr("gla_b", n), None, ALU.add))
            st["ms_read"] = t
            t_a = S.do(S.w(t).activation(BB, LG, ACT.Abs))
            t_m = V.do(V.w(t_a).tensor_scalar(LG, LG, 0.0, 1.0 / 16, ALU.min, ALU.mult))
            t = S.do(S.w(t_a).activation(BB, BB, ACT.Exp, scale=-1.0))
            t = S.do(S.w(t).activation(BB, BB, ACT.Ln, bias=cn("one")))
            t = V.do(V.w(t, t_m).scalar_tensor_tensor(LG, BB, -1.0 / 16, LG, ALU.mult, ALU.add))
            yield
            t = scan(BB, LG, 4, E1, t)
            PE.w(*vb_marks, *b_marks)
            V.w(t, *b_marks)
            G.w(*b_marks)
            yield from gla_heads(4, 2, QB, KB, BB, VB, ONE_256, lambda n: pr("gla_norm", n), YR[:, 8:16, :],
                                 E1, KT1, MS, RED)

        def scan(dst, src, H, tmp, mark):
            n = H * T
            ones = tmp[:, 0:H, :].rearrange("p h t -> p (h t)")
            t = G.do(G.w(mark).memset(ones, 1.0))
            t = G.do(G.w(t).memset(ones.rearrange("p (m w) -> p m w", w=128)[:, :, 0:1], 0.0))
            return V.do(V.w(t, mark).tensor_tensor_scan(dst.rearrange("p h t -> p (h t)"), ones,
                                                        src.rearrange("p h t -> p (h t)"), 0.0, ALU.mult, ALU.add))

        background.append(gla())
        g_marks = []

        def gate(gi, ps, done):
            j = len(g_marks)
            t = S.do(S.w(done).activation(GT[:, 4 * j:4 * j + 4, :], ps[:, :, :], ACT.Silu))
            g_marks.append(t)
            return t

        def gated(order=(0, 1, 2, 3)):
            marks = [None] * NT
            for g in order:
                y = YR[:, 4 * g:4 * g + 4, :]
                t = V.do(V.w(g_marks[g], S.now(), V.now(), PE.now()).tensor_tensor(y, y, GT[:, 4 * g:4 * g + 4, :],
                                                                                   ALU.mult))
                t = split_x(XH[:, 4 * g:4 * g + 4, :], XL[:, 4 * g:4 * g + 4, :], y, t, PE.now())
                marks[4 * g:4 * g + 4] = [t] * 4
            return XH, XL, marks

        gemm(["gate"] * 4, x, gate)
        drain()
        x = gated()
        gemm(["o"] * 4, x, residual(None))

        barrier()
        st = {}
        YR = scr(0, 16, T)
        GT = scr(4096, 16, T)
        VI = scr(8192, 2, 1024)
        R0 = 10240
        BT = [scr(R0, 8, 128), scr(R0 + 1024, 8, 128)]
        CT = [scr(R0 + 2048, 32, 16), scr(R0 + 2560, 32, 16)]
        CP = [scr(R0 + 3072, 32, 16), scr(R0 + 3584, 32, 16)]
        CW = [scr(R0 + 4096, 640), scr(R0 + 4736, 640)]
        SP5 = scr(R0 + 5376, 16, 32)
        T1, T2, T3, ZR, ZI, VR, VJ, MG, CO, SI = (scr(R0 + 5888 + 512 * n, 2, T) for n in range(10))
        SQC = [scr(R0, 4, T), scr(R0 + 1024, 4, T)]
        x = rms_norm(lambda k: pr("norm", 16 + k), SQC)
        barrier()
        d_s5 = Queue(None, sem("d_s5"))
        for i, name in enumerate(("s5_bT_re", "s5_bT_im")):
            dma(d_s5, BT[i].rearrange("p a b -> p (a b)"), A[name])
        for i, name in enumerate(("s5_cT_re", "s5_cT_im")):
            t_s5 = dma(d_s5, CT[i].rearrange("p a b -> p (a b)"), A[name])
        G.do(G.w().memset(CW[0], 0.0))
        t_cw = G.do(G.w().memset(CW[1], 0.0))

        u_marks = []
        gemm(["u"] * 2, x, keep(YR, 4, marks=u_marks))

        def tt(out_, a, b, op, *marks):
            return V.do(V.w(*marks).tensor_tensor(out_, a, b, op))

        def s5():
            lr, li, ld = pr("lam_re", 0, 32), pr("lam_im", 0, 32), pr("log_dt", 0, 32)
            p = [SP5[:, n, :] for n in range(16)]
            dt, mag, ang, th, cs, sn, ar, ai, nr, inv, cr, ci, tmp, tmp2 = p[:14]
            t = S.do(S.w().activation(dt, ld, ACT.Exp))
            tt(ang, li, dt, ALU.mult, t)
            t = tt(tmp, lr, dt, ALU.mult)
            t_mag = S.do(S.w(t).activation(mag, tmp, ACT.Exp))
            t = reduce_angle(th, ang, tmp2, V.now())
            t_s, t_c = cos_sin(cs, sn, th, tmp2, t)
            t = tt(ar, mag, cs, ALU.mult, t_s, t_c, t_mag)
            t = tt(ai, mag, sn, ALU.mult)
            t = V.do(V.w(t).tensor_scalar(nr, ar, -1.0, None, ALU.add))
            t = tt(inv, lr, lr, ALU.mult)
            t = tt(tmp, li, li, ALU.mult, t_mag)
            t = tt(inv, inv, tmp, ALU.add, t)
            t = V.do(V.w(t).reciprocal(inv, inv))
            t = tt(cr, nr, lr, ALU.mult, t)
            t = tt(tmp, ai, li, ALU.mult, t)
            t = tt(cr, cr, tmp, ALU.add, t)
            t = tt(cr, cr, inv, ALU.mult, t)
            t = tt(ci, ai, lr, ALU.mult, t)
            t = tt(tmp, nr, li, ALU.mult, t)
            t = tt(ci, ci, tmp, ALU.subtract, t)
            t = tt(ci, ci, inv, ALU.mult, t)
            X = MG.rearrange("p a b -> p (a b)").rearrange("p (a b) -> p a b", b=16)
            t = tt(CP[0], CT[0], bcl(cr, 16), ALU.mult, t, t_s5)
            t = tt(X, CT[1], bcl(ci, 16), ALU.mult, t)
            t = tt(CP[0], CP[0], X, ALU.subtract, t)
            t = tt(CP[1], CT[0], bcl(ci, 16), ALU.mult, t)
            t = tt(X, CT[1], bcl(cr, 16), ALU.mult, t)
            t = tt(CP[1], CP[1], X, ALU.add, t)
            t = V.do(V.w(t).tensor_scalar(CP[1], CP[1], -1.0, None, ALU.mult))
            t_cp = t
            yield
            PE.w(t_s5, *u_marks)
            time = cn("time")
            t_y = None
            for n in range(16):
                j, i0 = n // 2, 2 * n
                if n % 2 == 0:
                    G.w(t_cp, t_cw, st.get("yb"))
                    for r in range(2):
                        for e in range(2):
                            dst = CW[r].rearrange("p (q s) -> p q s", s=160)[64 * e:64 * e + 64, :, 16 * e:16 * e + 16]
                            G.w(G.now())
                            t_w = G.do(nc.gpsimd.tensor_copy(dst, CP[r][64 * e:64 * e + 64, 4 * j:4 * j + 4, :]))
                PE.w(st.get("br"))
                for r in range(2):
                    for c in range(2):
                        q = (i0 + c) % 4
                        rows = slice(32 * q, 32 * q + 32)
                        t_b = PE.do(mm(PB[:, c, T * r:T * r + T], BT[r][rows, j, :], YR[rows, j, :], r == 0, True))
                V.w(V.now())
                for c in range(2):
                    t = V.do(nc.vector.tensor_scalar(T1[:, c, :], time, th[:, i0 + c:i0 + c + 1], None, ALU.mult))
                    S.w(t_mag, V.now())
                for c in range(2):
                    t_g = S.do(nc.scalar.activation(MG[:, c, :], time, ACT.Identity, scale=0.0,
                                                    bias=mag[:, i0 + c:i0 + c + 1]))
                t_g = G.do(G.w(t_g, G.now()).memset(MG[:, :, 0:1], 0.0))
                t = reduce_angle(T2, T1, T3, t)
                t_s, t_c = cos_sin(CO, SI, T2, T3, t)
                yield
                br = PB[:, 0:2, 0:T]
                bi = PB[:, 0:2, T:2 * T]
                V.w(t_b, t_s, t_c)
                V.do(nc.vector.tensor_tensor(VR, br, CO, ALU.mult))
                V.do(nc.vector.tensor_tensor(T1, bi, SI, ALU.mult))
                V.do(nc.vector.tensor_tensor(VJ, bi, CO, ALU.mult))
                t = V.do(nc.vector.tensor_tensor(T2, br, SI, ALU.mult))
                st["br"] = t
                V.w(t)
                V.do(nc.vector.tensor_tensor(VR, VR, T1, ALU.add))
                t = V.do(nc.vector.tensor_tensor(VJ, VJ, T2, ALU.subtract))
                V.w(t, t_g, st.get("yb"))

                def flat(a):
                    return a.rearrange("p a b -> p (a b)")

                V.do(nc.vector.tensor_tensor_scan(flat(ZR), flat(MG), flat(VR), 0.0, ALU.mult, ALU.add))
                t = V.do(nc.vector.tensor_tensor_scan(flat(ZI), flat(MG), flat(VJ), 0.0, ALU.mult, ALU.add))
                yield
                V.w(t)
                V.do(nc.vector.tensor_tensor(T1, ZR, CO, ALU.mult))
                V.do(nc.vector.tensor_tensor(T2, ZI, SI, ALU.mult))
                V.do(nc.vector.tensor_tensor(VR, ZR, SI, ALU.mult))
                t = V.do(nc.vector.tensor_tensor(VJ, ZI, CO, ALU.mult))
                V.w(t)
                V.do(nc.vector.tensor_tensor(ZR, T1, T2, ALU.subtract))
                t = V.do(nc.vector.tensor_tensor(ZI, VR, VJ, ALU.add))
                PE.w(t, t_w, t_y)
                for c in range(2):
                    q = (i0 + c) % 4
                    for r, z in enumerate((ZR, ZI)):
                        last = mm(PB[:, 2, 0:T], CW[r][:, 128 * q:128 * q + 128], z[:, c, :],
                                  q == 0 and r == 0, q == 3 and r == 1)
                st["yb"] = PE.do(last)
                if n % 2:
                    t = V.do(V.w(st["yb"], *u_marks).scalar_tensor_tensor(
                        YR[:, j, :], YR[:, j, :], pr("s5_d", j), PB[:, 2, 0:T], ALU.mult, ALU.add))
                    t_y = S.do(S.w(t).activation(YR[:, j, :], YR[:, j, :], ACT.Gelu_apprx_tanh))
                yield

        background.append(s5())
        g_marks = []
        gemm(["gate"] * 4, x, gate)
        vi_marks = []
        gemm(["idd"] * 2, x, v_evac(VI, vi_marks), row_major=True)
        drain()
        barrier()

        ms_free = st.get("br")
        st = {"of": None}
        KD = scr(R0, 8, T)
        BD = scr(R0 + 2048, 8, T)
        QH = scr(R0 + 4096, 8, T)
        E1 = scr(R0 + 6144, 8, T)
        KT1 = scr(R0 + 8192, 8, T)
        W0 = R0 + 10240
        MS = scr(W0, 1024)
        RED = scr(W0 + 1024, 384)
        OF = scr(W0 + 1408, 1, T)
        OQ = scr(W0 + 1664, 1, T)
        SM = scr(W0 + 1920, 32)
        LB, OM = SM[:, 0:8], SM[:, 8:16]
        gm = pr("gamma", 0, 16)
        t = tt(SM[:, 16:24], gm[:, 0:8], gm[:, 8:16], ALU.max)
        t = tt(LB, gm[:, 0:8], SM[:, 16:24], ALU.subtract, t)
        t = tt(OM, gm[:, 8:16], SM[:, 16:24], ALU.subtract, t)
        t = S.do(S.w(t).activation(SM[:, 0:16], SM[:, 0:16], ACT.Exp))
        t = tt(SM[:, 16:24], LB, OM, ALU.add, t)
        t = V.do(V.w(t).reciprocal(SM[:, 24:32], SM[:, 16:24]))
        t = tt(LB, LB, SM[:, 24:32], ALU.mult, t)
        t = tt(OM, OM, SM[:, 24:32], ALU.mult, t)
        t = tt(SM[:, 16:24], LB, OM, ALU.add, t)
        t = tt(LB, SM[:, 16:24], LB, ALU.subtract, t)
        t_lb = V.do(V.w(t).tensor_scalar(OM, LB, -1.0, 1.0, ALU.mult, ALU.add))
        f_marks = []

        def forget(gi, ps, done):
            j = len(f_marks)
            ff = E1[:, 4 * j:4 * j + 4, :]
            t_f = S.do(S.w(done).activation(ff, ps[:, :, :], ACT.Sigmoid))
            V.w(t_f, t_lb)
            for n in range(4):
                k = 4 * j + n
                t = V.do(nc.vector.tensor_scalar(E1[:, k, :], E1[:, k, :], OM[:, k:k + 1], LB[:, k:k + 1], ALU.mult,
                                                 ALU.add))
            V.do(V.w(t).tensor_scalar(KD[:, 4 * j:4 * j + 4, :], ff, -1.0, 1.0, ALU.mult, ALU.add))
            f_marks.append(S.do(S.w(t).activation(QH[:, 4 * j:4 * j + 4, :], ff, ACT.Ln)))
            return t_f

        gemm(["fd"] * 2, x, forget)
        t_scan = scan(BD, QH, 8, E1, V.now() if V.w(f_marks[1]) and G.w(f_marks[1]) else None)
        q_marks = []

        def query(gi, ps, done):
            j = len(q_marks)
            t = S.do(S.w(done, t_scan).activation(QH[:, 4 * j:4 * j + 4, :], ps[:, :, :], ACT.Silu))
            q_marks.append(t)
            return t

        gemm(["qd"] * 2, x, query)
        marks = []
        for g in range(2):
            t = split_x(XH[:, 4 * g:4 * g + 4, :], XL[:, 4 * g:4 * g + 4, :], YR[:, 4 * g:4 * g + 4, :], PE.now())
            marks += [t] * 4

        def hgrn():
            PE.w(*vi_marks, *q_marks)
            V.w(t_scan, *q_marks)
            G.w(t_scan, *q_marks)
            yield from gla_heads(8, 1, QH, KD, BD, VI, ONE_128, lambda n: pr("hgrn_norm", n), YR[:, 8:16, :],
                                 E1, KT1, MS, RED)

        background.append(hgrn())
        glu_marks = []

        def glu(gi, ps, done):
            j = len(glu_marks) // 2
            for n in range(0, 4, 2):
                k = 4 * j + n
                S.w(done, glu_marks[-1] if glu_marks else None)
                for m in range(2):
                    t = S.do(nc.scalar.activation(SG[:, m, :], ps[:, n + m, :], ACT.Sigmoid,
                                                  bias=pr("b_glu", k + m)))
                glu_marks.append(tt(YR[:, k:k + 2, :], YR[:, k:k + 2, :], SG, ALU.mult, t))
            return t

        SG = scr(W0 + 1952, 2, T)
        gemm(["glu"] * 2, (XH, XL, marks), glu)
        drain()
        x = gated()
        gemm(["o"] * 4, x, residual(None))
        barrier()
        out_v = out.rearrange("(t p) n -> p t n", p=128)

        def store(g, t):
            dma(d_out, out_v[:, 4 * g:4 * g + 4, :], XA[:, 4 * g:4 * g + 4, :], t)

        rms_norm(lambda k: pr("final", k), [scr(0, 4, T), scr(1024, 4, T)], store)
        SP.w(d_out.now())


def feature_tiles(a):
    a = np.asarray(a)
    return np.ascontiguousarray(a.reshape(-1, a.shape[-1] // 128, 128).transpose(2, 0, 1)).reshape(128, -1)


def state_tiles(a):
    return np.ascontiguousarray(np.asarray(a).reshape(32, 128).T)


def kernel(**inputs):
    import concourse.bacc as bacc
    from concourse.bass_utils import run_bass_kernel_spmd

    a = {k: np.asarray(v) for k, v in inputs.items()}
    packed = {
        "ln_g": feature_tiles(a["ln_g"].reshape(4, D)), "ln_b": feature_tiles(a["ln_b"].reshape(4, D)),
        "a_conv": feature_tiles(a["a_conv_w"][0]), "f_conv": feature_tiles(a["ffn_conv_w"].reshape(6, 2 * DFF)),
        "f_bias": feature_tiles(a["ffn_conv_b"]), "subln": feature_tiles(a["b_subln_g"]),
        "norm": feature_tiles(a["norm_g_2"]), "final": feature_tiles(a["final_g_2"].reshape(1, D)),
        "gla_b": feature_tiles(a["gla_b_gate_2"]), "gla_norm": feature_tiles(a["gla_norm_g_2"]),
        "lam_re": state_tiles(a["s5_lam_re_2"][0]), "lam_im": state_tiles(a["s5_lam_im_2"][0]),
        "log_dt": state_tiles(np.repeat(a["s5_log_dt_2"][0][:, None], 64, 1)),
        "s5_d": feature_tiles(a["s5_d_2"].reshape(1, 1024)), "b_glu": feature_tiles(a["s5_b_glu_2"]),
        "gamma": feature_tiles(a["hgrn_gamma_2"]), "hgrn_norm": feature_tiles(a["hgrn_norm_g_2"]),
        "b_lambda": feature_tiles(a["b_lambda"][0]),
    }
    params = np.zeros((128, NPARAM), np.float32)
    for name, (lo, hi) in PARAM.items():
        params[:, lo:hi] = packed[name]

    def b_tiles(b):
        b = b[0].reshape(8, 4, 2, 64, 16)
        o = np.zeros((4, 2, 16, 8, 2, 64), np.float32)
        for e in range(2):
            o[:, e, :, :, e, :] = b[:, :, e].transpose(1, 3, 0, 2)
        return o.reshape(128, 1024)

    def c_tiles(c):
        return np.ascontiguousarray(c[0].reshape(32, 2, 16, 64).transpose(1, 3, 0, 2)).reshape(128, 512)

    arrays = {
        "consts": constants(), "params": params, "xT": np.ascontiguousarray(a["x"][0].T),
        "positions": np.ascontiguousarray(a["positions"][0]),
        "a_w_in": a["a_w_in"][0], "a_w_out": a["a_w_out"][0], "kv_w_k": a["kv_w_k"], "kv_w_v": a["kv_w_v"],
        "b_w_q": a["b_w_q"][0], "b_w_o": a["b_w_o"][0], "ffn_w_up": a["ffn_w_up"], "ffn_w_down": a["ffn_w_down"],
        "ab_w_in": a["ab_w_in_2"][0], "gla_w_gate": a["gla_w_gate_2"][0], "ab_w_out": a["ab_w_out_2"][0],
        "cd_w_in": a["cd_w_in_2"][0], "s5_w_glu": a["s5_w_glu_2"][0], "cd_w_out": a["cd_w_out_2"][0],
        "s5_bT_re": b_tiles(a["s5_b_re_2"]), "s5_bT_im": b_tiles(a["s5_b_im_2"]),
        "s5_cT_re": c_tiles(a["s5_c_re_2"]), "s5_cT_im": c_tiles(a["s5_c_im_2"]),
    }
    nc = bacc.Bacc("TRN2", target_bir_lowering=False, num_devices=1)
    ins = {n: nc.dram_tensor(n, v.shape, mybir.dt.from_np(v.dtype), kind="ExternalInput").ap()
           for n, v in arrays.items()}
    out = nc.dram_tensor("out", (D, T), F32, kind="ExternalOutput").ap()
    two_block_model(nc, ins, out)
    r = run_bass_kernel_spmd(nc, [arrays], core_ids=[0])
    return np.ascontiguousarray(r.results[0]["out"].T)[None]
```

```python
import math
from collections import deque
from contextlib import ExitStack

import numpy as np

import concourse.bass as bass
from concourse import mybir

F32 = mybir.dt.float32
BF16 = mybir.dt.bfloat16
I32 = mybir.dt.int32
ALU = mybir.AluOpType
ACT = mybir.ActivationFunctionType
AX = mybir.AxisListType

D = 2048
T = 256
NT = D // 128
DFF = 5632
NF = DFF // 128
ALPHA = 4.0 ** 0.25
LAM_INIT = 0.8 - 0.6 * math.exp(-0.3)
NEG = -1e30
RF = 4
RB = 4
LA = 3

MAGIC = 12582912.0
TWO_PI = 2.0 * math.pi
C1 = 6.28125
C2 = float(np.float32(np.round((TWO_PI - C1) * 2.0 ** 21) / 2.0 ** 21))
C3 = float(np.float32(TWO_PI - C1 - C2))
PI_CLAMP = 3.1415925


def columns(spec):
    at, out = 0, {}
    for name, n in spec:
        out[name] = (at, at + n)
        at += n
    return out, at


CONST, NCONST = columns([("ident", 128), ("rope", 32), ("freq", 1), ("eps5", 1), ("eps6", 1), ("one", 1),
                         ("halfpi", 1), ("zero", 1), ("mask", 384), ("dmask", 384), ("dcount", 384),
                         ("lmask", 1024), ("time", 256)])
PARAM, NPARAM = columns([("ln_g", 64), ("ln_b", 64), ("a_conv", 48), ("f_conv", 528), ("f_bias", 176),
                         ("subln", 2), ("norm", 32), ("final", 16), ("gla_b", 4), ("gla_norm", 8),
                         ("lam_re", 32), ("lam_im", 32), ("log_dt", 32), ("s5_d", 8), ("b_glu", 8),
                         ("gamma", 16), ("hgrn_norm", 8), ("b_lambda", 4)])


def constants():
    c = np.zeros((128, NCONST), np.float32)

    def put(name, v):
        a, b = CONST[name]
        c[:, a:b] = v

    put("ident", np.eye(128))
    rope = np.zeros((128, 32))
    for i in range(16):
        rope[i + 16, i] = -1.0
        rope[i, i + 16] = 1.0
    put("rope", rope)
    freq = np.float32(500000.0) ** (-np.arange(0, 32, 2, dtype=np.float32) / np.float32(32))
    col = np.zeros((128, 1))
    col[0:16, 0] = freq
    col[16:32, 0] = freq
    put("freq", col)
    put("eps5", 1e-5)
    put("eps6", 1e-6)
    put("one", 1.0)
    put("halfpi", math.pi / 2)
    i = np.arange(128)[:, None]
    j = np.arange(128)[None, :]
    tri = np.where(j <= i, 0.0, NEG)
    put("mask", np.concatenate([np.zeros((128, 128)), tri, tri], 1))
    d = np.concatenate([128 + i - j, i - j, i - j], 1)
    count = (d >= 0) * ((d <= 128).astype(int) + (d % 4 == 0) + (d % 16 == 0))
    put("dmask", np.where(count > 0, 0.0, NEG))
    put("dcount", count)
    lm = np.zeros((128, 8, 128))
    lm[:, 0, :] = i == j
    for l in range(1, 8):
        h = 2 ** (l - 1)
        lm[:, l, :] = (i // (2 * h) == j // (2 * h)) & (i % (2 * h) < h) & (j % (2 * h) >= h)
    put("lmask", lm.reshape(128, 1024))
    put("time", np.arange(256)[None, :])
    return c


class Queue:

    def __init__(self, eng, sem):
        self.eng, self.sem, self.n, self.seen = eng, sem, 0, {}

    def w(self, *marks):
        for m in marks:
            if m is None:
                continue
            q, v = m
            if self.seen.get(id(q), 0) < v:
                self.eng.wait_ge(q.sem, v)
                self.seen[id(q)] = v
        return self.eng

    def do(self, ins, by=1):
        ins.then_inc(self.sem, by)
        self.n += by
        return self, self.n

    def now(self):
        return (self, self.n) if self.n else None


def two_block_model(nc, A, out):
    ctx = ExitStack()
    with ctx:
        def sb(name, shape, dt=F32):
            return ctx.enter_context(nc.sbuf_tensor(name, shape, dt))

        def sem(name):
            return ctx.enter_context(nc.semaphore(name))

        XA = sb("XA", [128, NT, T])
        XH = sb("XH", [128, NT, T], BF16)
        XL = sb("XL", [128, NT, T], BF16)
        WF = sb("WF", [128, RF, 4, 512])
        WH = sb("WH", [128, RB, 4, 512], BF16)
        WL = sb("WL", [128, RB, 4, 512], BF16)
        CN = sb("CN", [128, NCONST])
        PR = sb("PR", [128, NPARAM])
        ONE_D = sb("ONE_D", [128, 128])
        ONE_256 = sb("ONE_256", [128, 128])
        ONE_128 = sb("ONE_128", [128, 128])
        SCR = sb("SCR", [128, 23040])
        STAT = sb("STAT", [128, 4, T])
        MAG = sb("MAG", [128, 32])
        PSG = [ctx.enter_context(nc.psum_tensor(f"PSG{i}", [128, 4, T], F32)) for i in range(2)]
        PB = ctx.enter_context(nc.psum_tensor("PB", [128, 4, 512], F32))

        PE = Queue(nc.tensor, sem("s_pe"))
        V = Queue(nc.vector, sem("s_v"))
        S = Queue(nc.scalar, sem("s_s"))
        G = Queue(nc.gpsimd, sem("s_g"))
        SP = Queue(nc.sync, sem("s_sp"))
        d_in = Queue(None, sem("d_in"))
        d_w = [Queue(None, sem(f"d_w{i}")) for i in range(RF)]
        d_out = [Queue(None, sem(f"d_out{i}")) for i in range(2)]

        def dma(q, dst, src, *marks):
            return q.do(SP.w(*marks).dma_start(dst, src), 16)

        def cn(name, a=0, n=None):
            lo, hi = CONST[name]
            return CN[:, lo + a:hi if n is None else lo + a + n]

        def pr(name, a=0, n=1):
            lo = PARAM[name][0]
            return PR[:, lo + a:lo + a + n]

        def bc(ap, n):
            return ap.unsqueeze(1).broadcast_to([128, n, ap.shape[-1]])

        def bcl(ap, n):
            return ap.unsqueeze(2).broadcast_to([ap.shape[0], ap.shape[1], n])

        def scr(at, *shape, dt=F32):
            n = int(np.prod(shape))
            words = n if dt == F32 else n // 2
            v = SCR[:, at:at + words]
            if dt != F32:
                v = v.bitcast(dt)
            if len(shape) == 2:
                v = v.rearrange("p (a b) -> p a b", b=shape[1])
            if len(shape) == 3:
                v = v.rearrange("p (a b c) -> p a b c", b=shape[1], c=shape[2])
            return v

        def barrier():
            drain()
            marks = [q.now() for q in (PE, V, S, G)]
            for q in (PE, V, S, G, SP):
                q.w(*[m for m in marks if m and m[0] is not q])
                if q.now() and q in (V, S, G):
                    q.w(q.now())

        background = deque()

        def step():
            while background:
                try:
                    next(background[0])
                    return
                except StopIteration:
                    background.popleft()

        def drain():
            while background:
                step()

        t_cn = dma(d_in, CN[:, :], A["consts"])
        t_cn = dma(d_in, PR[:, :], A["params"])
        t_in = dma(d_in, XA[:, :, :], A["xT"].rearrange("(t p) n -> p t n", p=128))
        G.do(G.w().memset(ONE_D[:, :], 1.0 / D))
        G.do(G.w().memset(ONE_256[:, :], 1.0 / 256))
        t_one = G.do(G.w().memset(ONE_128[:, :], 1.0 / 128))
        for q in (PE, V, S, G):
            q.w(t_in, t_one)

        groups = []

        def add(w, col, width, rows, tag):
            groups.append(dict(w=w, col=col, width=width, rows=list(rows), tag=tag))

        def whole(K):
            return range(0, K, 512)

        for j in range(4):
            for part, tag in ((1, "b"), (2, "c"), (0, "a")):
                add(A["a_w_in"], part * D + j * 512, 512, whole(D), tag)
        for j in range(4):
            add(A["a_w_out"], j * 512, 512, whole(D), "o")

        def add_ffn(l):
            for j in range(11):
                add(A["ffn_w_up"][l], j * 512, 512, whole(D), "g")
                add(A["ffn_w_up"][l], DFF + j * 512, 512, whole(D), "u")
            for j in range(4):
                add(A["ffn_w_down"][l], j * 512, 512, whole(DFF), "down")

        add_ffn(0)
        for j in range(4):
            add(A["kv_w_k"], j * 512, 512, whole(D), "k")
            add(A["b_w_q"], j * 512, 512, whole(D), "q")
        for j in range(4):
            add(A["kv_w_v"], j * 512, 512, whole(D), "v")
        for j in range(4):
            add(A["b_w_o"], j * 512, 512, whole(D), "o")
        add_ffn(1)
        for tag, col, n in [("kb", 3584, 1), ("qb", 3072, 1), ("glow", 5120, 1), ("vb", 4096, 2), ("va", 2048, 2),
                            ("ka", 1024, 2), ("qa", 0, 2)]:
            for j in range(n):
                if tag == "glow":
                    add(A["ab_w_in"], col, 16, [0], tag)
                else:
                    add(A["ab_w_in"], col + 512 * j, 512, whole(D), tag)
        for j in (2, 3, 0, 1):
            add(A["ab_w_in"], 5136 + 512 * j, 512, whole(D), "gate")
        for j in range(4):
            add(A["ab_w_out"], j * 512, 512, (1024, 1536, 0, 512), "o")
        for tag, col, n in [("u", 0, 2), ("fd", 2048, 2), ("qd", 1024, 2), ("idd", 3072, 2)]:
            for j in range(n):
                add(A["cd_w_in"], col + 512 * j, 512, whole(D), tag)
        for j in (2, 3, 0, 1):
            add(A["cd_w_in"], 4096 + 512 * j, 512, whole(D), "gate")
        for j in range(2):
            add(A["s5_w_glu"], j * 512, 512, whole(1024), "glu")
        for half in (0, 1024):
            for j in range(4):
                add(A["cd_w_out"], j * 512, 512, (half, half + 512), "o")

        chunks = []
        for g in groups:
            g["first"] = len(chunks)
            for k0 in g["rows"]:
                chunks.append((g, k0, 512 if g["width"] == 512 else D))

        def shaped(ring, i, rows, width):
            if width == 512:
                return ring[:, i, :, :]
            n = rows // 128 * width
            return ring[:, i, 0, 0:n].rearrange("p (t n) -> p t n", n=width)

        t_load, t_split, t_used = {}, {}, {}

        def load(i):
            if i >= len(chunks) or i in t_load:
                return
            g, k0, rows = chunks[i]
            src = g["w"][k0:k0 + rows, g["col"]:g["col"] + g["width"]].rearrange("(t p) n -> p t n", p=128)
            before = t_split.get(i - RF, (None, None))
            t_load[i] = dma(d_w[i % RF], shaped(WF, i % RF, rows, g["width"]), src, *before)

        def split(i):
            if i >= len(chunks) or i in t_split:
                return
            load(i)
            g, k0, rows = chunks[i]
            w, h, l = (shaped(r, i % n, rows, g["width"]) for r, n in ((WF, RF), (WH, RB), (WL, RB)))
            free = t_used.get(i - RB)
            t_h = S.do(S.w(t_load[i], free).activation(h, w, ACT.Copy))
            t_l = V.do(V.w(t_load[i], t_h, free).tensor_tensor(l, w, h, ALU.subtract))
            t_split[i] = (t_h, t_l)
            load(i + RF)

        for i in range(RF):
            load(i)

        state = dict(g=0, free=[None, None], rate=1)

        def gemm(tags, x, evac, row_major=False):
            xh, xl, xt = x
            for tag in tags:
                gi = state["g"]
                g = groups[gi]
                assert g["tag"] == tag, (g["tag"], tag)
                state["g"] += 1
                ps = PSG[gi % 2]
                psr = ps[:, :, :].rearrange("p a b -> p (a b)").rearrange("p (t n) -> p t n", n=512)
                PE.w(state["free"][gi % 2])
                for c, k0 in enumerate(g["rows"]):
                    i = g["first"] + c
                    for ahead in range(LA + 1):
                        if ahead == 0 or i + ahead - RB in t_used or i + ahead < RB:
                            split(i + ahead)
                    rows = chunks[i][2]
                    h, l = (shaped(r, i % RB, rows, g["width"]) for r in (WH, WL))
                    PE.w(*t_split[i])
                    nk = rows // 128
                    for kk in range(nk):
                        k = k0 // 128 + kk
                        while xt[k] is None:
                            step()
                        PE.w(xt[k])
                        st = c == 0 and kk == 0
                        sp = c == len(g["rows"]) - 1 and kk == nk - 1
                        if g["width"] == 16:
                            for n, (a, b) in enumerate(((h, xh), (h, xl), (l, xh))):
                                last = nc.tensor.matmul(ps[0:16, 0, :], a[:, kk, :], b[:, k, :],
                                                        start=st and n == 0, stop=sp and n == 2,
                                                        skip_group_check=True)
                        elif row_major:
                            for m in range(2):
                                cs = slice(m * 128, m * 128 + 128)
                                for n, (a, b) in enumerate(((xh, h), (xh, l), (xl, h))):
                                    last = nc.tensor.matmul(psr[:, m, :], a[:, k, cs], b[:, kk, :],
                                                            start=st and n == 0, stop=sp and n == 2,
                                                            skip_group_check=True)
                        else:
                            for m in range(4):
                                cs = slice(m * 128, m * 128 + 128)
                                for n, (a, b) in enumerate(((h, xh), (h, xl), (l, xh))):
                                    last = nc.tensor.matmul(ps[:, m, :], a[:, kk, cs], b[:, k, :],
                                                            start=st and n == 0 and m % 2 == 0,
                                                            stop=sp and n == 2, skip_group_check=True)
                        if kk == 1 and state["rate"] > 1:
                            step()
                    t_used[i] = PE.do(last)
                    for _ in range(max(1, state["rate"] - 1)):
                        step()
                done = PE.now()
                state["free"][gi % 2] = evac(gi, psr if row_major else ps, done)

        def split_x(hi, lo, src, *marks):
            t_h = S.do(S.w(*marks).activation(hi, src, ACT.Copy))
            return V.do(V.w(t_h, *marks).tensor_tensor(lo, src, hi, ALU.subtract))

        def mm(o, lhsT, rhs, start, stop):
            return nc.tensor.matmul(o, lhsT, rhs, start=start, stop=stop, skip_group_check=True)

        def rstd(src, mark, eps, dst):
            t = S.do(S.w(mark).activation(dst, src, ACT.Sqrt, bias=cn(eps)))
            return V.do(V.w(t).reciprocal(dst, dst))

        def tiles(g):
            return XA[:, 4 * g:4 * g + 4, :]

        def sum_tiles(bank, src, marks, first, last):
            PE.w(*marks)
            for n in range(4):
                t = mm(PB[:, bank, 0:T], ONE_D[:, :], src[:, n, :], first and n == 0, last and n == 3)
            return PE.do(t)

        def residual(scale, SQ, stats):
            at = [0]

            def evac(gi, ps, done):
                g = at[0]
                at[0] += 1
                x = tiles(g)
                if scale is None:
                    t = V.do(V.w(done).tensor_tensor(x, ps[:, :, :], x, ALU.add))
                else:
                    t = V.do(V.w(done).scalar_tensor_tensor(x, x, scale, ps[:, :, :], ALU.mult, ALU.add))
                if stats == "layer":
                    background.append(layer_stats(g, t))
                elif stats == "rms":
                    background.append(square(g, t))
                return t

            def square(g, t):
                t = S.do(S.w(t, state.get(("sq", g % 2))).activation(SQ[g % 2], tiles(g), ACT.Square))
                yield
                state[("sq", g % 2)] = state["squares"] = sum_tiles(1, SQ[g % 2], [t], g == 0, g == 3)
                yield

            def centre(g, t):
                return V.do(V.w(t).tensor_tensor(tiles(g), tiles(g), bc(STAT[:, 0, :], 4), ALU.subtract))

            def layer_stats(g, t):
                if g < 3:
                    t = sum_tiles(0, tiles(g), [t], g == 0, g == 2)
                    yield
                if g == 2:
                    t_c = S.do(S.w(t).activation(STAT[:, 0, :], PB[:, 0, 0:T], ACT.Copy, scale=4.0 / 3.0))
                    yield
                    for q in range(3):
                        t = centre(q, t_c)
                        yield
                        yield from square(q, t)
                if g == 3:
                    t = centre(3, t)
                    gen = square(3, t)
                    next(gen)
                    state["rest"] = sum_tiles(2, tiles(3), [t], True, True)
                    yield from gen

            return evac

        def layer_norm(which, SQ, squares=False):
            drain()
            m, r = STAT[:, 1, :], STAT[:, 2, :]
            t_m = S.do(S.w(state["rest"]).activation(m, PB[:, 2, 0:T], ACT.Copy))
            t_q = S.do(S.w(t_m).activation(r, m, ACT.Square))
            t = V.do(V.w(t_q, state["squares"]).tensor_tensor(r, PB[:, 1, 0:T], r, ALU.subtract))
            t_r = rstd(r, t, "eps5", r)
            marks = []
            t_sq = [None, None]
            for g in range(4):
                x = tiles(g)
                t = V.do(V.w(t_m).tensor_tensor(x, x, bc(m, 4), ALU.subtract))
                t = V.do(V.w(t, t_r).tensor_tensor(x, x, bc(r, 4), ALU.mult))
                V.w(t)
                for n in range(4):
                    k = 4 * g + n
                    t = V.do(nc.vector.tensor_scalar(XA[:, k, :], XA[:, k, :], pr("ln_g", 16 * which + k),
                                                     pr("ln_b", 16 * which + k), ALU.mult, ALU.add))
                if squares:
                    t = S.do(S.w(t, t_sq[g % 2]).activation(SQ[g % 2], x, ACT.Square))
                    t_sq[g % 2] = state["squares"] = sum_tiles(1, SQ[g % 2], [t], g == 0, g == 3)
                else:
                    t = split_x(XH[:, 4 * g:4 * g + 4, :], XL[:, 4 * g:4 * g + 4, :], x, t)
                    marks += [t] * 4
            return XH, XL, marks

        def rms_norm(weight, XN, store=None):
            drain()
            r = STAT[:, 3, :]
            t_r = rstd(PB[:, 1, 0:T], state["squares"], "eps6", r)
            marks = []
            free = [None, None]
            for g in range(4):
                V.w(t_r, free[g % 2])
                for n in range(4):
                    k = 4 * g + n
                    t = V.do(nc.vector.scalar_tensor_tensor(XN[g % 2][:, n, :], XA[:, k, :], weight(k), r,
                                                            ALU.mult, ALU.mult))
                if store:
                    free[g % 2] = store(g, XN[g % 2], t)
                else:
                    t = split_x(XH[:, 4 * g:4 * g + 4, :], XL[:, 4 * g:4 * g + 4, :], XN[g % 2], t)
                    free[g % 2] = t
                    marks += [t] * 4
            return XH, XL, marks

        marks = []
        for g in range(4):
            t = split_x(XH[:, 4 * g:4 * g + 4, :], XL[:, 4 * g:4 * g + 4, :], XA[:, 4 * g:4 * g + 4, :])
            marks += [t] * 4
        x = (XH, XL, marks)

        YH = scr(0, NT, T, dt=BF16)
        YL = scr(2048, NT, T, dt=BF16)
        CB = scr(4096, 4, T)
        CX = scr(5120, 4, T + 2)
        CA = scr(6160, 4, T)
        YF = scr(7184, 4, T)
        y_marks = []
        st = {}
        t_pad = G.do(G.w().memset(CX[:, :, 0:2], 0.0))

        def mixer(gi, ps, done):
            tag = groups[gi]["tag"]
            j = gi // 3
            if tag == "b":
                st["c"] = S.do(S.w(done, st.get("cx")).activation(CB, ps[:, :, :], ACT.Copy))
                return st["c"]
            if tag == "c":
                st["cx"] = V.do(V.w(done, st["c"], st.get("conv"), t_pad).tensor_tensor(
                    CX[:, :, 2:T + 2], ps[:, :, :], CB, ALU.mult))
                return st["cx"]
            ts = []
            for n in range(4):
                V.w(st["cx"], st.get("yf"))
                ts.append(V.do(nc.vector.tensor_scalar(CA[:, n, :], CX[:, n, 0:T], pr("a_conv", 4 * j + n), None,
                                                       ALU.mult)))
            for tap in (1, 2):
                for n in range(4):
                    V.w(ts[n])
                    ts[n] = V.do(nc.vector.scalar_tensor_tensor(
                        CA[:, n, :], CX[:, n, tap:tap + T], pr("a_conv", 16 * tap + 4 * j + n), CA[:, n, :],
                        ALU.mult, ALU.add))
            st["conv"] = ts[3]
            t = V.do(V.w(done, ts[3], st.get("y")).tensor_tensor(YF, ps[:, :, :], CA, ALU.mult))
            st["yf"] = t
            st["y"] = split_x(YH[:, 4 * j:4 * j + 4, :], YL[:, 4 * j:4 * j + 4, :], YF, t)
            y_marks.extend([st["y"]] * 4)
            return t

        gemm(["b", "c", "a"] * 4, x, mixer)
        SQA = [scr(8208, 4, T), scr(9232, 4, T)]
        gemm(["o"] * 4, (YH, YL, y_marks), residual(ALPHA, SQA, "layer"))
        x = layer_norm(0, SQA)

        def ffn(l, x, meanwhile=None):
            barrier()
            if meanwhile:
                background.append(meanwhile())
            HH = scr(0, NF, T, dt=BF16)
            HL = scr(NF * 128, NF, T, dt=BF16)
            B0 = NF * 256
            GA = scr(B0, 4, T)
            GS = scr(B0 + 1024, 4, T)
            UA = scr(B0 + 2048, 4, T)
            HF = scr(B0 + 3072, 4, T)
            SQF = [scr(B0 + 4096, 4, T), scr(B0 + 5120, 4, T)]
            h_marks = []
            st = {}

            def evac(gi, ps, done):
                tag = groups[gi]["tag"]
                j = st.get("j", 0)
                dst, base, free = (GA, 0, st.get("gs")) if tag == "g" else (UA, NF, st.get("hf"))
                ts = []
                for n in range(4):
                    f = base + 4 * j + n
                    S.w(done, free)
                    ts.append(S.do(nc.scalar.activation(dst[:, n, :], ps[:, n, :], ACT.Identity,
                                                        bias=pr("f_bias", 88 * l + f),
                                                        scale=pr("f_conv", 264 * l + 176 + f))))
                for tap, sh in ((1, 1), (0, 2)):
                    for n in range(4):
                        f = base + 4 * j + n
                        V.w(ts[n], ts[n | 1])
                        ts[n] = V.do(nc.vector.scalar_tensor_tensor(
                            dst[:, n, sh:T], ps[:, n, 0:T - sh], pr("f_conv", 264 * l + 88 * tap + f),
                            dst[:, n, sh:T], ALU.mult, ALU.add))
                if tag == "g":
                    st["gs"] = S.do(S.w(ts[3], st.get("hf")).activation(GS, GA, ACT.Silu))
                else:
                    st["hf"] = V.do(V.w(ts[3], st["gs"], st.get("h")).tensor_tensor(HF, UA, GS, ALU.mult))
                    st["h"] = split_x(HH[:, 4 * j:4 * j + 4, :], HL[:, 4 * j:4 * j + 4, :], HF, st["hf"])
                    h_marks.extend([st["h"]] * 4)
                    st["j"] = j + 1
                return ts[3]

            gemm(["g", "u"] * 11, x, evac)
            gemm(["down"] * 4, (HH, HL, h_marks), residual(ALPHA, SQF, "layer"))
            return layer_norm(2 * l + 1, SQF, squares=l == 1)

        x = ffn(0, x)

        barrier()
        KA = [scr(0, 4, T), scr(1024, 4, T)]
        QA = [scr(2048, 4, T), scr(3072, 4, T)]
        VT = scr(4096, 2, D)
        YH = scr(8192, NT, T, dt=BF16)
        YL = scr(10240, NT, T, dt=BF16)
        COS = scr(12288, T)
        SIN = scr(12544, T)
        RT = scr(12800, 4, T)
        SS = scr(13824, 2, 384)
        PP = scr(14592, 2, 384)
        AA = scr(15360, 384)
        AT8 = scr(15744, 8, 384)
        OF = scr(18816, 2, T)
        OQ = scr(19328, 2, T)
        SM = scr(19840, 64)
        SQB = [scr(19904, 4, T), scr(20928, 4, T)]
        POSI = scr(19904, T).bitcast(I32)
        GN = SM[:, 32:34]
        LAM = SM[:, 34:35]

        def reduce_angle(dst, src, tmp, *marks):
            t = V.do(V.w(*marks).tensor_scalar(tmp, src, 1.0 / TWO_PI, MAGIC, ALU.mult, ALU.add))
            t = V.do(V.w(t).tensor_scalar(tmp, tmp, MAGIC, None, ALU.subtract))
            t = V.do(V.w(t).scalar_tensor_tensor(dst, tmp, -C1, src, ALU.mult, ALU.add))
            t = V.do(V.w(t).scalar_tensor_tensor(dst, tmp, -C2, dst, ALU.mult, ALU.add))
            t = V.do(V.w(t).scalar_tensor_tensor(dst, tmp, -C3, dst, ALU.mult, ALU.add))
            return V.do(V.w(t).tensor_scalar(dst, dst, PI_CLAMP, -PI_CLAMP, ALU.min, ALU.max))

        def cos_sin(cos, sin, ang, tmp, mark, *free):
            t_s = S.do(S.w(mark, *free).activation(sin, ang, ACT.Sin))
            t_a = S.do(S.w(mark).activation(tmp, ang, ACT.Abs))
            return t_s, S.do(S.w(t_a).activation(cos, tmp, ACT.Sin, bias=cn("halfpi"), scale=-1.0))

        d_pos = Queue(None, sem("d_pos"))
        t_p = dma(d_pos, POSI, A["positions"].partition_broadcast(128))
        t = V.do(V.w(t_p).tensor_scalar(RT[:, 0, :], POSI, 1.0, None, ALU.mult))
        t = V.do(V.w(t).tensor_scalar(RT[:, 0, :], RT[:, 0, :], cn("freq"), None, ALU.mult))
        t = reduce_angle(RT[:, 1, :], RT[:, 0, :], RT[:, 2, :], t)
        t_sin, t_cos = cos_sin(COS, SIN, RT[:, 1, :], RT[:, 2, :], t)

        lb = pr("b_lambda", 0, 4)
        V.do(V.w().tensor_tensor(SM[:, 36:37], lb[:, 0:1], lb[:, 1:2], ALU.mult))
        t = V.do(V.w().tensor_tensor(SM[:, 37:38], lb[:, 2:3], lb[:, 3:4], ALU.mult))
        PE.w(t)
        t = PE.do(mm(PB[:, 3, 0:2], ONE_128[:, :], SM[:, 36:38], True, True))
        t = S.do(S.w(t).activation(SM[:, 38:40], PB[:, 3, 0:2], ACT.Exp, scale=128.0))
        t = V.do(V.w(t).tensor_tensor(SM[:, 40:41], SM[:, 38:39], SM[:, 39:40], ALU.subtract))
        t_lam = V.do(V.w(t).tensor_scalar(LAM, SM[:, 40:41], LAM_INIT, None, ALU.add))
        t_gn = V.do(V.w().tensor_scalar(GN, pr("subln", 0, 2), 1.0 - LAM_INIT, None, ALU.mult))

        def v_evac(dst, marks, then=None):
            def evac(gi, ps, done):
                j = len(marks)
                t = S.do(S.w(done).activation(dst[:, :, 512 * j:512 * j + 512], ps, ACT.Copy))
                marks.append(t)
                if then:
                    then(j, t)
                return t
            return evac

        def rotate(dst, ps, done, *free):
            t = S.do(S.w(done, *free).activation(dst, ps[:, :, :], ACT.Copy))
            yield t
            PE.w(t, st.get("rope"), st.get("ss"))
            for m in range(2):
                t_r = PE.do(mm(PB[0:32, m, :], CN[0:32, CONST["rope"][0]:CONST["rope"][1]],
                               dst[0:32, 2 * m:2 * m + 2, :], True, True))
            yield
            sw = PB[0:32, 0:2, :].rearrange("p a (b t) -> p (a b) t", t=T)

            def b32(ap):
                return ap[0:32, :].unsqueeze(1).broadcast_to([32, 4, T])

            t1 = V.do(V.w(t_r, t_sin, st.get("rope")).tensor_tensor(RT[0:32, :, :], sw, b32(SIN), ALU.mult))
            t2 = V.do(V.w(t_cos).tensor_tensor(dst[0:32, :, :], dst[0:32, :, :], b32(COS), ALU.mult))
            st["rope"] = V.do(V.w(t1, t2).tensor_tensor(dst[0:32, :, :], dst[0:32, :, :], RT[0:32, :, :], ALU.add))
            yield

        def scores(q, k, pair, scale, mask):
            PE.w(st.get("ss"), st.get("rope"))
            for c, a in enumerate(pair):
                mm(PB[:, c, 0:256], q[:, a, 128:256], k[:, a, :], True, True)
                t = PE.do(mm(PB[:, c, 256:384], q[:, a, 0:128], k[:, a, 0:128], False, True))
            yield
            V.w(t, st.get("exp"))
            for c in range(2):
                t = V.do(nc.vector.scalar_tensor_tensor(SS[:, c, :], PB[:, c, 0:384], scale, mask, ALU.mult, ALU.add))
            st["ss"] = t
            V.w(t)
            V.do(nc.vector.tensor_reduce(SM[:, 0:2], SS[:, :, 0:256], AX.X, ALU.max, negate=True))
            st["max"] = V.do(nc.vector.tensor_reduce(SM[:, 2:4], SS[:, :, 256:384], AX.X, ALU.max, negate=True))
            yield

        def exps(mark, *free):
            S.w(mark, *free)
            for c in range(2):
                S.do(nc.scalar.activation(PP[:, c, 0:256], SS[:, c, 0:256], ACT.Exp, bias=SM[:, c:c + 1],
                                          accum_out=SM[:, 4 + c:5 + c]))
                t = S.do(nc.scalar.activation(PP[:, c, 256:384], SS[:, c, 256:384], ACT.Exp,
                                              bias=SM[:, 2 + c:3 + c], accum_out=SM[:, 6 + c:7 + c]))
            st["exp"] = t
            return t

        def turn(a, at, mark, *free):
            PE.w(mark, st.get("at"), st.get("ln"))
            PE.do(nc.tensor.transpose(PB[:, 2, 0:128], a[:, 256:384], cn("ident")))
            PE.do(nc.tensor.transpose(PB[:, 2, 128:256], a[:, 0:128], cn("ident")))
            t = st["tr"] = PE.do(nc.tensor.transpose(PB[:, 2, 256:384], a[:, 128:256], cn("ident")))
            yield
            st["at"] = S.do(S.w(t, *free).activation(at, PB[:, 2, 0:384], ACT.Copy))
            yield

        def weighted(v, col, nv, at, mark):
            PE.w(mark, st.get("of"))
            for e in range(nv):
                c = slice(col + 128 * e, col + 128 * e + 128)
                mm(PB[:, 3, T * e:T * e + T], v[:, 0, c], at[:, 0:256], e == 0, False)
                t = PE.do(mm(PB[:, 3, T * e + 128:T * e + T], v[:, 1, c], at[:, 256:384], False, True))
            st["pv"] = t
            return t

        def head_norm(nv, mark, ones, eps):
            o = PB[:, 3, 0:nv * T].rearrange("p (a b) -> p a b", b=T)
            t_o = S.do(S.w(mark, st.get("ofu")).activation(OF[:, 0:nv, :], o, ACT.Copy))
            t_q = S.do(S.w(st.get("ms")).activation(OQ[:, 0:nv, :], o, ACT.Square))
            st["of"] = t_q
            yield
            PE.w(t_q, st.get("ln"), st.get("at"), st.get("cross"))
            for e in range(nv):
                t = PE.do(mm(PB[:, 2, 0:T], ones[:, :], OQ[:, e, :], e == 0, e == nv - 1))
            st["ms"] = t
            yield
            t = S.do(S.w(t, st.get("ofu")).activation(STAT[:, 3, :], PB[:, 2, 0:T], ACT.Ln, bias=cn(eps)))
            st["ln"] = t
            t = S.do(S.w(t).activation(STAT[:, 3, :], STAT[:, 3, :], ACT.Exp, scale=-0.5))
            st["rms"] = (t, t_o)
            yield

        st = {}
        y_marks = [None] * NT
        v_marks = []

        def diff_scores(h, Q, K, first):
            yield from scores(Q, K, (first, first + 1), 128.0 ** -0.5, cn("mask"))
            t = exps(st["max"], st.get("aa"))
            t = V.do(V.w(t).reciprocal(SM[:, 8:12], SM[:, 4:8]))
            t = V.do(V.w(t, t_lam).tensor_scalar(SM[:, 12:16], SM[:, 8:12], LAM, -1.0, ALU.mult, ALU.mult))
            V.w(t, st.get("tr"))
            for sl, b in ((slice(0, 256), 0), (slice(256, 384), 2)):
                t = V.do(nc.vector.tensor_scalar(AA[:, sl], PP[:, 0, sl], SM[:, 8 + b:9 + b], None, ALU.mult))
            V.w(t)
            for sl, b in ((slice(0, 256), 0), (slice(256, 384), 2)):
                t = V.do(nc.vector.scalar_tensor_tensor(AA[:, sl], PP[:, 1, sl], SM[:, 13 + b:14 + b], AA[:, sl],
                                                        ALU.mult, ALU.add))
            st["aa"] = t
            yield
            yield from turn(AA, AT8[:, h, :], t)
            st[("at", h)] = st["at"]

        def diff_out(h, t_v):
            t = weighted(VT, 256 * h, 2, AT8[:, h, :], st[("at", h)])
            yield
            yield from head_norm(2, t, ONE_256, "eps5")
            V.w(*st["rms"])
            V.w(t_gn)
            for e in range(2):
                t = V.do(nc.vector.scalar_tensor_tensor(OF[:, e, :], OF[:, e, :], GN[:, e:e + 1], STAT[:, 3, :],
                                                        ALU.mult, ALU.mult))
            st["ofu"] = split_x(YH[:, 2 * h:2 * h + 2, :], YL[:, 2 * h:2 * h + 2, :], OF, t)
            y_marks[2 * h] = y_marks[2 * h + 1] = st["ofu"]
            yield

        def k_evac(gi, ps, done):
            j = st["kn"] = st.get("kn", -1) + 1
            while j >= 2 and ("q", j - 2) not in st:
                step()
            gen = rotate(KA[j % 2], ps, done, st.get(("q", j - 2)))
            t = next(gen)
            background.append(gen)
            return t

        def q_evac(gi, ps, done):
            j = st["kn"]
            gen = rotate(QA[j % 2], ps, done, st.get(("q", j - 2)))
            t = next(gen)

            def heads():
                yield from gen
                PE.w(st["rope"])
                yield from diff_scores(2 * j, QA[j % 2], KA[j % 2], 0)
                yield from diff_scores(2 * j + 1, QA[j % 2], KA[j % 2], 2)
                st[("q", j)] = st["tr"]

            background.append(heads())
            return t

        def outputs(j, t):
            def gen():
                PE.w(t)
                yield from diff_out(2 * j, t)
                yield from diff_out(2 * j + 1, t)
            background.append(gen())

        state["rate"] = 3
        for j in range(4):
            gemm(["k"], x, k_evac)
            gemm(["q"], x, q_evac)
        gemm(["v"] * 4, x, v_evac(VT, v_marks, outputs), row_major=True)
        gemm(["o"] * 4, (YH, YL, y_marks), residual(ALPHA, SQB, "layer"))
        state["rate"] = 1
        x = layer_norm(2, SQB)

        CSD = nc.dram_tensor("s5_rotation", (16, 128, 4 * T), F32).ap()
        CWD = nc.dram_tensor("s5_outputs", (8, 128, 1280), F32).ap()
        d_s5 = Queue(None, sem("d_s5"))
        d_cw = Queue(None, sem("d_cw"))
        d_cs = Queue(None, sem("d_cs"))

        def pool_dma(q, dst, src, *marks):
            return q.do(G.w(*marks).dma_start(dst, src), 16)

        def tt(out_, a, b, op, *marks):
            return V.do(V.w(*marks).tensor_tensor(out_, a, b, op))

        def s5_tables():
            R = 17408
            CT = [scr(R, 32, 16), scr(R + 512, 32, 16)]
            CO, SI = scr(R, 2, T), scr(R + 512, 2, T)
            CS = scr(R, 4 * T)
            CP = [scr(R + 1024, 32, 16), scr(R + 1536, 32, 16)]
            CW = scr(R + 2048, 1280)
            SP5 = scr(R + 3328, 16, 32)
            T1, T2, T3 = (scr(R + 3840 + 512 * n, 2, T) for n in range(3))
            for i, name in enumerate(("s5_cT_re", "s5_cT_im")):
                t_ct = pool_dma(d_s5, CT[i].rearrange("p a b -> p (a b)"), A[name])
            t_cw = G.do(G.w().memset(CW, 0.0))
            lr, li, ld = pr("lam_re", 0, 32), pr("lam_im", 0, 32), pr("log_dt", 0, 32)
            p = [SP5[:, n, :] for n in range(16)]
            dt, ang, th, cs, sn, ar, ai, nr, inv, cr, ci, tmp, tmp2 = p[:13]
            t = S.do(S.w().activation(dt, ld, ACT.Exp))
            tt(ang, li, dt, ALU.mult, t)
            t = tt(tmp, lr, dt, ALU.mult)
            t_mag = S.do(S.w(t).activation(MAG[:, :], tmp, ACT.Exp))
            state["mag"] = t_mag
            yield
            t = reduce_angle(th, ang, tmp2, V.now())
            yield
            t_s, t_c = cos_sin(cs, sn, th, tmp2, t)
            t = tt(ar, MAG[:, :], cs, ALU.mult, t_s, t_c, t_mag)
            t_ai = tt(ai, MAG[:, :], sn, ALU.mult)
            t_nr = V.do(V.w(t).tensor_scalar(nr, ar, -1.0, None, ALU.add))
            t = tt(inv, lr, lr, ALU.mult)
            t2 = tt(tmp, li, li, ALU.mult, t_mag)
            t = tt(inv, inv, tmp, ALU.add, t, t2)
            t = V.do(V.w(t).reciprocal(inv, inv))
            yield
            t2 = tt(cr, nr, lr, ALU.mult, t_nr, t_ai, t)
            t = tt(tmp, ai, li, ALU.mult)
            t = tt(cr, cr, tmp, ALU.add, t, t2)
            t = tt(cr, cr, inv, ALU.mult, t)
            t2 = tt(ci, ai, lr, ALU.mult)
            t = tt(tmp, nr, li, ALU.mult, t)
            t = tt(ci, ci, tmp, ALU.subtract, t, t2)
            t = tt(ci, ci, inv, ALU.mult, t)
            yield
            X = T1.rearrange("p a b -> p (a b)").rearrange("p (a b) -> p a b", b=16)
            t2 = tt(CP[0], CT[0], bcl(cr, 16), ALU.mult, t, t_ct)
            t = tt(X, CT[1], bcl(ci, 16), ALU.mult)
            t = tt(CP[0], CP[0], X, ALU.subtract, t, t2)
            t2 = tt(CP[1], CT[0], bcl(ci, 16), ALU.mult)
            t = tt(X, CT[1], bcl(cr, 16), ALU.mult, t)
            t = V.do(V.w(t, t2).scalar_tensor_tensor(CP[1], X, -1.0, CP[1], ALU.mult, ALU.subtract))
            yield
            for j in range(8):
                G.w(t, t_cw)
                for r in range(2):
                    for e in range(2):
                        dst = CW[:, 640 * r:640 * r + 640].rearrange("p (q s) -> p q s", s=160)
                        G.w(G.now())
                        t_w = G.do(nc.gpsimd.tensor_copy(dst[64 * e:64 * e + 64, :, 16 * e:16 * e + 16],
                                                         CP[r][64 * e:64 * e + 64, 4 * j:4 * j + 4, :]))
                t_cw = pool_dma(d_cw, CWD[j], CW, t_w)
                yield
            time = cn("time")
            t_cs = None
            for n in range(16):
                V.w(t, t_s, t_c)
                for c in range(2):
                    t1 = V.do(nc.vector.tensor_scalar(T1[:, c, :], time, th[:, 2 * n + c:2 * n + c + 1], None,
                                                      ALU.mult))
                t1 = reduce_angle(T2, T1, T3, t1)
                yield
                t_s, t_c = cos_sin(CO, SI, T2, T3, t1, t_cs)
                t_cs = pool_dma(d_cs, CSD[n], CS, t_s, t_c)
                yield

        x = ffn(1, x, s5_tables)

        def gla_heads(H, nv, q, k, b, v, v_marks, ones, weight, dst, E, MS, RED):
            for h in range(H):
                bb, kk, qq = b[:, h, :], k[:, h, :], q[:, h, :]
                V.w(st.get("e_used"))
                for l in range(1, 8):
                    w = 2 ** l
                    src = bb.rearrange("p (n w) -> p n w", w=w)
                    mid = src[:, :, w // 2 - 1:w // 2].broadcast_to([128, T // w, w])
                    V.do(nc.vector.tensor_tensor(E[:, l - 1, :].rearrange("p (n w) -> p n w", w=w), src, mid,
                                                 ALU.subtract))
                t = V.do(nc.vector.tensor_scalar(E[:, 7, 0:128], bb[:, 0:128], bb[:, 127:128], None, ALU.subtract))
                S.w(st.get("e_used"))
                t_b = S.do(nc.scalar.activation(E[:, 7, 128:256], bb[:, 128:256], ACT.Copy))
                t = S.do(S.w(t, t_b).activation(E, E, ACT.Abs))
                t = S.do(S.w(t).activation(E, E, ACT.Exp, scale=-1.0))
                yield
                V.w(t)
                for l in range(1, 9):
                    w = 2 ** l
                    for side, f in ((0, kk), (1, qq)):
                        e = E[:, l - 1, :].rearrange("p (n w) -> p n w", w=w)[:, :, side * w // 2:(side + 1) * w // 2]
                        f = f.rearrange("p (n w) -> p n w", w=w)[:, :, side * w // 2:(side + 1) * w // 2]
                        t = V.do(nc.vector.tensor_tensor(e, e, f, ALU.mult))
                t_e = t
                yield
                for m in range(2):
                    c = slice(128 * m, 128 * m + 128)
                    PE.w(t_e, st.get("ms_read"), st.get("ss"))
                    for l in range(8):
                        lhs, rhs = (kk[:, c], qq[:, c]) if l == 0 else (E[:, l - 1, c], E[:, l - 1, c])
                        last = mm(PB[:, l // 4, 128 * (l % 4):128 * (l % 4) + 128], lhs, rhs, l % 4 == 0, True)
                    t = PE.do(last)
                    if m == 0:
                        PE.w(st.get("cross"), st.get("ln"), st.get("at"))
                        t_x = PE.do(mm(PB[:, 2, 0:128], E[:, 7, 0:128], E[:, 7, 128:256], True, True))
                    else:
                        st["e_used"] = t
                    yield
                    if m == 0:
                        t_x = st["cross"] = S.do(S.w(t_x, st.get("pv")).activation(RED[:, 128:256], PB[:, 2, 0:128],
                                                                                   ACT.Copy))
                    t = V.do(V.w(t, st.get("red")).tensor_tensor(
                        MS, PB[:, 0:2, :].rearrange("p a b -> p (a b)"), cn("lmask"), ALU.mult))
                    st["ms_read"] = t
                    V.w(t, st.get("pv"))
                    t = st["red"] = V.do(nc.vector.tensor_reduce(RED[:, 256 * m:256 * m + 128],
                                                                 MS.rearrange("p (l t) -> p t l", l=8), AX.X, ALU.add))
                    yield
                PE.w(t_x, *v_marks)
                t = weighted(v, 128 * nv * h, nv, RED, t)
                yield
                yield from head_norm(nv, t, ones, "eps6")
                V.w(*st["rms"])
                for e in range(nv):
                    t = V.do(nc.vector.scalar_tensor_tensor(dst[:, nv * h + e, :], OF[:, e, :], weight(nv * h + e),
                                                            STAT[:, 3, :], ALU.mult, ALU.mult))
                st["ofu"] = st[("y", h)] = t
                yield

        def scan(dst, src, H, ones, *marks):
            t = G.do(G.w(*marks).memset(ones, 1.0))
            t = G.do(G.w(t).memset(ones.rearrange("p (m w) -> p m w", w=128)[:, :, 0:1], 0.0))
            return V.do(V.w(t, *marks).tensor_tensor_scan(dst.rearrange("p h t -> p (h t)"), ones,
                                                          src.rearrange("p h t -> p (h t)"), 0.0, ALU.mult, ALU.add))

        barrier()
        st = {}
        KB = scr(0, 4, T)
        QB = scr(1024, 4, T)
        BB = scr(2048, 4, T)
        VB = scr(3072, 2, 1024)
        GT = scr(0, 16, T)
        VA = scr(5120, 2, 1024)
        KD = scr(7168, 8, T)
        QD = scr(9216, 8, T)
        YR = scr(11264, 16, T)
        LG = scr(11264, 4, T)
        E1 = scr(15360, 8, T)
        MS = scr(17408, 1024)
        RED = scr(18432, 384)
        SS = scr(18816, 2, 384)
        PP = scr(19584, 2, 384)
        AT = scr(20352, 384)
        OF = scr(20736, 2, T)
        OQ = scr(21248, 2, T)
        SM = scr(21760, 64)
        GW = scr(21824, 512)
        GL = scr(22336, T)
        XN = [E1[:, 0:4, :], E1[:, 4:8, :]]
        d_gw = Queue(None, sem("d_gw"))
        t_gw = pool_dma(d_gw, GW[0:16, :], A["gla_w_gate"])
        x = rms_norm(lambda k: pr("norm", k), XN)

        def keep(dst, scale=1.0, marks=None):
            at = [0]

            def evac(gi, ps, done):
                j = at[0]
                at[0] += 1
                t = S.do(S.w(done).activation(dst[:, 4 * j:4 * j + 4, :], ps[:, :, :], ACT.Copy, scale=scale))
                marks.append(t)
                return t
            return evac

        def low(gi, ps, done):
            st["gl"] = S.do(S.w(done).activation(GL[0:16, :], ps[0:16, 0, :], ACT.Copy))
            return st["gl"]

        def gla_decay():
            PE.w(t_gw, st["gl"])
            for n in range(4):
                t = PE.do(mm(PB[:, n // 2, T * (n % 2):T * (n % 2) + T], GW[0:16, 128 * n:128 * n + 128], GL[0:16, :],
                             n % 2 == 0, True))
            yield
            V.w(t)
            for n in range(4):
                t = V.do(nc.vector.tensor_scalar(LG[:, n, :], PB[:, n // 2, T * (n % 2):T * (n % 2) + T],
                                                 pr("gla_b", n), None, ALU.add))
            st["ms_read"] = t
            t_a = S.do(S.w(t).activation(BB, LG, ACT.Abs))
            t_m = V.do(V.w(t_a).tensor_scalar(LG, LG, 0.0, 1.0 / 16, ALU.min, ALU.mult))
            t = S.do(S.w(t_a).activation(BB, BB, ACT.Exp, scale=-1.0))
            t = S.do(S.w(t).activation(BB, BB, ACT.Ln, bias=cn("one")))
            t = V.do(V.w(t, t_m).scalar_tensor_tensor(LG, BB, -1.0 / 16, LG, ALU.mult, ALU.add))
            yield
            st["scan"] = scan(BB, LG, 4, MS, t)
            yield

        def gla():
            PE.w(*b_marks)
            V.w(st["scan"], *b_marks)
            S.w(st["scan"])
            yield from gla_heads(4, 2, QB, KB, BB, VB, vb_marks, ONE_256, lambda n: pr("gla_norm", n), YR[:, 8:16, :],
                                 E1, MS, RED)
            st["gla"] = (st["ofu"], PE.now())

        def dilated():
            PE.w(*va_marks, *a_marks)
            for h in range(0, 8, 2):
                PE.w(st.get("ms_read"))
                yield from scores(QD, KD, (h, h + 1), 128.0 ** -0.5, cn("dmask"))
                t = exps(st["max"], st.get("tr"))
                t = V.do(V.w(t).tensor_tensor(PP, PP, bc(cn("dcount"), 2), ALU.mult))
                V.w(t)
                V.do(nc.vector.tensor_reduce(SM[:, 8:10], PP[:, :, 0:256], AX.X, ALU.add))
                t = V.do(nc.vector.tensor_reduce(SM[:, 10:12], PP[:, :, 256:384], AX.X, ALU.add))
                t = V.do(V.w(t).reciprocal(SM[:, 12:16], SM[:, 8:12]))
                V.w(t)
                for c in range(2):
                    V.do(nc.vector.tensor_scalar(PP[:, c, 0:256], PP[:, c, 0:256], SM[:, 12 + c:13 + c], None,
                                                 ALU.mult))
                    t = V.do(nc.vector.tensor_scalar(PP[:, c, 256:384], PP[:, c, 256:384], SM[:, 14 + c:15 + c],
                                                     None, ALU.mult))
                yield
                t_w = t
                for c in range(2):
                    yield from turn(PP[:, c, :], AT, t_w, st.get("pv"))
                    t = weighted(VA, 128 * (h + c), 1, AT, st["at"])
                    yield
                    st["of"] = S.do(S.w(t).activation(YR[:, h + c, :], PB[:, 3, 0:T], ACT.Copy))
                    st[("dil", h + c)] = st["of"]
                    yield

        g_marks = {}

        def gate(gi, ps, done):
            j = (2, 3, 0, 1)[len(g_marks)]
            g_marks[j] = S.do(S.w(done, *st.get("gt_free", ())).activation(GT[:, 4 * j:4 * j + 4, :], ps[:, :, :],
                                                                         ACT.Silu))
            return g_marks[j]

        def gated(g, y, marks, mark, free):
            t = tt(y, y, GT[:, 4 * g:4 * g + 4, :], ALU.mult, g_marks[g], mark)
            t = split_x(XH[:, 4 * g:4 * g + 4, :], XL[:, 4 * g:4 * g + 4, :], y, t, free)
            marks[4 * g:4 * g + 4] = [t] * 4

        b_marks, vb_marks, va_marks, a_marks = [], [], [], []
        state["rate"] = 3
        gemm(["kb"], x, keep(KB, marks=b_marks))
        gemm(["qb"], x, keep(QB, 128.0 ** -0.5, marks=b_marks))
        gemm(["glow"], x, low)
        background.append(gla_decay())
        gemm(["vb"] * 2, x, v_evac(VB, vb_marks), row_major=True)
        background.append(gla())
        gemm(["va"] * 2, x, v_evac(VA, va_marks), row_major=True)
        gemm(["ka"] * 2, x, keep(KD, marks=a_marks))
        gemm(["qa"] * 2, x, keep(QD, marks=a_marks))
        while "gla" not in st:
            step()
        st["gt_free"] = st["gla"]
        background.append(dilated())
        gemm(["gate"] * 4, x, gate)
        x_used = PE.now()
        marks = [None] * NT
        for g in (2, 3):
            gated(g, YR[:, 4 * g:4 * g + 4, :], marks, st["ofu"], x_used)

        def gated_dilated():
            for g in range(2):
                gated(g, YR[:, 4 * g:4 * g + 4, :], marks, st[("dil", 4 * g + 3)], x_used)
                yield

        background.append(gated_dilated())
        gemm(["o"] * 4, (XH, XL, marks), residual(None, XN, "rms"))
        state["rate"] = 1

        barrier()
        st = {}
        U = scr(0, 8, T)
        GT = scr(2048, 16, T)
        FF = scr(2048, 8, T)
        ONES = scr(4096, 2048)
        VI = scr(6144, 2, 1024)
        KD = scr(8192, 8, T)
        BD = scr(10240, 8, T)
        QH = scr(12288, 8, T)
        R = 14336
        BT = scr(R, 2, 2, 128)
        CW = scr(R + 512, 1280)
        CS = [scr(R + 1792, 4, T), scr(R + 2816, 4, T)]
        VR, VJ, T1, T2, X1, X2, MG = (scr(R + 3840 + 512 * n, 2, T) for n in range(7))
        E1 = scr(R, 8, T)
        MS = scr(R + 2048, 1024)
        RED = scr(R + 3072, 384)
        OF = scr(R + 3456, 1, T)
        OQ = scr(R + 3712, 1, T)
        SM = scr(R + 7424, 32)
        SG = scr(R + 7456, 2, T)
        XN = [scr(8192, 4, T), scr(9216, 4, T)]
        x = rms_norm(lambda k: pr("norm", 16 + k), XN)

        u_marks = []

        def s5():
            PE.w(*u_marks)
            d_bt = [Queue(None, sem(f"d_bt{n}")) for n in range(2)]
            d_ci = Queue(None, sem("d_ci"))
            d_ro = [Queue(None, sem(f"d_ro{n}")) for n in range(2)]
            flat = "p a b -> p (a b)"
            G.w(d_cs.now(), d_cw.now())

            def bt(j, *free):
                for r, name in enumerate(("s5_bT_re", "s5_bT_im")):
                    t = pool_dma(d_bt[j % 2], BT[:, j % 2, r, :], A[name][:, 128 * j:128 * j + 128], *free)
                return t

            def cs(n, *free):
                return pool_dma(d_ro[n % 2], CS[n % 2].rearrange(flat), CSD[n], *free)

            t_bt = [bt(0), bt(1)]
            t_cw = pool_dma(d_ci, CW, CWD[0])
            t_cs = [cs(0), cs(1)]
            used_b = {}

            def product(n):
                j = n // 2
                PE.w(t_bt[j % 2], st.get("br"))
                for r in range(2):
                    for c in range(2):
                        q = (2 * n + c) % 4
                        rows = slice(32 * q, 32 * q + 32)
                        t = PE.do(mm(PB[:, c, T * r:T * r + T], BT[rows, j % 2, r, :], U[rows, j, :], r == 0, True))
                if n % 2 and j + 2 < 8:
                    t_bt[j % 2] = bt(j + 2, t)
                return t

            t_b = product(0)
            t_y = None
            yield
            for n in range(16):
                j, i0 = n // 2, 2 * n
                CO, SI = CS[n % 2][:, 0:2, :], CS[n % 2][:, 2:4, :]
                S.w(st.get("scan"), state["mag"])
                for c in range(2):
                    t_g = S.do(nc.scalar.activation(MG[:, c, :], cn("time"), ACT.Identity, scale=0.0,
                                                    bias=MAG[:, i0 + c:i0 + c + 1]))
                t_g = S.do(S.w(t_g).activation(MG[:, :, 0:1], MG[:, :, 0:1], ACT.Copy, scale=0.0))
                br, bi = PB[:, 0:2, 0:T], PB[:, 0:2, T:2 * T]
                V.w(t_b, t_cs[n % 2], st.get("yb"))
                V.do(nc.vector.tensor_tensor(VR, br, CO, ALU.mult))
                V.do(nc.vector.tensor_tensor(T1, bi, SI, ALU.mult))
                V.do(nc.vector.tensor_tensor(VJ, bi, CO, ALU.mult))
                t = st["br"] = V.do(nc.vector.tensor_tensor(T2, br, SI, ALU.mult))
                V.w(t)
                V.do(nc.vector.tensor_tensor(VR, VR, T1, ALU.add))
                t = V.do(nc.vector.tensor_tensor(VJ, VJ, T2, ALU.subtract))
                yield
                if n < 15:
                    t_b = product(n + 1)
                V.w(t, t_g)
                V.do(nc.vector.tensor_tensor_scan(X1.rearrange(flat), MG.rearrange(flat), VR.rearrange(flat), 0.0,
                                                  ALU.mult, ALU.add))
                t = V.do(nc.vector.tensor_tensor_scan(X2.rearrange(flat), MG.rearrange(flat), VJ.rearrange(flat), 0.0,
                                                      ALU.mult, ALU.add))
                st["scan"] = t
                yield
                V.w(t)
                V.do(nc.vector.tensor_tensor(T1, X1, CO, ALU.mult))
                V.do(nc.vector.tensor_tensor(T2, X2, SI, ALU.mult))
                V.do(nc.vector.tensor_tensor(VR, X1, SI, ALU.mult))
                t = V.do(nc.vector.tensor_tensor(VJ, X2, CO, ALU.mult))
                if n < 14:
                    t_cs[n % 2] = cs(n + 2, t)
                V.w(t)
                V.do(nc.vector.tensor_tensor(T1, T1, T2, ALU.subtract))
                t = V.do(nc.vector.tensor_tensor(VR, VR, VJ, ALU.add))
                yield
                PE.w(t, t_cw, t_y)
                for c in range(2):
                    q = (i0 + c) % 4
                    for r, z in enumerate((T1, VR)):
                        last = mm(PB[:, 2, 0:T], CW[:, 640 * r + 128 * q:640 * r + 128 * q + 128], z[:, c, :],
                                  q == 0 and r == 0, q == 3 and r == 1)
                st["yb"] = PE.do(last)
                if n % 2:
                    if j < 7:
                        t_cw = pool_dma(d_ci, CW, CWD[j + 1], st["yb"])
                    yield
                    t_y = V.do(V.w(st["yb"]).scalar_tensor_tensor(U[:, j, :], U[:, j, :], pr("s5_d", j),
                                                                  PB[:, 2, 0:T], ALU.mult, ALU.add))
                    st[("u", j)] = t_y
                yield
            for g in range(2):
                t = st[("g", g)] = S.do(S.w(t_y).activation(U[:, 4 * g:4 * g + 4, :], U[:, 4 * g:4 * g + 4, :],
                                                            ACT.Gelu_apprx_tanh))
            st["s5"] = t
            yield

        LB, OM = SM[:, 0:8], SM[:, 8:16]
        gm = pr("gamma", 0, 16)
        t = tt(SM[:, 16:24], gm[:, 0:8], gm[:, 8:16], ALU.max)
        tt(LB, gm[:, 0:8], SM[:, 16:24], ALU.subtract, t)
        t = tt(OM, gm[:, 8:16], SM[:, 16:24], ALU.subtract)
        t = S.do(S.w(t).activation(SM[:, 0:16], SM[:, 0:16], ACT.Exp))
        t = tt(SM[:, 16:24], LB, OM, ALU.add, t)
        t = V.do(V.w(t).reciprocal(SM[:, 24:32], SM[:, 16:24]))
        tt(LB, LB, SM[:, 24:32], ALU.mult, t)
        t = tt(OM, OM, SM[:, 24:32], ALU.mult)
        t = tt(SM[:, 16:24], LB, OM, ALU.add, t)
        t = tt(LB, SM[:, 16:24], LB, ALU.subtract, t)
        t_lb = V.do(V.w(t).tensor_scalar(OM, LB, -1.0, 1.0, ALU.mult, ALU.add))
        f_marks = []

        def forget(gi, ps, done):
            j = len(f_marks)
            ff = FF[:, 4 * j:4 * j + 4, :]
            t_f = S.do(S.w(done).activation(ff, ps[:, :, :], ACT.Sigmoid))
            V.w(t_f, t_lb)
            for n in range(4):
                k = 4 * j + n
                t = V.do(nc.vector.tensor_scalar(FF[:, k, :], FF[:, k, :], OM[:, k:k + 1], LB[:, k:k + 1], ALU.mult,
                                                 ALU.add))
            st["kd"] = V.do(V.w(t).tensor_scalar(KD[:, 4 * j:4 * j + 4, :], ff, -1.0, 1.0, ALU.mult, ALU.add))
            f_marks.append(S.do(S.w(st["kd"]).activation(ff, ff, ACT.Ln)))
            return t_f

        q_marks, vi_marks = [], []

        def query(gi, ps, done):
            j = len(q_marks)
            t = S.do(S.w(done).activation(QH[:, 4 * j:4 * j + 4, :], ps[:, :, :], ACT.Silu))
            q_marks.append(t)
            return t

        def hgrn():
            PE.w(*q_marks)
            V.w(t_scan, *q_marks)
            S.w(t_scan)
            yield from gla_heads(8, 1, QH, KD, BD, VI, vi_marks, ONE_128, lambda n: pr("hgrn_norm", n), QH,
                                 E1, MS, RED)

        g_marks = {}
        gemm(["u"] * 2, x, keep(U, marks=u_marks))
        background.append(s5())
        state["rate"] = 3
        gemm(["fd"] * 2, x, forget)
        t_scan = scan(BD, FF, 8, ONES, *f_marks)
        st["gt_free"] = (t_scan,)
        gemm(["qd"] * 2, x, query)
        gemm(["idd"] * 2, x, v_evac(VI, vi_marks), row_major=True)
        gemm(["gate"] * 4, x, gate)
        x_used = PE.now()
        while "s5" not in st:
            step()
        marks = [None] * NT
        for g in range(2):
            t = split_x(XH[:, 4 * g:4 * g + 4, :], XL[:, 4 * g:4 * g + 4, :], U[:, 4 * g:4 * g + 4, :],
                        st[("g", g)], x_used)
            marks[4 * g:4 * g + 4] = [t] * 4
        V.w(st["yb"])
        S.w(st["yb"], V.now())
        PE.w(t)
        hg = hgrn()
        background.append(hg)
        glu_marks = []

        def glu(gi, ps, done):
            j = len(glu_marks) // 2
            for n in range(0, 4, 2):
                k = 4 * j + n
                S.w(done, glu_marks[-1] if glu_marks else None)
                for m in range(2):
                    t = S.do(nc.scalar.activation(SG[:, m, :], ps[:, n + m, :], ACT.Sigmoid,
                                                  bias=pr("b_glu", k + m)))
                glu_marks.append(tt(U[:, k:k + 2, :], U[:, k:k + 2, :], SG, ALU.mult, t))
            return t

        gemm(["glu"] * 2, (XH, XL, marks), glu)
        x_used = PE.now()
        marks = [None] * NT
        for g in range(2):
            gated(g, U[:, 4 * g:4 * g + 4, :], marks, glu_marks[-1], x_used)

        def gated_hgrn():
            for g in range(2, 4):
                gated(g, QH[:, 4 * g - 8:4 * g - 4, :], marks, st[("y", 4 * g - 5)], None)
                yield

        background.append(gated_hgrn())
        gemm(["o"] * 4, (XH, XL, marks), residual(None, None, None))
        while marks[-1] is None:
            step()
        XN = [scr(R, 4, T), scr(R + 1024, 4, T)]
        V.w(PE.now(), S.now())
        S.w(PE.now(), V.now())
        gemm(["o"] * 4, (XH, XL, marks), residual(None, XN, "rms"))
        out_v = out.rearrange("(t p) n -> p t n", p=128)
        XO = [scr(R + 2048, 4, T), scr(R + 3072, 4, T)]

        def store(g, src, t):
            return dma(d_out[g % 2], out_v[:, 4 * g:4 * g + 4, :], src, t)

        rms_norm(lambda k: pr("final", k), XO, store)
        SP.w(d_out[0].now(), d_out[1].now(), d_cs.now(), d_cw.now())


def feature_tiles(a):
    a = np.asarray(a)
    return np.ascontiguousarray(a.reshape(-1, a.shape[-1] // 128, 128).transpose(2, 0, 1)).reshape(128, -1)


def state_tiles(a):
    return np.ascontiguousarray(np.asarray(a).reshape(32, 128).T)


def kernel(**inputs):
    import concourse.bacc as bacc
    from concourse.bass_utils import run_bass_kernel_spmd

    a = {k: np.asarray(v) for k, v in inputs.items()}
    packed = {
        "ln_g": feature_tiles(a["ln_g"].reshape(4, D)), "ln_b": feature_tiles(a["ln_b"].reshape(4, D)),
        "a_conv": feature_tiles(a["a_conv_w"][0]), "f_conv": feature_tiles(a["ffn_conv_w"].reshape(6, 2 * DFF)),
        "f_bias": feature_tiles(a["ffn_conv_b"]), "subln": feature_tiles(a["b_subln_g"]),
        "norm": feature_tiles(a["norm_g_2"]), "final": feature_tiles(a["final_g_2"].reshape(1, D)),
        "gla_b": feature_tiles(a["gla_b_gate_2"]), "gla_norm": feature_tiles(a["gla_norm_g_2"]),
        "lam_re": state_tiles(a["s5_lam_re_2"][0]), "lam_im": state_tiles(a["s5_lam_im_2"][0]),
        "log_dt": state_tiles(np.repeat(a["s5_log_dt_2"][0][:, None], 64, 1)),
        "s5_d": feature_tiles(a["s5_d_2"].reshape(1, 1024)), "b_glu": feature_tiles(a["s5_b_glu_2"]),
        "gamma": feature_tiles(a["hgrn_gamma_2"]), "hgrn_norm": feature_tiles(a["hgrn_norm_g_2"]),
        "b_lambda": feature_tiles(a["b_lambda"][0]),
    }
    params = np.zeros((128, NPARAM), np.float32)
    for name, (lo, hi) in PARAM.items():
        params[:, lo:hi] = packed[name]

    def b_tiles(b):
        b = b[0].reshape(8, 4, 2, 64, 16)
        o = np.zeros((4, 2, 16, 8, 2, 64), np.float32)
        for e in range(2):
            o[:, e, :, :, e, :] = b[:, :, e].transpose(1, 3, 0, 2)
        return o.reshape(128, 1024)

    def c_tiles(c):
        return np.ascontiguousarray(c[0].reshape(32, 2, 16, 64).transpose(1, 3, 0, 2)).reshape(128, 512)

    arrays = {
        "consts": constants(), "params": params, "xT": np.ascontiguousarray(a["x"][0].T),
        "positions": np.ascontiguousarray(a["positions"][0]),
        "a_w_in": a["a_w_in"][0], "a_w_out": a["a_w_out"][0], "kv_w_k": a["kv_w_k"], "kv_w_v": a["kv_w_v"],
        "b_w_q": a["b_w_q"][0], "b_w_o": a["b_w_o"][0], "ffn_w_up": a["ffn_w_up"], "ffn_w_down": a["ffn_w_down"],
        "ab_w_in": a["ab_w_in_2"][0], "gla_w_gate": a["gla_w_gate_2"][0], "ab_w_out": a["ab_w_out_2"][0],
        "cd_w_in": a["cd_w_in_2"][0], "s5_w_glu": a["s5_w_glu_2"][0], "cd_w_out": a["cd_w_out_2"][0],
        "s5_bT_re": b_tiles(a["s5_b_re_2"]), "s5_bT_im": b_tiles(a["s5_b_im_2"]),
        "s5_cT_re": c_tiles(a["s5_c_re_2"]), "s5_cT_im": c_tiles(a["s5_c_im_2"]),
    }
    nc = bacc.Bacc("TRN2", target_bir_lowering=False, num_devices=1)
    ins = {n: nc.dram_tensor(n, v.shape, mybir.dt.from_np(v.dtype), kind="ExternalInput").ap()
           for n, v in arrays.items()}
    out = nc.dram_tensor("out", (D, T), F32, kind="ExternalOutput").ap()
    two_block_model(nc, ins, out)
    r = run_bass_kernel_spmd(nc, [arrays], core_ids=[0])
    return np.ascontiguousarray(r.results[0]["out"].T)[None]
```

```python
import math
from collections import deque
from contextlib import ExitStack

import numpy as np

import concourse.bass as bass
from concourse import mybir

F32 = mybir.dt.float32
BF16 = mybir.dt.bfloat16
I32 = mybir.dt.int32
ALU = mybir.AluOpType
ACT = mybir.ActivationFunctionType
AX = mybir.AxisListType

D = 2048
T = 256
NT = D // 128
DFF = 5632
NF = DFF // 128
ALPHA = 4.0 ** 0.25
LAM_INIT = 0.8 - 0.6 * math.exp(-0.3)
NEG = -1e30
RF = 3
RB = 5
LA = 3

MAGIC = 12582912.0
TWO_PI = 2.0 * math.pi
C1 = 6.28125
C2 = float(np.float32(np.round((TWO_PI - C1) * 2.0 ** 21) / 2.0 ** 21))
C3 = float(np.float32(TWO_PI - C1 - C2))
PI_CLAMP = 3.1415925


def columns(spec):
    at, out = 0, {}
    for name, n in spec:
        out[name] = (at, at + n)
        at += n
    return out, at


CONST, NCONST = columns([("ident", 128), ("rope", 32), ("freq", 1), ("eps5", 1), ("eps6", 1), ("one", 1),
                         ("halfpi", 1), ("zero", 1), ("mask", 384), ("dmask", 384), ("dcount", 384),
                         ("lmask", 1024), ("time", 256)])
PARAM, NPARAM = columns([("ln_g", 64), ("ln_b", 64), ("a_conv", 48), ("f_conv", 528), ("f_bias", 176),
                         ("subln", 2), ("norm", 32), ("final", 16), ("gla_b", 4), ("gla_norm", 8),
                         ("lam_re", 32), ("lam_im", 32), ("log_dt", 32), ("s5_d", 8), ("b_glu", 8),
                         ("gamma", 16), ("hgrn_norm", 8), ("b_lambda", 4)])


def constants():
    c = np.zeros((128, NCONST), np.float32)

    def put(name, v):
        a, b = CONST[name]
        c[:, a:b] = v

    put("ident", np.eye(128))
    rope = np.zeros((128, 32))
    for i in range(16):
        rope[i + 16, i] = -1.0
        rope[i, i + 16] = 1.0
    put("rope", rope)
    freq = np.float32(500000.0) ** (-np.arange(0, 32, 2, dtype=np.float32) / np.float32(32))
    col = np.zeros((128, 1))
    col[0:16, 0] = freq
    col[16:32, 0] = freq
    put("freq", col)
    put("eps5", 1e-5)
    put("eps6", 1e-6)
    put("one", 1.0)
    put("halfpi", math.pi / 2)
    i = np.arange(128)[:, None]
    j = np.arange(128)[None, :]
    tri = np.where(j <= i, 0.0, NEG)
    put("mask", np.concatenate([np.zeros((128, 128)), tri, tri], 1))
    d = np.concatenate([128 + i - j, i - j, i - j], 1)
    count = (d >= 0) * ((d <= 128).astype(int) + (d % 4 == 0) + (d % 16 == 0))
    put("dmask", np.where(count > 0, 0.0, NEG))
    put("dcount", count)
    lm = np.zeros((128, 8, 128))
    lm[:, 0, :] = i == j
    for l in range(1, 8):
        h = 2 ** (l - 1)
        lm[:, l, :] = (i // (2 * h) == j // (2 * h)) & (i % (2 * h) < h) & (j % (2 * h) >= h)
    put("lmask", lm.reshape(128, 1024))
    put("time", np.arange(256)[None, :])
    return c


class Queue:

    def __init__(self, eng, sem):
        self.eng, self.sem, self.n, self.seen = eng, sem, 0, {}

    def w(self, *marks):
        for m in marks:
            if m is None:
                continue
            q, v = m
            if self.seen.get(id(q), 0) < v:
                self.eng.wait_ge(q.sem, v)
                self.seen[id(q)] = v
        return self.eng

    def do(self, ins, by=1):
        ins.then_inc(self.sem, by)
        self.n += by
        return self, self.n

    def now(self):
        return (self, self.n) if self.n else None


def two_block_model(nc, A, out):
    ctx = ExitStack()
    with ctx:
        def sb(name, shape, dt=F32):
            return ctx.enter_context(nc.sbuf_tensor(name, shape, dt))

        def sem(name):
            return ctx.enter_context(nc.semaphore(name))

        XA = sb("XA", [128, NT, T])
        XH = sb("XH", [128, NT, T], BF16)
        XL = sb("XL", [128, NT, T], BF16)
        WF = sb("WF", [128, RF, 4, 512])
        WH = sb("WH", [128, RB, 4, 512], BF16)
        WL = sb("WL", [128, RB, 4, 512], BF16)
        CN = sb("CN", [128, NCONST])
        PR = sb("PR", [128, NPARAM])
        ONE_D = sb("ONE_D", [128, 128])
        ONE_256 = sb("ONE_256", [128, 128])
        ONE_128 = sb("ONE_128", [128, 128])
        SCR = sb("SCR", [128, 22848])
        STAT = sb("STAT", [128, 4, T])
        SUMS = sb("SUMS", [128, 2, T])
        MAG = sb("MAG", [128, 32])
        PSG = [ctx.enter_context(nc.psum_tensor(f"PSG{i}", [128, 4, T], F32)) for i in range(2)]
        PB = ctx.enter_context(nc.psum_tensor("PB", [128, 4, 512], F32))

        PE = Queue(nc.tensor, sem("s_pe"))
        V = Queue(nc.vector, sem("s_v"))
        S = Queue(nc.scalar, sem("s_s"))
        G = Queue(nc.gpsimd, sem("s_g"))
        SP = Queue(nc.sync, sem("s_sp"))
        d_in = Queue(None, sem("d_in"))
        d_x = [Queue(None, sem(f"d_x{g}")) for g in range(4)]
        d_w = [Queue(None, sem(f"d_w{i}")) for i in range(RF)]
        d_out = [Queue(None, sem(f"d_out{i}")) for i in range(2)]

        def dma(q, dst, src, *marks):
            return q.do(SP.w(*marks).dma_start(dst, src), 16)

        def cn(name, a=0, n=None):
            lo, hi = CONST[name]
            return CN[:, lo + a:hi if n is None else lo + a + n]

        def pr(name, a=0, n=1):
            lo = PARAM[name][0]
            return PR[:, lo + a:lo + a + n]

        def bc(ap, n):
            return ap.unsqueeze(1).broadcast_to([128, n, ap.shape[-1]])

        def bcl(ap, n):
            return ap.unsqueeze(2).broadcast_to([ap.shape[0], ap.shape[1], n])

        def scr(at, *shape, dt=F32):
            n = int(np.prod(shape))
            words = n if dt == F32 else n // 2
            v = SCR[:, at:at + words]
            if dt != F32:
                v = v.bitcast(dt)
            if len(shape) == 2:
                v = v.rearrange("p (a b) -> p a b", b=shape[1])
            if len(shape) == 3:
                v = v.rearrange("p (a b c) -> p a b c", b=shape[1], c=shape[2])
            return v

        def barrier(marks=None):
            drain()
            marks = marks or [q.now() for q in (PE, V, S, G)]
            for q in (PE, V, S, G, SP):
                q.w(*[m for m in marks if m and m[0] is not q])
                q.w(*[m for m in marks if m and m[0] is q and q is not PE])

        background = deque()

        def step():
            while background:
                try:
                    next(background[0])
                    return
                except StopIteration:
                    background.popleft()

        def drain():
            while background:
                step()

        G.do(G.w().memset(ONE_D[:, :], 1.0 / D))
        G.do(G.w().memset(ONE_256[:, :], 1.0 / 256))
        t_one = G.do(G.w().memset(ONE_128[:, :], 1.0 / 128))

        groups = []

        def add(w, col, width, rows, tag):
            groups.append(dict(w=w, col=col, width=width, rows=list(rows), tag=tag))

        def whole(K):
            return range(0, K, 512)

        for j in range(4):
            for part, tag in ((1, "b"), (2, "c"), (0, "a")):
                add(A["a_w_in"], part * D + j * 512, 512, whole(D), tag)
        for j in range(4):
            add(A["a_w_out"], j * 512, 512, whole(D), "o")

        def add_ffn(l):
            for j in range(11):
                add(A["ffn_w_up"][l], j * 512, 512, whole(D), "g")
                add(A["ffn_w_up"][l], DFF + j * 512, 512, whole(D), "u")
            for j in range(4):
                add(A["ffn_w_down"][l], j * 512, 512, whole(DFF), "down")

        add_ffn(0)
        for j in range(4):
            add(A["kv_w_k"], j * 512, 512, whole(D), "k")
            add(A["b_w_q"], j * 512, 512, whole(D), "q")
        for j in range(4):
            add(A["kv_w_v"], j * 512, 512, whole(D), "v")
        for j in range(4):
            add(A["b_w_o"], j * 512, 512, whole(D), "o")
        add_ffn(1)
        for tag, col, n in [("kb", 3584, 1), ("qb", 3072, 1), ("glow", 5120, 1), ("vb", 4096, 2), ("ka", 1024, 2),
                            ("qa", 0, 2), ("va", 2048, 2)]:
            for j in range(n):
                if tag == "glow":
                    add(A["ab_w_in"], col, 16, [0], tag)
                else:
                    add(A["ab_w_in"], col + 512 * j, 512, whole(D), tag)
        for j in (2, 3, 0, 1):
            add(A["ab_w_in"], 5136 + 512 * j, 512, whole(D), "gate")
        for j in range(4):
            add(A["ab_w_out"], j * 512, 512, (1024, 1536, 0, 512), "o")
        for tag, col, n in [("u", 0, 2), ("fd", 2048, 2), ("qd", 1024, 2), ("idd", 3072, 2)]:
            for j in range(n):
                add(A["cd_w_in"], col + 512 * j, 512, whole(D), tag)
        for j in (2, 3, 0):
            add(A["cd_w_in"], 4096 + 512 * j, 512, whole(D), "gate")
        for j in range(2):
            add(A["s5_w_glu"], j * 512, 512, whole(1024), "glu")
        add(A["cd_w_in"], 4096 + 512, 512, whole(D), "gate")
        for half in (0, 1024):
            for j in range(4):
                add(A["cd_w_out"], j * 512, 512, (half, half + 512), "o")

        chunks = []
        for g in groups:
            g["first"] = len(chunks)
            for k0 in g["rows"]:
                chunks.append((g, k0, 512 if g["width"] == 512 else D))

        def shaped(ring, i, rows, width):
            if width == 512:
                return ring[:, i, :, :]
            n = rows // 128 * width
            return ring[:, i, 0, 0:n].rearrange("p (t n) -> p t n", n=width)

        t_load, t_split, t_used = {}, {}, {}

        def load(i):
            if i >= len(chunks) or i in t_load:
                return
            g, k0, rows = chunks[i]
            src = g["w"][k0:k0 + rows, g["col"]:g["col"] + g["width"]].rearrange("(t p) n -> p t n", p=128)
            before = t_split.get(i - RF, (None, None))
            t_load[i] = dma(d_w[i % RF], shaped(WF, i % RF, rows, g["width"]), src, *before)

        def split(i):
            if i >= len(chunks) or i in t_split:
                return
            load(i)
            g, k0, rows = chunks[i]
            w, h, l = (shaped(r, i % n, rows, g["width"]) for r, n in ((WF, RF), (WH, RB), (WL, RB)))
            free = t_used.get(i - RB)
            t_h = S.do(S.w(t_load[i], free).activation(h, w, ACT.Copy))
            t_l = V.do(V.w(t_load[i], t_h, free).tensor_tensor(l, w, h, ALU.subtract))
            t_split[i] = (t_h, t_l)
            load(i + RF)

        t_x = []
        for g in range(4):
            c = slice(4 * g, 4 * g + 4)
            t_x.append(dma(d_x[g], XA[:, c, :], A["xT"].rearrange("(t p) n -> p t n", p=128)[:, c, :]))
            if g < RF:
                load(g)
        dma(d_in, CN[:, :], A["consts"])
        t_cn = dma(d_in, PR[:, :], A["params"])

        state = dict(g=0, free=[None, None], rate=1)

        def gemm(tags, x, evac, row_major=False):
            xt = x[2]
            xh, xl = (y if isinstance(y, list) else [y[:, k, :] for k in range(y.shape[1])] for y in x[:2])
            for tag in tags:
                gi = state["g"]
                g = groups[gi]
                assert g["tag"] == tag, (g["tag"], tag)
                state["g"] += 1
                ps = PSG[gi % 2]
                psr = ps[:, :, :].rearrange("p a b -> p (a b)").rearrange("p (t n) -> p t n", n=512)
                PE.w(state["free"][gi % 2])
                for c, k0 in enumerate(g["rows"]):
                    i = g["first"] + c
                    for ahead in range(LA + 1):
                        if ahead == 0 or i + ahead - RB in t_used or i + ahead < RB:
                            split(i + ahead)
                    rows = chunks[i][2]
                    h, l = (shaped(r, i % RB, rows, g["width"]) for r in (WH, WL))
                    PE.w(*t_split[i])
                    nk = rows // 128
                    for kk in range(nk):
                        k = k0 // 128 + kk
                        while xt[k] is None:
                            step()
                        PE.w(xt[k])
                        st = c == 0 and kk == 0
                        sp = c == len(g["rows"]) - 1 and kk == nk - 1
                        if g["width"] == 16:
                            for n, (a, b) in enumerate(((h, xh), (h, xl), (l, xh))):
                                last = nc.tensor.matmul(ps[0:16, 0, :], a[:, kk, :], b[k],
                                                        start=st and n == 0, stop=sp and n == 2,
                                                        skip_group_check=True)
                        elif row_major:
                            for m in range(2):
                                cs = slice(m * 128, m * 128 + 128)
                                for n, (a, b) in enumerate(((xh, h), (xh, l), (xl, h))):
                                    last = nc.tensor.matmul(psr[:, m, :], a[k][:, cs], b[:, kk, :],
                                                            start=st and n == 0, stop=sp and n == 2,
                                                            skip_group_check=True)
                        else:
                            for m in range(4):
                                cs = slice(m * 128, m * 128 + 128)
                                for n, (a, b) in enumerate(((h, xh), (h, xl), (l, xh))):
                                    last = nc.tensor.matmul(ps[:, m, :], a[:, kk, cs], b[k],
                                                            start=st and n == 0 and m % 2 == 0,
                                                            stop=sp and n == 2, skip_group_check=True)
                        if kk == 1 and state["rate"] > 1:
                            step()
                    t_used[i] = PE.do(last)
                    for _ in range(max(1, state["rate"] - 1)):
                        step()
                done = PE.now()
                state["free"][gi % 2] = evac(gi, psr if row_major else ps, done)

        def split_x(hi, lo, src, *marks):
            t_h = S.do(S.w(*marks).activation(hi, src, ACT.Copy))
            return V.do(V.w(t_h, *marks).tensor_tensor(lo, src, hi, ALU.subtract))

        def low_half(lo, src, hi, t_h):
            return V.do(V.w(t_h).tensor_tensor(lo, src, hi, ALU.subtract))

        def mm(o, lhsT, rhs, start, stop):
            return nc.tensor.matmul(o, lhsT, rhs, start=start, stop=stop, skip_group_check=True)

        GROUPS = [(0, 4), (4, 4), (8, 4), (12, 4)]
        EAGER = [(0, 1), (1, 3), (4, 4), (8, 4), (12, 4)]

        def rstd(src, mark, eps, dst):
            t = S.do(S.w(mark).activation(dst, src, ACT.Sqrt, bias=cn(eps)))
            return V.do(V.w(t).reciprocal(dst, dst))

        def tiles(g):
            return XA[:, 4 * g:4 * g + 4, :]

        def add_tiles(src, *marks):
            i = state["sum"] = 1 - state.get("sum", 1)
            return V.do(V.w(state.get(("sum", i)), *marks).tensor_reduce(
                SUMS[:, i, :], src.rearrange("p n t -> p t n"), AX.X, ALU.add)), i

        def sum_features(bank, mark, i, first, last):
            PE.w(mark)
            t = state[("sum", i)] = PE.do(mm(PB[:, bank, 0:T], ONE_D[:, :], SUMS[:, i, :], first, last))
            return t

        def sum_tiles(bank, mark, src, first, last):
            PE.w(mark)
            for n in range(4):
                t = mm(PB[:, bank, 0:T], ONE_D[:, :], src[:, n, :], first and n == 0, last and n == 3)
            return PE.do(t)

        def residual(scale, SQ, stats):
            at = [0]

            def evac(gi, ps, done):
                g = at[0]
                at[0] += 1
                x = tiles(g)
                if scale is None:
                    t = V.do(V.w(done).tensor_tensor(x, ps[:, :, :], x, ALU.add))
                else:
                    t = V.do(V.w(done).scalar_tensor_tensor(x, x, scale, ps[:, :, :], ALU.mult, ALU.add))
                if stats == "layer":
                    background.append(layer_stats(g, t))
                elif stats == "rms":
                    background.append(square(g, t))
                return t

            def square(g, t):
                t = S.do(S.w(t, state.get(("sq", g % 2))).activation(SQ[g % 2], tiles(g), ACT.Square))
                yield
                if g == 3:
                    state[("sq", 1)] = state["squares"] = sum_tiles(1, t, SQ[1], False, True)
                else:
                    t, i = add_tiles(SQ[g % 2], t)
                    state[("sq", g % 2)] = t
                    yield
                    state["squares"] = sum_features(1, t, i, g == 0, False)
                yield

            def centre(g, t):
                return V.do(V.w(t).tensor_tensor(tiles(g), tiles(g), bc(STAT[:, 0, :], 4), ALU.subtract))

            def layer_stats(g, t):
                if g < 3:
                    t, i = add_tiles(tiles(g), t)
                    yield
                    t = sum_features(0, t, i, g == 0, g == 2)
                    yield
                if g == 2:
                    t_c = S.do(S.w(t).activation(STAT[:, 0, :], PB[:, 0, 0:T], ACT.Copy, scale=4.0 / 3.0))
                    yield
                    for q in range(3):
                        yield from square(q, centre(q, t_c))
                if g == 3:
                    t = centre(3, t)
                    gen = square(3, t)
                    next(gen)
                    state["rest"] = sum_tiles(2, t, tiles(3), True, True)
                    yield from gen

            return evac

        def layer_norm(which, SQ, squares=False):
            drain()
            state["region"] = [q.now() for q in (PE, V, S, G)]
            m, r = STAT[:, 1, :], STAT[:, 2, :]
            t_m = S.do(S.w(state["rest"]).activation(m, PB[:, 2, 0:T], ACT.Copy))
            t_q = S.do(S.w(t_m).activation(r, m, ACT.Square))
            t = V.do(V.w(t_q, state["squares"]).tensor_tensor(r, PB[:, 1, 0:T], r, ALU.subtract))
            t_r = rstd(r, t, "eps5", r)
            marks = []
            t_sq = [None, None]
            lo = None
            for g, (a, n) in enumerate(GROUPS if squares else EAGER):
                c = slice(a, a + n)
                x = XA[:, c, :]
                t = V.do(V.w(t_m).tensor_tensor(x, x, bc(m, n), ALU.subtract))
                t = V.do(V.w(t, t_r).tensor_tensor(x, x, bc(r, n), ALU.mult))
                if lo:
                    marks += [low_half(*lo[1:])] * lo[0]
                    lo = None
                S.w(t)
                for k in range(a, a + n):
                    t = S.do(nc.scalar.activation(XA[:, k, :], XA[:, k, :], ACT.Identity,
                                                  bias=pr("ln_b", 16 * which + k), scale=pr("ln_g", 16 * which + k)))
                if squares:
                    t = S.do(S.w(t, t_sq[g % 2]).activation(SQ[g % 2], x, ACT.Square))
                    t_sq[g % 2] = state["squares"] = sum_tiles(1, t, SQ[g % 2], g == 0, g == 3)
                else:
                    t = S.do(S.w(t).activation(XH[:, c, :], x, ACT.Copy))
                    lo = (n, XL[:, c, :], x, XH[:, c, :], t)
            if lo:
                marks += [low_half(*lo[1:])] * lo[0]
            return XH, XL, marks

        def rms_norm(weight, XN, store=None):
            drain()
            r = STAT[:, 3, :]
            t_r = rstd(PB[:, 1, 0:T], state["squares"], "eps6", r)
            marks = []
            free = [None, None]
            lo = None
            for g, (a, n) in enumerate(GROUPS if store else EAGER):
                c, y = slice(a, a + n), XN[g % 2][:, 0:n, :]
                V.w(t_r, free[g % 2])
                for i in range(n):
                    t = V.do(nc.vector.scalar_tensor_tensor(y[:, i, :], XA[:, a + i, :], weight(a + i), r, ALU.mult,
                                                            ALU.mult))
                if store:
                    free[g % 2] = store(g, y, t)
                else:
                    t = S.do(S.w(t, free[g % 2]).activation(XH[:, c, :], y, ACT.Copy))
                    if lo:
                        free[(g - 1) % 2] = low_half(*lo[1:])
                        marks += [free[(g - 1) % 2]] * lo[0]
                    lo = (n, XL[:, c, :], y, XH[:, c, :], t)
            if lo:
                marks += [low_half(*lo[1:])] * lo[0]
            return XH, XL, marks

        marks = []
        for g in range(4):
            t = split_x(XH[:, 4 * g:4 * g + 4, :], XL[:, 4 * g:4 * g + 4, :], XA[:, 4 * g:4 * g + 4, :],
                        t_x[g])
            marks += [t] * 4
            if g < RF:
                split(g)
        x = (XH, XL, marks)

        YH = scr(0, NT, T, dt=BF16)
        YL = scr(2048, NT, T, dt=BF16)
        CB = scr(4096, 4, T)
        CX = scr(5120, 4, T + 2)
        CA = scr(6160, 4, T)
        YF = scr(7184, 4, T)
        y_marks = []
        st = {}
        t_pad = G.do(G.w().memset(CX[:, :, 0:2], 0.0))

        def mixer(gi, ps, done):
            tag = groups[gi]["tag"]
            j = gi // 3
            for q in (PE, V, S, G):
                q.w(t_cn, t_one)
            if tag == "b":
                st["c"] = S.do(S.w(done, st.get("cx")).activation(CB, ps[:, :, :], ACT.Copy))
                return st["c"]
            if tag == "c":
                st["cx"] = V.do(V.w(done, st["c"], st.get("conv"), t_pad).tensor_tensor(
                    CX[:, :, 2:T + 2], ps[:, :, :], CB, ALU.mult))
                return st["cx"]
            ts = []
            for n in range(4):
                V.w(st["cx"], st.get("yf"))
                ts.append(V.do(nc.vector.tensor_scalar(CA[:, n, :], CX[:, n, 0:T], pr("a_conv", 4 * j + n), None,
                                                       ALU.mult)))
            for tap in (1, 2):
                for n in range(4):
                    V.w(ts[n])
                    ts[n] = V.do(nc.vector.scalar_tensor_tensor(
                        CA[:, n, :], CX[:, n, tap:tap + T], pr("a_conv", 16 * tap + 4 * j + n), CA[:, n, :],
                        ALU.mult, ALU.add))
            st["conv"] = ts[3]
            t = V.do(V.w(done, ts[3], st.get("y")).tensor_tensor(YF, ps[:, :, :], CA, ALU.mult))
            st["yf"] = t
            st["y"] = split_x(YH[:, 4 * j:4 * j + 4, :], YL[:, 4 * j:4 * j + 4, :], YF, t)
            y_marks.extend([st["y"]] * 4)
            return t

        gemm(["b", "c", "a"] * 4, x, mixer)
        SQA = [scr(8208, 4, T), scr(9232, 4, T)]
        state["rate"] = 4
        gemm(["o"] * 4, (YH, YL, y_marks), residual(ALPHA, SQA, "layer"))
        state["rate"] = 1
        x = layer_norm(0, SQA)

        def ffn(l, x, meanwhile=None):
            barrier(state["region"])
            if meanwhile:
                background.append(meanwhile())
            HH = scr(0, NF, T, dt=BF16)
            HL = scr(NF * 128, NF, T, dt=BF16)
            B0 = NF * 256
            GA = scr(B0, 4, T)
            GS = scr(B0 + 1024, 4, T)
            UA = scr(B0 + 2048, 4, T)
            HF = scr(B0 + 3072, 4, T)
            SQF = [scr(B0 + 4096, 4, T), scr(B0 + 5120, 4, T)]
            h_marks = []
            st = {}

            def evac(gi, ps, done):
                tag = groups[gi]["tag"]
                j = st.get("j", 0)
                dst, base, free = (GA, 0, st.get("gs")) if tag == "g" else (UA, NF, st.get("hf"))
                ts = []
                for n in range(4):
                    f = base + 4 * j + n
                    S.w(done, free)
                    ts.append(S.do(nc.scalar.activation(dst[:, n, :], ps[:, n, :], ACT.Identity,
                                                        bias=pr("f_bias", 88 * l + f),
                                                        scale=pr("f_conv", 264 * l + 176 + f))))
                for tap, sh in ((1, 1), (0, 2)):
                    for n in range(4):
                        f = base + 4 * j + n
                        V.w(ts[n], ts[n | 1])
                        ts[n] = V.do(nc.vector.scalar_tensor_tensor(
                            dst[:, n, sh:T], ps[:, n, 0:T - sh], pr("f_conv", 264 * l + 88 * tap + f),
                            dst[:, n, sh:T], ALU.mult, ALU.add))
                if tag == "g":
                    st["gs"] = S.do(S.w(ts[3], st.get("hf")).activation(GS, GA, ACT.Silu))
                else:
                    st["hf"] = V.do(V.w(ts[3], st["gs"], st.get("h")).tensor_tensor(HF, UA, GS, ALU.mult))
                    st["h"] = split_x(HH[:, 4 * j:4 * j + 4, :], HL[:, 4 * j:4 * j + 4, :], HF, st["hf"])
                    h_marks.extend([st["h"]] * 4)
                    st["j"] = j + 1
                return ts[3]

            gemm(["g", "u"] * 11, x, evac)
            gemm(["down"] * 4, (HH, HL, h_marks), residual(ALPHA, SQF, "layer"))
            return layer_norm(2 * l + 1, SQF, squares=l == 1)

        def reduce_angle(dst, src, tmp, *marks):
            t = V.do(V.w(*marks).tensor_scalar(tmp, src, 1.0 / TWO_PI, MAGIC, ALU.mult, ALU.add))
            t = V.do(V.w(t).tensor_scalar(tmp, tmp, MAGIC, None, ALU.subtract))
            t = V.do(V.w(t).scalar_tensor_tensor(dst, tmp, -C1, src, ALU.mult, ALU.add))
            t = V.do(V.w(t).scalar_tensor_tensor(dst, tmp, -C2, dst, ALU.mult, ALU.add))
            t = V.do(V.w(t).scalar_tensor_tensor(dst, tmp, -C3, dst, ALU.mult, ALU.add))
            return V.do(V.w(t).tensor_scalar(dst, dst, PI_CLAMP, -PI_CLAMP, ALU.min, ALU.max))

        def cos_sin(cos, sin, ang, tmp, mark, *free):
            t_s = S.do(S.w(mark, *free).activation(sin, ang, ACT.Sin))
            t_a = S.do(S.w(mark).activation(tmp, ang, ACT.Abs))
            return t_s, S.do(S.w(t_a).activation(cos, tmp, ACT.Sin, bias=cn("halfpi"), scale=-1.0))

        COS = scr(21952, T)
        SIN = scr(22208, T)
        SM = scr(19840, 64)
        GN = SM[:, 32:34]
        LAM = SM[:, 34:35]
        ready = {}

        def attention_tables():
            RT = scr(19904, 3, T)
            POSI = scr(20928, T).bitcast(I32)
            d_pos = Queue(None, sem("d_pos"))
            t_p = dma(d_pos, POSI, A["positions"].partition_broadcast(128))
            yield
            t = V.do(V.w(t_p).tensor_scalar(RT[:, 0, :], POSI, 1.0, None, ALU.mult))
            t = V.do(V.w(t).tensor_scalar(RT[:, 0, :], RT[:, 0, :], cn("freq"), None, ALU.mult))
            t = reduce_angle(RT[:, 1, :], RT[:, 0, :], RT[:, 2, :], t)
            yield
            ready["sin"], ready["cos"] = cos_sin(COS, SIN, RT[:, 1, :], RT[:, 2, :], t)
            lb = pr("b_lambda", 0, 4)
            V.do(V.w().tensor_tensor(SM[:, 36:37], lb[:, 0:1], lb[:, 1:2], ALU.mult))
            t = V.do(V.w().tensor_tensor(SM[:, 37:38], lb[:, 2:3], lb[:, 3:4], ALU.mult))
            yield
            PE.w(t)
            t = PE.do(mm(PB[:, 3, 0:2], ONE_128[:, :], SM[:, 36:38], True, True))
            yield
            t = S.do(S.w(t).activation(SM[:, 38:40], PB[:, 3, 0:2], ACT.Exp, scale=128.0))
            t = V.do(V.w(t).tensor_tensor(SM[:, 40:41], SM[:, 38:39], SM[:, 39:40], ALU.subtract))
            ready["lam"] = V.do(V.w(t).tensor_scalar(LAM, SM[:, 40:41], LAM_INIT, None, ALU.add))
            ready["gn"] = V.do(V.w().tensor_scalar(GN, pr("subln", 0, 2), 1.0 - LAM_INIT, None, ALU.mult))
            yield

        x = ffn(0, x, attention_tables)

        barrier(state["region"])
        KA = [scr(0, 4, T), scr(1024, 4, T)]
        QA = [scr(2048, 4, T), scr(3072, 4, T)]
        VT = scr(4096, 2, D)
        YH = scr(8192, NT, T, dt=BF16)
        YL = scr(10240, NT, T, dt=BF16)
        RT = scr(12800, 4, T)
        SS = scr(13824, 2, 384)
        PP = scr(14592, 2, 384)
        AA = scr(15360, 384)
        AT8 = scr(15744, 8, 384)
        OF = scr(18816, 2, T)
        OQ = scr(19328, 2, T)
        SQB = [scr(19904, 4, T), scr(20928, 4, T)]

        def v_evac(dst, marks, then=None):
            def evac(gi, ps, done):
                j = len(marks)
                t = S.do(S.w(done).activation(dst[:, :, 512 * j:512 * j + 512], ps, ACT.Copy))
                marks.append(t)
                if then:
                    then(j, t)
                return t
            return evac

        def rotate(dst, ps, done, *free):
            t = S.do(S.w(done, *free).activation(dst, ps[:, :, :], ACT.Copy))
            yield t
            PE.w(t, st.get("rope"), st.get("ss"))
            for m in range(2):
                t_r = PE.do(mm(PB[0:32, m, :], CN[0:32, CONST["rope"][0]:CONST["rope"][1]],
                               dst[0:32, 2 * m:2 * m + 2, :], True, True))
            yield
            sw = PB[0:32, 0:2, :].rearrange("p a (b t) -> p (a b) t", t=T)

            def b32(ap):
                return ap[0:32, :].unsqueeze(1).broadcast_to([32, 4, T])

            t1 = V.do(V.w(t_r, ready["sin"], st.get("rope")).tensor_tensor(RT[0:32, :, :], sw, b32(SIN), ALU.mult))
            t2 = V.do(V.w(ready["cos"]).tensor_tensor(dst[0:32, :, :], dst[0:32, :, :], b32(COS), ALU.mult))
            st["rope"] = V.do(V.w(t1, t2).tensor_tensor(dst[0:32, :, :], dst[0:32, :, :], RT[0:32, :, :], ALU.add))
            yield

        def scores(q, k, pair, scale, mask):
            PE.w(st.get("ss"), st.get("rope"))
            for c, a in enumerate(pair):
                mm(PB[:, c, 0:256], q[:, a, 128:256], k[:, a, :], True, True)
                t = PE.do(mm(PB[:, c, 256:384], q[:, a, 0:128], k[:, a, 0:128], False, True))
            yield
            V.w(t, st.get("exp"))
            for c in range(2):
                t = V.do(nc.vector.scalar_tensor_tensor(SS[:, c, :], PB[:, c, 0:384], scale, mask, ALU.mult, ALU.add))
            st["ss"] = t
            V.w(t)
            V.do(nc.vector.tensor_reduce(SM[:, 0:2], SS[:, :, 0:256], AX.X, ALU.max, negate=True))
            st["max"] = V.do(nc.vector.tensor_reduce(SM[:, 2:4], SS[:, :, 256:384], AX.X, ALU.max, negate=True))
            yield

        def exps(mark, *free):
            S.w(mark, *free)
            for c in range(2):
                S.do(nc.scalar.activation(PP[:, c, 0:256], SS[:, c, 0:256], ACT.Exp, bias=SM[:, c:c + 1],
                                          accum_out=SM[:, 4 + c:5 + c]))
                t = S.do(nc.scalar.activation(PP[:, c, 256:384], SS[:, c, 256:384], ACT.Exp,
                                              bias=SM[:, 2 + c:3 + c], accum_out=SM[:, 6 + c:7 + c]))
            st["exp"] = t
            return t

        def turn(a, at, mark, *free):
            PE.w(mark, st.get("at"), st.get("ln"))
            PE.do(nc.tensor.transpose(PB[:, 2, 0:128], a[:, 256:384], cn("ident")))
            PE.do(nc.tensor.transpose(PB[:, 2, 128:256], a[:, 0:128], cn("ident")))
            t = st["tr"] = PE.do(nc.tensor.transpose(PB[:, 2, 256:384], a[:, 128:256], cn("ident")))
            yield
            st["at"] = S.do(S.w(t, *free).activation(at, PB[:, 2, 0:384], ACT.Copy))
            yield

        def weighted(v, col, nv, at, mark):
            PE.w(mark, st.get("of"))
            for e in range(nv):
                c = slice(col + 128 * e, col + 128 * e + 128)
                mm(PB[:, 3, T * e:T * e + T], v[:, 0, c], at[:, 0:256], e == 0, False)
                t = PE.do(mm(PB[:, 3, T * e + 128:T * e + T], v[:, 1, c], at[:, 256:384], False, True))
            st["pv"] = t
            return t

        def head_norm(nv, mark, ones, eps):
            o = PB[:, 3, 0:nv * T].rearrange("p (a b) -> p a b", b=T)
            t_o = S.do(S.w(mark, st.get("ofu")).activation(OF[:, 0:nv, :], o, ACT.Copy))
            t_q = S.do(S.w(st.get("ms")).activation(OQ[:, 0:nv, :], o, ACT.Square))
            st["of"] = t_q
            yield
            PE.w(t_q, st.get("ln"), st.get("at"), st.get("cross"))
            for e in range(nv):
                t = PE.do(mm(PB[:, 2, 0:T], ones[:, :], OQ[:, e, :], e == 0, e == nv - 1))
            st["ms"] = t
            yield
            t = S.do(S.w(t, st.get("ofu")).activation(STAT[:, 3, :], PB[:, 2, 0:T], ACT.Ln, bias=cn(eps)))
            st["ln"] = t
            t = S.do(S.w(t).activation(STAT[:, 3, :], STAT[:, 3, :], ACT.Exp, scale=-0.5))
            st["rms"] = (t, t_o)
            yield

        st = {}
        y_marks = [None] * NT
        v_marks = []

        def diff_scores(h, Q, K, first):
            yield from scores(Q, K, (first, first + 1), 128.0 ** -0.5, cn("mask"))
            t = exps(st["max"], st.get("aa"))
            t = V.do(V.w(t).reciprocal(SM[:, 8:12], SM[:, 4:8]))
            t = V.do(V.w(t, ready["lam"]).tensor_scalar(SM[:, 12:16], SM[:, 8:12], LAM, -1.0, ALU.mult, ALU.mult))
            V.w(t, st.get("tr"))
            for sl, b in ((slice(0, 256), 0), (slice(256, 384), 2)):
                t = V.do(nc.vector.tensor_scalar(AA[:, sl], PP[:, 0, sl], SM[:, 8 + b:9 + b], None, ALU.mult))
            V.w(t)
            for sl, b in ((slice(0, 256), 0), (slice(256, 384), 2)):
                t = V.do(nc.vector.scalar_tensor_tensor(AA[:, sl], PP[:, 1, sl], SM[:, 13 + b:14 + b], AA[:, sl],
                                                        ALU.mult, ALU.add))
            st["aa"] = t
            yield
            yield
            yield from turn(AA, AT8[:, h, :], t)
            st[("at", h)] = st["at"]

        def diff_out(h, t_v):
            t = weighted(VT, 256 * h, 2, AT8[:, h, :], st[("at", h)])
            yield
            yield from head_norm(2, t, ONE_256, "eps5")
            V.w(*st["rms"])
            V.w(ready["gn"])
            for e in range(2):
                t = V.do(nc.vector.scalar_tensor_tensor(OF[:, e, :], OF[:, e, :], GN[:, e:e + 1], STAT[:, 3, :],
                                                        ALU.mult, ALU.mult))
            st["ofu"] = split_x(YH[:, 2 * h:2 * h + 2, :], YL[:, 2 * h:2 * h + 2, :], OF, t)
            y_marks[2 * h] = y_marks[2 * h + 1] = st["ofu"]
            yield

        def k_evac(gi, ps, done):
            j = st["kn"] = st.get("kn", -1) + 1
            while j >= 2 and ("q", j - 2) not in st:
                step()
            gen = rotate(KA[j % 2], ps, done, st.get(("q", j - 2)))
            t = next(gen)
            background.append(gen)
            return t

        def q_evac(gi, ps, done):
            j = st["kn"]
            gen = rotate(QA[j % 2], ps, done, st.get(("q", j - 2)))
            t = next(gen)

            def heads():
                yield from gen
                yield
                PE.w(st["rope"])
                yield from diff_scores(2 * j, QA[j % 2], KA[j % 2], 0)
                yield from diff_scores(2 * j + 1, QA[j % 2], KA[j % 2], 2)
                st[("q", j)] = st["tr"]

            background.append(heads())
            return t

        def outputs(j, t):
            def gen():
                PE.w(t)
                yield from diff_out(2 * j, t)
                yield from diff_out(2 * j + 1, t)
            background.append(gen())

        state["rate"] = 3
        for j in range(4):
            gemm(["k"], x, k_evac)
            gemm(["q"], x, q_evac)
        gemm(["v"] * 4, x, v_evac(VT, v_marks, outputs), row_major=True)
        state["rate"] = 4
        gemm(["o"] * 4, (YH, YL, y_marks), residual(ALPHA, SQB, "layer"))
        state["rate"] = 1
        x = layer_norm(2, SQB)

        CSD = nc.dram_tensor("s5_rotation", (16, 128, 4 * T), F32).ap()
        CWD = nc.dram_tensor("s5_outputs", (8, 128, 1280), F32).ap()
        d_s5 = Queue(None, sem("d_s5"))
        d_cw = Queue(None, sem("d_cw"))
        d_cs = Queue(None, sem("d_cs"))

        def pool_dma(q, dst, src, *marks):
            return q.do(G.w(*marks).dma_start(dst, src), 16)

        def tt(out_, a, b, op, *marks):
            return V.do(V.w(*marks).tensor_tensor(out_, a, b, op))

        def s5_tables():
            R = 17408
            CT = [scr(R, 32, 16), scr(R + 512, 32, 16)]
            CO, SI = scr(R, 2, T), scr(R + 512, 2, T)
            CS = scr(R, 4 * T)
            CP = [scr(R + 1024, 32, 16), scr(R + 1536, 32, 16)]
            CW = scr(R + 2048, 1280)
            SP5 = scr(R + 3328, 16, 32)
            T1, T2, T3 = (scr(R + 3840 + 512 * n, 2, T) for n in range(3))
            for i, name in enumerate(("s5_cT_re", "s5_cT_im")):
                t_ct = pool_dma(d_s5, CT[i].rearrange("p a b -> p (a b)"), A[name])
            t_cw = G.do(G.w().memset(CW, 0.0))
            lr, li, ld = pr("lam_re", 0, 32), pr("lam_im", 0, 32), pr("log_dt", 0, 32)
            p = [SP5[:, n, :] for n in range(16)]
            dt, ang, th, cs, sn, ar, ai, nr, inv, cr, ci, tmp, tmp2 = p[:13]
            t = S.do(S.w().activation(dt, ld, ACT.Exp))
            tt(ang, li, dt, ALU.mult, t)
            t = tt(tmp, lr, dt, ALU.mult)
            t_mag = S.do(S.w(t).activation(MAG[:, :], tmp, ACT.Exp))
            state["mag"] = t_mag
            yield
            t = reduce_angle(th, ang, tmp2, V.now())
            yield
            t_s, t_c = cos_sin(cs, sn, th, tmp2, t)
            t = tt(ar, MAG[:, :], cs, ALU.mult, t_s, t_c, t_mag)
            t_ai = tt(ai, MAG[:, :], sn, ALU.mult)
            t_nr = V.do(V.w(t).tensor_scalar(nr, ar, -1.0, None, ALU.add))
            t = tt(inv, lr, lr, ALU.mult)
            t2 = tt(tmp, li, li, ALU.mult, t_mag)
            t = tt(inv, inv, tmp, ALU.add, t, t2)
            t = V.do(V.w(t).reciprocal(inv, inv))
            yield
            t2 = tt(cr, nr, lr, ALU.mult, t_nr, t_ai, t)
            t = tt(tmp, ai, li, ALU.mult)
            t = tt(cr, cr, tmp, ALU.add, t, t2)
            t = tt(cr, cr, inv, ALU.mult, t)
            t2 = tt(ci, ai, lr, ALU.mult)
            t = tt(tmp, nr, li, ALU.mult, t)
            t = tt(ci, ci, tmp, ALU.subtract, t, t2)
            t = tt(ci, ci, inv, ALU.mult, t)
            yield
            X = T1.rearrange("p a b -> p (a b)").rearrange("p (a b) -> p a b", b=16)
            t2 = tt(CP[0], CT[0], bcl(cr, 16), ALU.mult, t, t_ct)
            t = tt(X, CT[1], bcl(ci, 16), ALU.mult)
            t = tt(CP[0], CP[0], X, ALU.subtract, t, t2)
            t2 = tt(CP[1], CT[0], bcl(ci, 16), ALU.mult)
            t = tt(X, CT[1], bcl(cr, 16), ALU.mult, t)
            t = V.do(V.w(t, t2).scalar_tensor_tensor(CP[1], X, -1.0, CP[1], ALU.mult, ALU.subtract))
            yield
            for j in range(8):
                G.w(t, t_cw)
                for r in range(2):
                    for e in range(2):
                        dst = CW[:, 640 * r:640 * r + 640].rearrange("p (q s) -> p q s", s=160)
                        G.w(G.now())
                        t_w = G.do(nc.gpsimd.tensor_copy(dst[64 * e:64 * e + 64, :, 16 * e:16 * e + 16],
                                                         CP[r][64 * e:64 * e + 64, 4 * j:4 * j + 4, :]))
                t_cw = pool_dma(d_cw, CWD[j], CW, t_w)
                yield
            time = cn("time")
            t_cs = None
            for n in range(16):
                V.w(t, t_s, t_c)
                for c in range(2):
                    t1 = V.do(nc.vector.tensor_scalar(T1[:, c, :], time, th[:, 2 * n + c:2 * n + c + 1], None,
                                                      ALU.mult))
                t1 = reduce_angle(T2, T1, T3, t1)
                yield
                yield
                t_s, t_c = cos_sin(CO, SI, T2, T3, t1, t_cs)
                t_cs = pool_dma(d_cs, CSD[n], CS, t_s, t_c)
                yield
                yield
                yield

        x = ffn(1, x, s5_tables)

        def gla_heads(H, nv, q, k, b, v, v_marks, ones, weight, dst, E, MS, RED):
            used, decays = [None, None], {}

            def decay(h):
                bb, e = b[:, h, :], E[h % 2]
                V.w(used[h % 2])
                for l in range(1, 8):
                    w = 2 ** l
                    src = bb.rearrange("p (n w) -> p n w", w=w)
                    to = e[:, l - 1, :].rearrange("p (n w) -> p n w", w=w)
                    mid = src[:, :, w // 2 - 1:w // 2].broadcast_to([128, T // w, w // 2])
                    V.do(nc.vector.tensor_tensor(to[:, :, 0:w // 2], mid, src[:, :, 0:w // 2], ALU.subtract))
                    V.do(nc.vector.tensor_tensor(to[:, :, w // 2:w], src[:, :, w // 2:w], mid, ALU.subtract))
                t = V.do(nc.vector.tensor_scalar(e[:, 7, 0:128], bb[:, 0:128], bb[:, 127:128], -1.0, ALU.subtract,
                                                 ALU.mult))
                decays[h] = t

            def exponentials(h):
                e = E[h % 2]
                S.w(used[h % 2])
                t = S.do(nc.scalar.activation(e[:, 7, 128:256], b[:, h, 128:256], ACT.Copy))
                decays[h] = S.do(S.w(t, decays[h]).activation(e, e, ACT.Exp))

            def weigh(h):
                V.w(decays[h])
                for l in range(1, 9):
                    w = 2 ** l
                    for side, f in ((0, k), (1, q)):
                        half = slice(side * w // 2, (side + 1) * w // 2)
                        e = E[h % 2][:, l - 1, :].rearrange("p (n w) -> p n w", w=w)[:, :, half]
                        f = f[:, h, :].rearrange("p (n w) -> p n w", w=w)[:, :, half]
                        t = V.do(nc.vector.tensor_tensor(e, e, f, ALU.mult))
                decays[h] = t

            def head(h):
                kk, qq, e = k[:, h, :], q[:, h, :], E[h % 2]
                for m in range(2):
                    c = slice(128 * m, 128 * m + 128)
                    PE.w(decays[h], st.get("ms_read"), st.get("ss"))
                    for l in range(8):
                        lhs, rhs = (kk[:, c], qq[:, c]) if l == 0 else (e[:, l - 1, c], e[:, l - 1, c])
                        last = mm(PB[:, l // 4, 128 * (l % 4):128 * (l % 4) + 128], lhs, rhs, l % 4 == 0, True)
                    t = PE.do(last)
                    if m == 0:
                        PE.w(st.get("cross"), st.get("ln"), st.get("at"))
                        t_x = PE.do(mm(PB[:, 2, 0:128], e[:, 7, 0:128], e[:, 7, 128:256], True, True))
                    else:
                        used[h % 2] = t
                    yield
                    if m == 0:
                        t_x = st["cross"] = S.do(S.w(t_x, st.get("pv")).activation(RED[:, 128:256], PB[:, 2, 0:128],
                                                                                   ACT.Copy))
                    t = V.do(V.w(t, st.get("red")).tensor_tensor(
                        MS, PB[:, 0:2, :].rearrange("p a b -> p (a b)"), cn("lmask"), ALU.mult))
                    st["ms_read"] = t
                    V.w(t, st.get("pv"))
                    t = st["red"] = V.do(nc.vector.tensor_reduce(RED[:, 256 * m:256 * m + 128],
                                                                 MS.rearrange("p (l t) -> p t l", l=8), AX.X, ALU.add))
                    yield
                if h + 1 < H:
                    weigh(h + 1)
                yield
                if h + 2 < H:
                    decay(h + 2)
                yield
                PE.w(t_x, *v_marks)
                decays[h] = weighted(v, 128 * nv * h, nv, RED, t)
                yield
                if h + 2 < H:
                    exponentials(h + 2)
                yield

            def finish(h):
                yield from head_norm(nv, decays[h], ones, "eps6")
                V.w(*st["rms"])
                for e in range(nv):
                    t = V.do(nc.vector.scalar_tensor_tensor(dst[:, nv * h + e, :], OF[:, e, :], weight(nv * h + e),
                                                            STAT[:, 3, :], ALU.mult, ALU.mult))
                st["ofu"] = st[("y", h)] = t
                yield

            decay(0)
            exponentials(0)
            yield
            decay(1)
            exponentials(1)
            yield
            weigh(0)
            yield
            yield
            yield
            before = iter(())
            for h in range(H):
                for _ in head(h):
                    next(before, None)
                    yield
                for _ in before:
                    yield
                before = finish(h)
            yield from before

        def scan(dst, src, H, ones, *marks):
            t = G.do(G.w(*marks).memset(ones, 1.0))
            t = G.do(G.w(t).memset(ones.rearrange("p (m w) -> p m w", w=128)[:, :, 0:1], 0.0))
            return V.do(V.w(t, *marks).tensor_tensor_scan(dst.rearrange("p h t -> p (h t)"), ones,
                                                          src.rearrange("p h t -> p (h t)"), 0.0, ALU.mult, ALU.add))

        barrier()
        st = {}
        KB = scr(0, 4, T)
        QB = scr(1024, 4, T)
        BB = scr(2048, 4, T)
        VB = scr(3072, 2, 1024)
        GT = scr(0, 16, T)
        VA = scr(5120, 2, 1024)
        KD = scr(7168, 8, T)
        QD = scr(9216, 8, T)
        YR = scr(11264, 16, T)
        LG = scr(11264, 4, T)
        E1 = scr(15360, 8, T)
        E2 = scr(11264, 8, T)
        MS = scr(17408, 1024)
        RED = scr(18432, 384)
        SS = scr(18816, 2, 384)
        PP = scr(19584, 2, 384)
        AT = scr(20352, 384)
        OF = scr(20736, 2, T)
        OQ = scr(21248, 2, T)
        SM = scr(21760, 64)
        GW = scr(21824, 512)
        GL = scr(22336, T)
        YBH = scr(15360, 8, T, dt=BF16)
        YBL = scr(16384, 8, T, dt=BF16)
        XN = [E1[:, 0:4, :], E1[:, 4:8, :]]
        d_gw = Queue(None, sem("d_gw"))
        t_gw = pool_dma(d_gw, GW[0:16, :], A["gla_w_gate"])
        x = rms_norm(lambda k: pr("norm", k), XN)

        def keep(dst, scale=1.0, marks=None):
            at = [0]

            def evac(gi, ps, done):
                j = at[0]
                at[0] += 1
                t = S.do(S.w(done).activation(dst[:, 4 * j:4 * j + 4, :], ps[:, :, :], ACT.Copy, scale=scale))
                marks.append(t)
                return t
            return evac

        def low(gi, ps, done):
            st["gl"] = S.do(S.w(done).activation(GL[0:16, :], ps[0:16, 0, :], ACT.Copy))
            return st["gl"]

        def gla_decay():
            PE.w(t_gw, st["gl"])
            for n in range(4):
                t = PE.do(mm(PB[:, n // 2, T * (n % 2):T * (n % 2) + T], GW[0:16, 128 * n:128 * n + 128], GL[0:16, :],
                             n % 2 == 0, True))
            yield
            V.w(t)
            for n in range(4):
                t = V.do(nc.vector.tensor_scalar(LG[:, n, :], PB[:, n // 2, T * (n % 2):T * (n % 2) + T],
                                                 pr("gla_b", n), None, ALU.add))
            st["ms_read"] = t
            t_a = S.do(S.w(t).activation(BB, LG, ACT.Abs))
            t_m = V.do(V.w(t_a).tensor_scalar(LG, LG, 0.0, 1.0 / 16, ALU.min, ALU.mult))
            t = S.do(S.w(t_a).activation(BB, BB, ACT.Exp, scale=-1.0))
            t = S.do(S.w(t).activation(BB, BB, ACT.Ln, bias=cn("one")))
            t = V.do(V.w(t, t_m).scalar_tensor_tensor(LG, BB, -1.0 / 16, LG, ALU.mult, ALU.add))
            yield
            st["scan"] = scan(BB, LG, 4, MS, t)
            yield

        def gla():
            PE.w(*b_marks)
            V.w(st["scan"], *b_marks)
            S.w(st["scan"])
            yield from gla_heads(4, 2, QB, KB, BB, VB, vb_marks, ONE_256, lambda n: pr("gla_norm", n), YR[:, 8:16, :],
                                 (E1, E2), MS, RED)
            st["gla"] = (st["ofu"], PE.now())

        def dilated():
            PE.w(*a_marks)
            S.w(*st["gla"])
            for h in range(0, 8, 2):
                PE.w(st.get("ms_read"))
                yield from scores(QD, KD, (h, h + 1), 128.0 ** -0.5, cn("dmask"))
                t = exps(st["max"], st.get("tr"))
                t = V.do(V.w(t).tensor_tensor(PP, PP, bc(cn("dcount"), 2), ALU.mult))
                V.w(t)
                V.do(nc.vector.tensor_reduce(SM[:, 8:10], PP[:, :, 0:256], AX.X, ALU.add))
                t = V.do(nc.vector.tensor_reduce(SM[:, 10:12], PP[:, :, 256:384], AX.X, ALU.add))
                t = V.do(V.w(t).reciprocal(SM[:, 12:16], SM[:, 8:12]))
                V.w(t)
                for c in range(2):
                    V.do(nc.vector.tensor_scalar(PP[:, c, 0:256], PP[:, c, 0:256], SM[:, 12 + c:13 + c], None,
                                                 ALU.mult))
                    t = V.do(nc.vector.tensor_scalar(PP[:, c, 256:384], PP[:, c, 256:384], SM[:, 14 + c:15 + c],
                                                     None, ALU.mult))
                yield
                t_w = t
                for c in range(2):
                    yield
                    yield
                    yield from turn(PP[:, c, :], AT, t_w, st.get("pv"))
                    yield
                    while len(va_marks) < 2:
                        yield
                    PE.w(*va_marks)
                    t = weighted(VA, 128 * (h + c), 1, AT, st["at"])
                    yield
                    st["of"] = S.do(S.w(t).activation(YR[:, h + c, :], PB[:, 3, 0:T], ACT.Copy))
                    st[("dil", h + c)] = st["of"]
                    yield

        g_marks = {}

        def gate(gi, ps, done):
            j = (2, 3, 0, 1)[len(g_marks)]
            g_marks[j] = S.do(S.w(done, *st.get("gt_free", ())).activation(GT[:, 4 * j:4 * j + 4, :], ps[:, :, :],
                                                                         ACT.Silu))
            return g_marks[j]

        def gated(g, y, hi, lo, marks, mark, free):
            t = tt(y, y, GT[:, 4 * g:4 * g + 4, :], ALU.mult, g_marks[g], mark)
            t = split_x(hi, lo, y, t, free)
            marks[4 * g:4 * g + 4] = [t] * 4

        b_marks, vb_marks, va_marks, a_marks = [], [], [], []
        state["rate"] = 3
        gemm(["kb"], x, keep(KB, marks=b_marks))
        gemm(["qb"], x, keep(QB, 128.0 ** -0.5, marks=b_marks))
        gemm(["glow"], x, low)
        background.append(gla_decay())
        gemm(["vb"] * 2, x, v_evac(VB, vb_marks), row_major=True)
        background.append(gla())
        gemm(["ka"] * 2, x, keep(KD, marks=a_marks))
        gemm(["qa"] * 2, x, keep(QD, marks=a_marks))
        background.append(dilated())
        gemm(["va"] * 2, x, v_evac(VA, va_marks), row_major=True)
        while "gla" not in st:
            step()
        st["gt_free"] = st["gla"]
        marks = [None] * NT
        gemm(["gate"] * 2, x, gate)

        def gated_gla():
            for g in (2, 3):
                gated(g, YR[:, 4 * g:4 * g + 4, :], YBH[:, 4 * g - 8:4 * g - 4, :], YBL[:, 4 * g - 8:4 * g - 4, :],
                      marks, st["gla"][0], st["gla"][1])
                yield

        background.appendleft(gated_gla())
        gemm(["gate"] * 2, x, gate)
        x_used = PE.now()

        def gated_dilated():
            for g in range(2):
                c = slice(4 * g, 4 * g + 4)
                gated(g, YR[:, c, :], XH[:, c, :], XL[:, c, :], marks, st[("dil", 4 * g + 3)], x_used)
                yield

        background.append(gated_dilated())
        gemm(["o"] * 4, ([XH[:, k, :] for k in range(8)] + [YBH[:, k, :] for k in range(8)],
                         [XL[:, k, :] for k in range(8)] + [YBL[:, k, :] for k in range(8)], marks),
             residual(None, [scr(7168, 4, T), scr(8192, 4, T)], "rms"))
        state["rate"] = 1

        barrier()
        st = {}
        U = scr(0, 8, T)
        GT = scr(2048, 16, T)
        FF = scr(2048, 8, T)
        ONES = scr(4096, 2048)
        VI = scr(6144, 2, 1024)
        KD = scr(8192, 8, T)
        BD = scr(10240, 8, T)
        QH = scr(12288, 8, T)
        R = 14336
        BT = scr(R, 2, 2, 128)
        CW = scr(R + 512, 1280)
        CS = [scr(R + 1792, 4, T), scr(R + 2816, 4, T)]
        V1, V2, XS, P2 = (scr(R + 3840 + 1024 * n, 2, 2, T) for n in range(4))
        MG = scr(R + 7936, 2, T)
        E1 = scr(R, 8, T)
        E2 = scr(R + 3968, 8, T)
        MS = scr(R + 2048, 1024)
        RED = scr(R + 3072, 384)
        OF = scr(R + 3456, 1, T)
        OQ = scr(R + 3712, 1, T)
        SM = scr(R + 8448, 32)
        UH = scr(R + 6016, 8, T, dt=BF16)
        UL = scr(R + 7040, 8, T, dt=BF16)
        SG = STAT[:, 0:2, :]
        XN = [scr(8192, 4, T), scr(9216, 4, T)]
        x = rms_norm(lambda k: pr("norm", 16 + k), XN)

        u_marks = []

        def s5():
            PE.w(*u_marks)
            d_bt = [Queue(None, sem(f"d_bt{n}")) for n in range(2)]
            d_ci = Queue(None, sem("d_ci"))
            d_ro = [Queue(None, sem(f"d_ro{n}")) for n in range(2)]
            flat = "p a b -> p (a b)"
            G.w(d_cs.now(), d_cw.now())

            def bt(j, *free):
                for r, name in enumerate(("s5_bT_re", "s5_bT_im")):
                    t = pool_dma(d_bt[j % 2], BT[:, j % 2, r, :], A[name][:, 128 * j:128 * j + 128], *free)
                return t

            def cs(n, *free):
                return pool_dma(d_ro[n % 2], CS[n % 2].rearrange(flat), CSD[n], *free)

            t_bt = [bt(0), bt(1)]
            t_cw = pool_dma(d_ci, CW, CWD[0])
            t_cs = [cs(0), cs(1)]
            used_b = {}

            def product(n):
                j = n // 2
                PE.w(t_bt[j % 2], st.get("br"))
                for r in range(2):
                    for c in range(2):
                        q = (2 * n + c) % 4
                        rows = slice(32 * q, 32 * q + 32)
                        t = PE.do(mm(PB[:, c, T * r:T * r + T], BT[rows, j % 2, r, :], U[rows, j, :], r == 0, True))
                if n % 2 and j + 2 < 8:
                    t_bt[j % 2] = bt(j + 2, t)
                return t

            def over(ap):
                return ap.unsqueeze(1).broadcast_to([128, 2, 2, T])

            t_b = product(0)
            t_y = None
            yield
            for n in range(16):
                j, i0 = n // 2, 2 * n
                CO, SI = CS[n % 2][:, 0:2, :], CS[n % 2][:, 2:4, :]
                S.w(st.get("scan"), state["mag"])
                for c in range(2):
                    t_g = S.do(nc.scalar.activation(MG[:, c, :], cn("time"), ACT.Identity, scale=0.0,
                                                    bias=MAG[:, i0 + c:i0 + c + 1]))
                t_g = S.do(S.w(t_g).activation(MG[:, :, 0:1], MG[:, :, 0:1], ACT.Copy, scale=0.0))
                bu = PB[:, 0:2, :].rearrange("p c (r t) -> p r c t", t=T)
                V.w(t_b, t_cs[n % 2])
                t = V.do(nc.vector.tensor_tensor(V1, bu, over(CO), ALU.mult))
                t = st["br"] = V.do(nc.vector.tensor_tensor(V2, bu, over(SI), ALU.mult))
                V.w(t)
                V.do(nc.vector.tensor_tensor(V1[:, 0, :, :], V1[:, 0, :, :], V2[:, 1, :, :], ALU.add))
                t = V.do(nc.vector.tensor_tensor(V1[:, 1, :, :], V1[:, 1, :, :], V2[:, 0, :, :], ALU.subtract))
                yield
                if n < 15:
                    t_b = product(n + 1)
                V.w(t, t_g, st.get("yb"))
                for r in range(2):
                    t = V.do(nc.vector.tensor_tensor_scan(XS[:, r, :, :].rearrange(flat), MG.rearrange(flat),
                                                          V1[:, r, :, :].rearrange(flat), 0.0, ALU.mult, ALU.add))
                st["scan"] = t
                yield
                V.w(t)
                t = V.do(nc.vector.tensor_tensor(P2, XS, over(SI), ALU.mult))
                t = V.do(V.w(t).tensor_tensor(XS, XS, over(CO), ALU.mult))
                V.w(t)
                V.do(nc.vector.tensor_tensor(XS[:, 0, :, :], XS[:, 0, :, :], P2[:, 1, :, :], ALU.subtract))
                t = V.do(nc.vector.tensor_tensor(P2[:, 0, :, :], P2[:, 0, :, :], XS[:, 1, :, :], ALU.add))
                if n < 14:
                    t_cs[n % 2] = cs(n + 2, t)
                yield
                yield
                PE.w(t, t_cw, t_y)
                for c in range(2):
                    q = (i0 + c) % 4
                    parts = ((0, XS[:, 0, c, :]), (1, P2[:, 0, c, :]))
                    for i, (r, z) in enumerate(parts):
                        last = mm(PB[:, 2, 0:T], CW[:, 640 * r + 128 * q:640 * r + 128 * q + 128], z,
                                  q == 0 and i == 0, q == 3 and i == 1)
                st["yb"] = PE.do(last)
                if n % 2:
                    if j < 7:
                        t_cw = pool_dma(d_ci, CW, CWD[j + 1], st["yb"])
                    yield
                    t_y = V.do(V.w(st["yb"]).scalar_tensor_tensor(U[:, j, :], U[:, j, :], pr("s5_d", j),
                                                                  PB[:, 2, 0:T], ALU.mult, ALU.add))
                    st[("u", j)] = t_y
                yield
            for g in range(2):
                c = slice(4 * g, 4 * g + 4)
                t = S.do(S.w(t_y).activation(U[:, c, :], U[:, c, :], ACT.Gelu_apprx_tanh))
                t = S.do(S.w(t, st["yb"], V.now()).activation(UH[:, c, :], U[:, c, :], ACT.Copy))
                yield
                st[("g", g)] = V.do(V.w(t, st["yb"]).tensor_tensor(UL[:, c, :], U[:, c, :], UH[:, c, :], ALU.subtract))
                yield
            st["s5"] = t

        LB, OM = SM[:, 0:8], SM[:, 8:16]
        gm = pr("gamma", 0, 16)
        t = tt(SM[:, 16:24], gm[:, 0:8], gm[:, 8:16], ALU.max)
        tt(LB, gm[:, 0:8], SM[:, 16:24], ALU.subtract, t)
        t = tt(OM, gm[:, 8:16], SM[:, 16:24], ALU.subtract)
        t = S.do(S.w(t).activation(SM[:, 0:16], SM[:, 0:16], ACT.Exp))
        t = tt(SM[:, 16:24], LB, OM, ALU.add, t)
        t = V.do(V.w(t).reciprocal(SM[:, 24:32], SM[:, 16:24]))
        tt(LB, LB, SM[:, 24:32], ALU.mult, t)
        t = tt(OM, OM, SM[:, 24:32], ALU.mult)
        t = tt(SM[:, 16:24], LB, OM, ALU.add, t)
        t = tt(LB, SM[:, 16:24], LB, ALU.subtract, t)
        t_lb = V.do(V.w(t).tensor_scalar(OM, LB, -1.0, 1.0, ALU.mult, ALU.add))
        f_marks = []

        def forget(gi, ps, done):
            j = len(f_marks)
            ff = FF[:, 4 * j:4 * j + 4, :]
            t_f = S.do(S.w(done).activation(ff, ps[:, :, :], ACT.Sigmoid))
            V.w(t_f, t_lb)
            for n in range(4):
                k = 4 * j + n
                t = V.do(nc.vector.tensor_scalar(FF[:, k, :], FF[:, k, :], OM[:, k:k + 1], LB[:, k:k + 1], ALU.mult,
                                                 ALU.add))
            st["kd"] = V.do(V.w(t).tensor_scalar(KD[:, 4 * j:4 * j + 4, :], ff, -1.0, 1.0, ALU.mult, ALU.add))
            f_marks.append(S.do(S.w(st["kd"]).activation(ff, ff, ACT.Ln)))
            return t_f

        q_marks, vi_marks = [], []

        def query(gi, ps, done):
            j = len(q_marks)
            t = S.do(S.w(done).activation(QH[:, 4 * j:4 * j + 4, :], ps[:, :, :], ACT.Silu))
            q_marks.append(t)
            return t

        def hgrn():
            while "s5" not in st or "scan_b" not in st or len(vi_marks) < 2:
                yield
            PE.w(*q_marks, V.now())
            V.w(st["scan_b"], st["yb"], *q_marks)
            S.w(st["scan_b"], st["yb"], V.now())
            yield from gla_heads(8, 1, QH, KD, BD, VI, vi_marks, ONE_128, lambda n: pr("hgrn_norm", n), QH,
                                 (E1, E2), MS, RED)

        g_marks = {}
        gemm(["u"] * 2, x, keep(U, marks=u_marks))
        background.append(s5())
        background.append(hgrn())
        state["rate"] = 3
        gemm(["fd"] * 2, x, forget)
        st["scan_b"] = scan(BD, FF, 8, ONES, *f_marks)
        st["gt_free"] = (st["scan_b"],)
        gemm(["qd"] * 2, x, query)
        gemm(["idd"] * 2, x, v_evac(VI, vi_marks), row_major=True)
        gemm(["gate"] * 3, x, gate)
        while "s5" not in st:
            step()
        glu_marks = []

        def glu(gi, ps, done):
            j = len(glu_marks) // 2
            for n in range(0, 4, 2):
                k = 4 * j + n
                S.w(done, glu_marks[-1] if glu_marks else None)
                for m in range(2):
                    t = S.do(nc.scalar.activation(SG[:, m, :], ps[:, n + m, :], ACT.Sigmoid,
                                                  bias=pr("b_glu", k + m)))
                glu_marks.append(tt(U[:, k:k + 2, :], U[:, k:k + 2, :], SG, ALU.mult, t))
            return t

        gemm(["glu"] * 2, (UH, UL, [st[("g", k // 4)] for k in range(8)]), glu)
        glu_used = PE.now()
        marks = [None] * NT

        def gated_s5(g):
            c = slice(4 * g, 4 * g + 4)
            gated(g, U[:, c, :], UH[:, c, :], UL[:, c, :], marks, glu_marks[-1], glu_used)
            yield

        background.appendleft(gated_s5(0))
        gemm(["gate"], x, gate)
        x_used = PE.now()
        background.appendleft(gated_s5(1))

        def gated_hgrn():
            for g in range(2, 4):
                c = slice(4 * g, 4 * g + 4)
                gated(g, QH[:, 4 * g - 8:4 * g - 4, :], XH[:, c, :], XL[:, c, :], marks, st[("y", 4 * g - 5)], x_used)
                yield

        background.append(gated_hgrn())
        gemm(["o"] * 4, (UH, UL, marks), residual(None, None, None))
        while marks[-1] is None:
            step()
        XN = [scr(R, 4, T), scr(R + 1024, 4, T)]
        V.w(PE.now(), S.now())
        S.w(PE.now(), V.now())
        gemm(["o"] * 4, (XH, XL, marks), residual(None, XN, "rms"))
        out_v = out.rearrange("(t p) n -> p t n", p=128)
        XO = [scr(R + 2048, 4, T), scr(R + 3072, 4, T)]

        def store(g, src, t):
            return dma(d_out[g % 2], out_v[:, 4 * g:4 * g + 4, :], src, t)

        rms_norm(lambda k: pr("final", k), XO, store)
        SP.w(d_out[0].now(), d_out[1].now(), d_cs.now(), d_cw.now())


def feature_tiles(a):
    a = np.asarray(a)
    return np.ascontiguousarray(a.reshape(-1, a.shape[-1] // 128, 128).transpose(2, 0, 1)).reshape(128, -1)


def state_tiles(a):
    return np.ascontiguousarray(np.asarray(a).reshape(32, 128).T)


def kernel(**inputs):
    import concourse.bacc as bacc
    from concourse.bass_utils import run_bass_kernel_spmd

    a = {k: np.asarray(v) for k, v in inputs.items()}
    packed = {
        "ln_g": feature_tiles(a["ln_g"].reshape(4, D)), "ln_b": feature_tiles(a["ln_b"].reshape(4, D)),
        "a_conv": feature_tiles(a["a_conv_w"][0]), "f_conv": feature_tiles(a["ffn_conv_w"].reshape(6, 2 * DFF)),
        "f_bias": feature_tiles(a["ffn_conv_b"]), "subln": feature_tiles(a["b_subln_g"]),
        "norm": feature_tiles(a["norm_g_2"]), "final": feature_tiles(a["final_g_2"].reshape(1, D)),
        "gla_b": feature_tiles(a["gla_b_gate_2"]), "gla_norm": feature_tiles(a["gla_norm_g_2"]),
        "lam_re": state_tiles(a["s5_lam_re_2"][0]), "lam_im": state_tiles(a["s5_lam_im_2"][0]),
        "log_dt": state_tiles(np.repeat(a["s5_log_dt_2"][0][:, None], 64, 1)),
        "s5_d": feature_tiles(a["s5_d_2"].reshape(1, 1024)), "b_glu": feature_tiles(a["s5_b_glu_2"]),
        "gamma": feature_tiles(a["hgrn_gamma_2"]), "hgrn_norm": feature_tiles(a["hgrn_norm_g_2"]),
        "b_lambda": feature_tiles(a["b_lambda"][0]),
    }
    params = np.zeros((128, NPARAM), np.float32)
    for name, (lo, hi) in PARAM.items():
        params[:, lo:hi] = packed[name]

    def b_tiles(b):
        b = b[0].reshape(8, 4, 2, 64, 16)
        o = np.zeros((4, 2, 16, 8, 2, 64), np.float32)
        for e in range(2):
            o[:, e, :, :, e, :] = b[:, :, e].transpose(1, 3, 0, 2)
        return o.reshape(128, 1024)

    def c_tiles(c):
        return np.ascontiguousarray(c[0].reshape(32, 2, 16, 64).transpose(1, 3, 0, 2)).reshape(128, 512)

    arrays = {
        "consts": constants(), "params": params, "xT": np.ascontiguousarray(a["x"][0].T),
        "positions": np.ascontiguousarray(a["positions"][0]),
        "a_w_in": a["a_w_in"][0], "a_w_out": a["a_w_out"][0], "kv_w_k": a["kv_w_k"], "kv_w_v": a["kv_w_v"],
        "b_w_q": a["b_w_q"][0], "b_w_o": a["b_w_o"][0], "ffn_w_up": a["ffn_w_up"], "ffn_w_down": a["ffn_w_down"],
        "ab_w_in": a["ab_w_in_2"][0], "gla_w_gate": a["gla_w_gate_2"][0], "ab_w_out": a["ab_w_out_2"][0],
        "cd_w_in": a["cd_w_in_2"][0], "s5_w_glu": a["s5_w_glu_2"][0], "cd_w_out": a["cd_w_out_2"][0],
        "s5_bT_re": b_tiles(a["s5_b_re_2"]), "s5_bT_im": b_tiles(a["s5_b_im_2"]),
        "s5_cT_re": c_tiles(a["s5_c_re_2"]), "s5_cT_im": c_tiles(a["s5_c_im_2"]),
    }
    nc = bacc.Bacc("TRN2", target_bir_lowering=False, num_devices=1)
    ins = {n: nc.dram_tensor(n, v.shape, mybir.dt.from_np(v.dtype), kind="ExternalInput").ap()
           for n, v in arrays.items()}
    out = nc.dram_tensor("out", (D, T), F32, kind="ExternalOutput").ap()
    two_block_model(nc, ins, out)
    r = run_bass_kernel_spmd(nc, [arrays], core_ids=[0])
    return np.ascontiguousarray(r.results[0]["out"].T)[None]
```
